# Optimizing a Trainium2 kernel written in Bass

```python
import jax, jax.numpy as jnp
from jax import lax
import numpy as np

D_MODEL = 1024
BATCH = 1
SEQ = 1024
DEPTH = 1
DEC_BATCH = 8
DEC_SEQ = 8
PAST_LEN = 2048
PAGE_SIZE = 128

HEAD_DIM = 64
N_RWKV_HEADS = 8
RWKV_WIDTH = N_RWKV_HEADS * HEAD_DIM
N_Q_HEADS = 8
N_KV_HEADS = 2
GROUP = N_Q_HEADS // N_KV_HEADS
ATT_WIDTH = N_Q_HEADS * HEAD_DIM
KV_WIDTH = N_KV_HEADS * HEAD_DIM
MIX_WIDTH = RWKV_WIDTH + ATT_WIDTH
DECAY_LORA = 64
AAA_LORA = 64
GATE_LORA = 128
RWKV_COLS = 3 * RWKV_WIDTH + DECAY_LORA + AAA_LORA + GATE_LORA
IN_COLS = RWKV_COLS + ATT_WIDTH + 2 * KV_WIDTH
RWKV_SPLITS = (RWKV_WIDTH, 2 * RWKV_WIDTH, 3 * RWKV_WIDTH,
               3 * RWKV_WIDTH + DECAY_LORA, 3 * RWKV_WIDTH + DECAY_LORA + AAA_LORA)
WINDOW = 128
ROPE_THETA = 500000.0
ROPE_DIM = HEAD_DIM // 4
D_FF = 2816
N_ADA = 9
NORM_EPS = 1e-5
LNX_EPS = 64e-5
NEG_INF = -1e30

kernel_name = 'hymba_rwkv7_swa_sink_macaron_adaln_step'

def rms_norm(x, g):
    xf = x.astype(jnp.float32)
    y = xf * lax.rsqrt(jnp.mean(xf * xf, axis=-1, keepdims=True) + NORM_EPS)
    return (y * g.astype(jnp.float32)).astype(x.dtype)

def modulate(x, g, shift, scale):
    return rms_norm(x, g) * (1 + scale) + shift

def swiglu(h, w_gu, w_down):
    gate, up = jnp.split(h @ w_gu, 2, axis=-1)
    return (jax.nn.silu(gate) * up) @ w_down

def partial_rope(x, pos):
    inv_freq = ROPE_THETA ** (-jnp.arange(0, ROPE_DIM, 2, dtype=jnp.float32) / ROPE_DIM)
    ang = pos.astype(jnp.float32)[:, None] * inv_freq[None, :]
    cos, sin = jnp.cos(ang)[:, None, :], jnp.sin(ang)[:, None, :]
    xr = x[..., :ROPE_DIM].astype(jnp.float32)
    x1, x2 = xr[..., :ROPE_DIM // 2], xr[..., ROPE_DIM // 2:]
    rot = jnp.concatenate([x1 * cos - x2 * sin, x2 * cos + x1 * sin], axis=-1)
    return jnp.concatenate([rot.astype(x.dtype), x[..., ROPE_DIM:]], axis=-1)

def window_mask(q_pos, k_pos):
    qp, kp = q_pos[..., :, None], k_pos[..., None, :]
    return (kp <= qp) & (qp - kp < WINDOW) & (kp >= 0)

def sink_attention(q, k, v, mask, sinks):
    s = jnp.einsum('...qhgd,...khd->...hgqk', q.astype(jnp.float32), k.astype(jnp.float32)) * (HEAD_DIM ** -0.5)
    s = jnp.where(mask, s, NEG_INF)
    sink = sinks.astype(jnp.float32).reshape(N_KV_HEADS, GROUP, 1, 1)
    m = jnp.maximum(jnp.max(s, axis=-1, keepdims=True), sink)
    p = jnp.exp(s - m)
    p = p / (jnp.sum(p, axis=-1, keepdims=True) + jnp.exp(sink - m))
    o = jnp.einsum('...hgqk,...khd->...qhgd', p, v.astype(jnp.float32))
    return o.astype(v.dtype)

def swa_prompt(q, k, v, sinks):
    B, S = q.shape[:2]
    nb = S // WINDOW
    qb = q.reshape(B, nb, WINDOW, N_KV_HEADS, GROUP, HEAD_DIM)
    kb = k.reshape(B, nb, WINDOW, N_KV_HEADS, HEAD_DIM)
    vb = v.reshape(B, nb, WINDOW, N_KV_HEADS, HEAD_DIM)

    def with_prev(t):
        prev = jnp.pad(t[:, :-1], ((0, 0), (1, 0), (0, 0), (0, 0), (0, 0)))
        return jnp.concatenate([prev, t], axis=2)

    blk = jnp.arange(nb)[:, None] * WINDOW
    q_pos = blk + jnp.arange(WINDOW)[None, :]
    k_pos = blk - WINDOW + jnp.arange(2 * WINDOW)[None, :]
    mask = window_mask(q_pos, k_pos)[None, :, None, None]
    o = sink_attention(qb, with_prev(kb), with_prev(vb), mask, sinks)
    return o.reshape(B, S, ATT_WIDTH), k[:, -WINDOW:], v[:, -WINDOW:]

def swa_sample(q, k, v, k_buf, v_buf, pos0, sinks):
    B, T = q.shape[:2]
    kk = jnp.concatenate([k_buf.astype(k.dtype), k], axis=1)
    vv = jnp.concatenate([v_buf.astype(v.dtype), v], axis=1)
    q_pos = pos0 + jnp.arange(T)
    k_pos = jnp.concatenate([pos0 - WINDOW + jnp.arange(WINDOW), q_pos])
    mask = window_mask(q_pos, k_pos)[None, None, None]
    o = sink_attention(q.reshape(B, T, N_KV_HEADS, GROUP, HEAD_DIM), kk, vv, mask, sinks)
    return o.reshape(B, T, ATT_WIDTH), kk[:, -WINDOW:], vv[:, -WINDOW:]

def wkv7_step(S, inp):
    r, d, k, v, a, b = inp
    sa = jnp.einsum('bhij,bhj->bhi', S, a)
    S = S * d[:, :, None, :] + sa[..., None] * b[:, :, None, :] + v[..., None] * k[:, :, None, :]
    return S, jnp.einsum('bhij,bhj->bhi', S, r)

def rwkv7_heads(u, u_prev, S0, lw):
    f32 = jnp.float32
    B, T, _ = u.shape
    u_shift = jnp.concatenate([u_prev[:, None, :].astype(u.dtype), u[:, :-1]], axis=1)
    z = u + (u_shift - u) * lw['mu_shift']
    r, k, v, zw, za, zg = jnp.split(z, RWKV_SPLITS, axis=-1)
    w_log = -jax.nn.softplus(-(lw['rwkv_w0'] + jnp.tanh(zw) @ lw['rwkv_w2'])) - 0.5
    decay = jnp.exp(-jnp.exp(w_log.astype(f32)))
    a = jax.nn.sigmoid(lw['rwkv_a0'] + za @ lw['rwkv_a2'])
    g = jax.nn.sigmoid(zg) @ lw['rwkv_g2']
    heads = lambda t: t.astype(f32).reshape(B, T, N_RWKV_HEADS, HEAD_DIM)
    kk = heads(k * lw['rwkv_k_k'])
    kk = kk * lax.rsqrt(jnp.maximum(jnp.sum(kk * kk, axis=-1, keepdims=True), 1e-24))
    k = k * (1 + (a - 1) * lw['rwkv_k_a'])
    rh, kh, vh, ah, dh = heads(r), heads(k), heads(v), heads(a), heads(decay)
    seq = tuple(t.transpose(1, 0, 2, 3) for t in (rh, dh, kh, vh, -kk, kk * ah))
    S_new, o = lax.scan(wkv7_step, S0.astype(f32), seq)
    o = o.transpose(1, 0, 2, 3)
    mu = jnp.mean(o, axis=-1, keepdims=True)
    var = jnp.mean(jnp.square(o - mu), axis=-1, keepdims=True)
    o = ((o - mu) * lax.rsqrt(var + LNX_EPS)).reshape(B, T, RWKV_WIDTH)
    o = o * lw['ln_x_w'].astype(f32) + lw['ln_x_b'].astype(f32)
    bonus = jnp.sum(rh * kh * lw['rwkv_r_k'].astype(f32), axis=-1, keepdims=True) * vh
    o = (o + bonus.reshape(B, T, RWKV_WIDTH)) * g.astype(f32)
    return o.astype(u.dtype), S_new

def parallel_heads(h, u_prev, S0, k_buf, v_buf, pos0, lw):
    B, T, _ = h.shape
    proj = h @ lw['w_in']
    u = proj[..., :RWKV_COLS]
    q, k, v = jnp.split(proj[..., RWKV_COLS:], (ATT_WIDTH, ATT_WIDTH + KV_WIDTH), axis=-1)
    rwkv_out, S_new = rwkv7_heads(u, u_prev, S0, lw)
    pos = pos0 + jnp.arange(T)
    q = partial_rope(q.reshape(B, T, N_Q_HEADS, HEAD_DIM), pos)
    k = partial_rope(k.reshape(B, T, N_KV_HEADS, HEAD_DIM), pos)
    v = v.reshape(B, T, N_KV_HEADS, HEAD_DIM)
    if k_buf is None:
        att_out, k_new, v_new = swa_prompt(q, k, v, lw['attn_sinks'])
    else:
        att_out, k_new, v_new = swa_sample(q, k, v, k_buf, v_buf, pos0, lw['attn_sinks'])
    out = jnp.concatenate([rwkv_out, att_out], axis=-1) @ lw['w_out']
    return out, (S_new, u[:, -1], k_new, v_new)

def decoder_layer(x, c, S0, u_prev, k_buf, v_buf, pos0, lw):
    mods = (jax.nn.silu(c) @ lw['w_ada'] + lw['b_ada']).reshape(c.shape[0], N_ADA, 1, D_MODEL)
    sh1, sc1, gt1, sh2, sc2, gt2, sh3, sc3, gt3 = [mods[:, i] for i in range(N_ADA)]
    x = x + 0.5 * gt1 * swiglu(modulate(x, lw['norm_ffn1'], sh1, sc1), lw['ffn1_w_gu'], lw['ffn1_w_down'])
    m, st = parallel_heads(modulate(x, lw['norm_mix'], sh2, sc2), u_prev, S0, k_buf, v_buf, pos0, lw)
    x = x + gt2 * m
    x = x + 0.5 * gt3 * swiglu(modulate(x, lw['norm_ffn2'], sh3, sc3), lw['ffn2_w_gu'], lw['ffn2_w_down'])
    return x, st

def setup_inputs(seed: int = 0) -> dict:
    key = jax.random.key(seed)
    ks = iter(jax.random.split(key, 40))
    nrm = lambda shape, s: jax.random.normal(next(ks), shape, jnp.float32) * s
    uni = lambda shape, lo, hi: jax.random.uniform(next(ks), shape, jnp.float32, lo, hi)
    L = DEPTH
    return {
        'x_prompt': nrm((BATCH, SEQ, D_MODEL), 1.0),
        'x_sample': nrm((DEC_BATCH, DEC_SEQ, D_MODEL), 1.0),
        'c_prompt': nrm((BATCH, D_MODEL), 1.0),
        'c_sample': nrm((DEC_BATCH, D_MODEL), 1.0),
        'state_wkv': nrm((L, DEC_BATCH, N_RWKV_HEADS, HEAD_DIM, HEAD_DIM), 0.3),
        'state_shift': nrm((L, DEC_BATCH, RWKV_COLS), 1.0),
        'cache_k': nrm((L, DEC_BATCH, WINDOW, N_KV_HEADS, HEAD_DIM), 1.0),
        'cache_v': nrm((L, DEC_BATCH, WINDOW, N_KV_HEADS, HEAD_DIM), 1.0),
        'w_ada': nrm((L, D_MODEL, N_ADA * D_MODEL), 0.5 * D_MODEL ** -0.5),
        'b_ada': nrm((L, N_ADA * D_MODEL), 0.02),
        'norm_ffn1': 1.0 + nrm((L, D_MODEL), 0.02),
        'ffn1_w_gu': nrm((L, D_MODEL, 2 * D_FF), D_MODEL ** -0.5),
        'ffn1_w_down': nrm((L, D_FF, D_MODEL), D_FF ** -0.5),
        'norm_mix': 1.0 + nrm((L, D_MODEL), 0.02),
        'w_in': nrm((L, D_MODEL, IN_COLS), D_MODEL ** -0.5),
        'mu_shift': uni((L, RWKV_COLS), 0.0, 1.0),
        'rwkv_w0': uni((L, RWKV_WIDTH), -5.0, 0.0),
        'rwkv_w2': nrm((L, DECAY_LORA, RWKV_WIDTH), 0.5 * DECAY_LORA ** -0.5),
        'rwkv_a0': nrm((L, RWKV_WIDTH), 0.5),
        'rwkv_a2': nrm((L, AAA_LORA, RWKV_WIDTH), 0.5 * AAA_LORA ** -0.5),
        'rwkv_g2': nrm((L, GATE_LORA, RWKV_WIDTH), GATE_LORA ** -0.5),
        'rwkv_k_k': 0.85 + nrm((L, RWKV_WIDTH), 0.02),
        'rwkv_k_a': 1.0 + nrm((L, RWKV_WIDTH), 0.02),
        'rwkv_r_k': nrm((L, N_RWKV_HEADS, HEAD_DIM), 0.1),
        'ln_x_w': 1.0 + nrm((L, RWKV_WIDTH), 0.02),
        'ln_x_b': nrm((L, RWKV_WIDTH), 0.02),
        'attn_sinks': nrm((L, N_Q_HEADS), 1.0),
        'w_out': nrm((L, MIX_WIDTH, D_MODEL), MIX_WIDTH ** -0.5),
        'norm_ffn2': 1.0 + nrm((L, D_MODEL), 0.02),
        'ffn2_w_gu': nrm((L, D_MODEL, 2 * D_FF), D_MODEL ** -0.5),
        'ffn2_w_down': nrm((L, D_FF, D_MODEL), D_FF ** -0.5),
        'norm_final': 1.0 + nrm((D_MODEL,), 0.02),
    }

def reference(x_prompt, x_sample, c_prompt, c_sample, state_wkv, state_shift, cache_k, cache_v,
              w_ada, b_ada, norm_ffn1, ffn1_w_gu, ffn1_w_down, norm_mix, w_in, mu_shift,
              rwkv_w0, rwkv_w2, rwkv_a0, rwkv_a2, rwkv_g2, rwkv_k_k, rwkv_k_a, rwkv_r_k,
              ln_x_w, ln_x_b, attn_sinks, w_out, norm_ffn2, ffn2_w_gu, ffn2_w_down, norm_final):
    xp, xs = x_prompt, x_sample
    bp = x_prompt.shape[0]
    p_states, s_states = [], []
    for l in range(DEPTH):
        lw = {'w_ada': w_ada[l], 'b_ada': b_ada[l], 'norm_ffn1': norm_ffn1[l],
              'ffn1_w_gu': ffn1_w_gu[l], 'ffn1_w_down': ffn1_w_down[l], 'norm_mix': norm_mix[l],
              'w_in': w_in[l], 'mu_shift': mu_shift[l], 'rwkv_w0': rwkv_w0[l], 'rwkv_w2': rwkv_w2[l],
              'rwkv_a0': rwkv_a0[l], 'rwkv_a2': rwkv_a2[l], 'rwkv_g2': rwkv_g2[l],
              'rwkv_k_k': rwkv_k_k[l], 'rwkv_k_a': rwkv_k_a[l], 'rwkv_r_k': rwkv_r_k[l],
              'ln_x_w': ln_x_w[l], 'ln_x_b': ln_x_b[l], 'attn_sinks': attn_sinks[l],
              'w_out': w_out[l], 'norm_ffn2': norm_ffn2[l], 'ffn2_w_gu': ffn2_w_gu[l],
              'ffn2_w_down': ffn2_w_down[l]}
        S0_p = jnp.zeros((bp, N_RWKV_HEADS, HEAD_DIM, HEAD_DIM), jnp.float32)
        u0_p = jnp.zeros((bp, RWKV_COLS), xp.dtype)
        xp, st_p = decoder_layer(xp, c_prompt, S0_p, u0_p, None, None, 0, lw)
        xs, st_s = decoder_layer(xs, c_sample, state_wkv[l], state_shift[l], cache_k[l], cache_v[l], PAST_LEN, lw)
        p_states.append(st_p)
        s_states.append(st_s)
    y_prompt = rms_norm(xp, norm_final)
    y_sample = rms_norm(xs, norm_final)
    prompt_wkv = jnp.stack([st[0] for st in p_states])
    prompt_shift = jnp.stack([st[1] for st in p_states])
    prompt_k = jnp.stack([st[2] for st in p_states])
    prompt_v = jnp.stack([st[3] for st in p_states])
    sample_wkv = jnp.stack([st[0] for st in s_states])
    sample_shift = jnp.stack([st[1] for st in s_states])
    sample_k = jnp.stack([st[2] for st in s_states])
    sample_v = jnp.stack([st[3] for st in s_states])
    return (y_prompt, y_sample, prompt_wkv, prompt_shift, prompt_k, prompt_v,
            sample_wkv, sample_shift, sample_k, sample_v)


_drawn_inputs = setup_inputs


def setup_inputs(seed=0):
    import zlib

    import numpy as np

    out = dict(_drawn_inputs(seed))
    spreads = {}
    factors = {'norm_ffn1': 8.0,
     'ln_x_w': 182.015,
     'ln_x_b': 183.311,
     'attn_sinks': 200.0,
     'norm_ffn2': 22.336,
     'norm_final': 23.459,
     'rwkv_r_k': 8.0}
    for name, (base, spread) in spreads.items():
        noise = np.random.default_rng([zlib.crc32(name.encode()), seed]).standard_normal(out[name].shape)
        drawn = base * np.exp(spread * noise) if base else spread * noise
        out[name] = __import__('jax').numpy.asarray(drawn.astype(out[name].dtype))
    for name, factor in factors.items():
        out[name] = (out[name] * factor).astype(out[name].dtype)
    return out
```

```python
from contextlib import ExitStack

import numpy as np

import concourse.bass as bass
from concourse import mybir

F32 = mybir.dt.float32
F32R = mybir.dt.float32r
ALU = mybir.AluOpType
ACT = mybir.ActivationFunctionType
AX = mybir.AxisListType

P = 128
D = 1024
KD = D // P
NP_TOK = 1024
NSEQ = 8
TSEQ = 8
NS_TOK = NSEQ * TSEQ
T = NP_TOK + NS_TOK
D_FF = 2816
N_ADA = 9
HD = 64
RW = 512
PAIRS = RW // P
U_COLS = 1792
UC = U_COLS // P
WINDOW = 128
EPS = 1e-5
LNX_EPS = 64e-5

TILES = [(0, 364), (364, 364), (728, 360)]
TW = 364
NT = len(TILES)

LEVELS = (1, 2, 4, 8, 16, 32)
UW = 1 + NP_TOK + NSEQ * (TSEQ + 1)
W = UW - 1

ROWS1 = [("b_ada", N_ADA * KD), ("norm_ffn1", KD), ("norm_mix", KD), ("norm_ffn2", KD), ("norm_final", KD)]
ROWS2 = [("mu_shift", UC), ("rwkv_w0", PAIRS), ("rwkv_a0", PAIRS), ("rwkv_k_k", PAIRS), ("rwkv_k_a", PAIRS),
         ("rwkv_r_k", PAIRS), ("ln_x_w", PAIRS), ("ln_x_b", PAIRS)]


def row_starts(rows):
    at, out = 0, {}
    for name, n in rows:
        out[name] = at
        at += n
    return out, at


AT1, N1 = row_starts(ROWS1)
AT2, N2 = row_starts(ROWS2)

BASE = 16512
KB = 1024
TB = T * 4
CONST_AT = BASE
X_AT = BASE + 17 * KB
HH_AT = X_AT + KD * TB
HL_AT = HH_AT + KD * TB
WT_AT = HL_AT + KD * TB
ACT_AT = WT_AT + 64 * KB
TMP_AT = ACT_AT + 4 * TB
END = 229368
SLOT = 1472


def up32(n):
    return (n + 31) // 32 * 32


def make_constants():
    p = np.arange(P)
    blk = (p[:, None] // HD) == (p[None, :] // HD)
    lo, lc = p % HD, np.arange(HD)
    out = {
        "ident": np.eye(P),
        "mean_all": np.full((P, P), 1.0 / D),
        "head_sum": blk * 1.0,
        "head_mean": blk / HD,
    }
    rot = np.zeros((P, P))
    for h in range(2):
        for j in range(8):
            rot[h * HD + 8 + j, h * HD + j] = -1.0
            rot[h * HD + j, h * HD + 8 + j] = 1.0
    out["rot"] = rot
    same = (lo[:, None] // TSEQ) == (lc[None, :] // TSEQ)
    before, upto = lo[:, None] < lc[None, :], lo[:, None] <= lc[None, :]
    out["causal"] = np.concatenate([before, upto], axis=1)
    out["causal_s"] = np.concatenate([before & same, upto & same], axis=1)
    for m in LEVELS:
        t, s = lo[:, None] // m, lo[None, :] // m
        out[f"lev{m}"] = blk & (t % 2 == 1) & (s == t - 1)
    out["lev1T"] = out["lev1"].T
    out["seq_of"] = (lo[:, None] // TSEQ) == np.arange(NSEQ)[None, :]
    q, k = p[:, None], np.arange(2 * WINDOW)[None, :]
    ok = (k - WINDOW <= q) & (q - (k - WINDOW) < WINDOW)
    out["mask_p"] = np.where(ok, 0.0, -1e30)
    out["mask_p0"] = np.where(ok & (k >= WINDOW), 0.0, -1e30)
    t, k = p[:, None] % TSEQ, np.arange(WINDOW + TSEQ)[None, :]
    out["ones"] = np.ones((P, P))
    out["eps"] = np.full((P, 1), EPS)
    out["row_chunk"] = np.zeros((P, P))
    out["row_chunk"][0:4] = np.arange(4)[:, None] == (p[None, :] % 32) // TSEQ
    out["mask_s"] = np.where((k > t) & (k - WINDOW <= t), 0.0, -1e30)
    return {n: np.ascontiguousarray(a, np.float32) for n, a in out.items()}


def scan_keep():
    keep = np.ones((P, W), np.float32)
    keep[:, 0:NP_TOK:HD] = 0.0
    keep[:, NP_TOK + 1::TSEQ + 1] = 0.0
    return keep


def rope_tables():
    pos = np.concatenate([np.arange(NP_TOK), np.tile(2048 + np.arange(TSEQ), NSEQ)]).astype(np.float32)
    inv = np.float32(500000.0) ** (-np.arange(0, 16, 2, dtype=np.float32) / np.float32(16))
    ang = (pos[None, :] * inv[:, None].astype(np.float32)).astype(np.float32)
    cos, sin = np.ones((P, T), np.float32), np.zeros((P, T), np.float32)
    for h in range(2):
        for part in range(2):
            at = h * HD + 8 * part
            cos[at:at + 8], sin[at:at + 8] = np.cos(ang), np.sin(ang)
    return cos, sin


CONST = make_constants()
CONST_COL = {}
_at = 0
for _n, _a in CONST.items():
    CONST_COL[_n] = (_at, _a.shape[1])
    _at += _a.shape[1]
NCONST = _at


class Core:

    def __init__(self, nc, dram, ctx):
        self.nc, self.dram, self.ctx = nc, dram, ctx
        self.phase_sems = []
        self.psum = [ctx.enter_context(nc.psum_tensor(f"bank{i}", [P, 512], F32)) for i in range(8)]
        self.const = self.at("const", CONST_AT, [P, NCONST])
        o = up32(CONST_AT + 4 * NCONST)
        self.mods = self.at("mods", o, [P, N_ADA * KD, 9])
        o = up32(o + 4 * N_ADA * KD * 9)
        self.par1 = self.at("par1", o, [P, N1])
        o = up32(o + 4 * N1)
        self.par2 = self.at("par2", o, [P, N2])
        o = up32(o + 4 * N2)
        self.p_end = self.at("p_end", o, [P, PAIRS, NP_TOK // HD + NSEQ])
        o = up32(o + 4 * PAIRS * (NP_TOK // HD + NSEQ))
        assert o <= X_AT, o - CONST_AT
        self.x = self.at("x", X_AT, [P, KD, T])
        self.hh = self.at("hh", HH_AT, [P, KD, T], F32R)
        self.hl = self.at("hl", HL_AT, [P, KD, T], F32R)
        self.u = self.at("u", U_AT, [P, UC, UW])
        self.qkv = self.at("qkv", QKV_AT, [P, 6, T])

    def at(self, name, off, shape, dt=F32):
        assert off % 4 == 0 and off + 4 * int(np.prod(shape[1:])) <= END, name
        return self.nc.alloc_sbuf_tensor_at(name, shape, dt, offset=off)

    def c(self, name):
        a, n = CONST_COL[name]
        return self.const[:, a:a + n]

    def sem(self, name):
        sem = self.nc.alloc_semaphore(name)
        self.phase_sems.append(sem)
        return sem

    def release(self, keep=()):
        self.nc.clear_and_free_semaphores([s for s in self.phase_sems if s not in keep])
        self.nc.all_engine_barrier()
        self.phase_sems = list(keep)

    def p1(self, name, i):
        return self.par1[:, AT1[name] + i:AT1[name] + i + 1]

    def p2(self, name, i):
        return self.par2[:, AT2[name] + i:AT2[name] + i + 1]

    def mod(self, i, k, s0=0, n=1):
        return self.mods[:, i * KD + k, s0:s0 + n]


def per_seq(ap):
    return ap.rearrange("p (s t) -> p s t", t=TSEQ)


def over_tokens(ap):
    return ap.unsqueeze(2).broadcast_to([P, NSEQ, TSEQ])


def load_and_modulate(k):
    d = k.dram
    rows1 = k.at("rows1", TMP_AT, [P, P])
    rows2 = k.at("rows2", TMP_AT + 512, [P, P])
    c_rows = k.at("c_rows", ACT_AT, [9, D])
    c_silu = k.at("c_silu", ACT_AT + 4096, [9, D])
    x_in = [k.at(f"x_in{j}", ACT_AT + 8192 + 4096 * j, [P, D]) for j in range(2)]
    cT = k.at("cT", TMP_AT + 1024, [P, KD, 32])
    mod_rows = k.at("mod_rows", TMP_AT + 2048, [P, 2 * P])
    NQ = KD // 2
    w_ada = [k.at(f"w_ada{q}", WT_AT + 8 * KB * q, [P, 2, D]) for q in range(NQ)]

    const_in, rows_in, c_in = k.sem("const_in"), k.sem("rows_in"), k.sem("c_in")
    silu_done, par_mm, par_done, c_mm, c_done = (k.sem(n) for n in ("silu_done", "par_mm", "par_done", "c_mm", "c_done"))
    x_in_done = [k.sem(f"x_in_done{j}") for j in range(2)]
    xt_mm, xt_free = k.sem("xt_mm"), k.sem("xt_free")
    ada_in = [k.sem(f"ada_in{q}") for q in range(NQ)]
    ada_used, ada_mm, ada_rows, ada_turned, ada_free = (
        k.sem(n) for n in ("ada_used", "ada_mm", "ada_rows", "ada_turned", "ada_free"))
    mods_done = k.sem("mods_done")
    w_ada_view = d["w_ada"][0].rearrange("(q k p) (i n) -> q p i k n", p=P, k=2, n=D)

    with k.nc.Block() as block:
        @block.sync
        def _(sp):
            sp.dma_start(c_rows[0:1, :], d["c_prompt"]).then_inc(c_in, 16)
            sp.dma_start(c_rows[1:9, :], d["c_sample"]).then_inc(c_in, 16)
            sp.dma_start(k.const[:], d["consts"]).then_inc(const_in, 16)
            for names, tile, at in ((ROWS1, rows1, AT1), (ROWS2, rows2, AT2)):
                for name, n in names:
                    src = d[name]
                    flat = src.rearrange("(n p) -> n p", p=P) if len(src.shape) == 1 else (
                        src[0].rearrange("(n p) -> n p", p=P) if len(src.shape) == 2 else
                        src[0].rearrange("(n h) i -> n (h i)", h=2))
                    sp.dma_start(tile[at[name]:at[name] + n, :], flat).then_inc(rows_in, 16)
            for q in range(NQ):
                sp.dma_start(w_ada[q][:], w_ada_view[q][:, 0]).then_inc(ada_in[q], 16)
            with sp.Fori(0, N_ADA - 1) as i:
                for q in range(NQ):
                    sp.wait_ge(ada_used, NQ * i + q + 1)
                    sp.dma_start(w_ada[q][:], w_ada_view[q][:, bass.ds(i + 1, 1)].rearrange("p o k n -> p (o k) n")
                                 ).then_inc(ada_in[q], 16)

        @block.gpsimd
        def _(pool):
            xv = d["x_prompt"][0].rearrange("(i j p) n -> j p i n", p=P, j=2)
            for j in range(2):
                pool.dma_start(x_in[j][:], xv[j][:, 0]).then_inc(x_in_done[j], 16)
            with pool.Fori(1, NP_TOK // P // 2) as i:
                for j in range(2):
                    pool.wait_ge(xt_mm, 2 * i + j - 1)
                    pool.dma_start(x_in[j][:], xv[j][:, bass.ds(i, 1)].rearrange("p o n -> p (o n)")
                                   ).then_inc(x_in_done[j], 16)
            pool.wait_ge(xt_mm, NP_TOK // P - 1)
            pool.dma_start(x_in[0][0:NS_TOK, :], d["x_sample"].rearrange("s t n -> (s t) n")).then_inc(x_in_done[0], 16)

        @block.scalar
        def _(act):
            act.wait_ge(c_in, 32)
            act.activation(c_silu[:], c_rows[:], ACT.Silu).then_inc(silu_done, 1)
            act.sem_inc(xt_free, 2)

            def evac(j, dst, n):
                for h in range(2):
                    ins = act.copy(dst[:, 4 * h:4 * h + 4, :], k.psum[2 + 2 * j + h][:, 0:4 * n].rearrange(
                        "p (c t) -> p c t", t=n))
                ins.then_inc(xt_free, 1)

            with act.Fori(0, NP_TOK // P // 2) as i:
                for j in range(2):
                    act.wait_ge(xt_mm, 2 * i + j + 1)
                    evac(j, k.x[:, :, bass.ds(256 * i + 128 * j, P)], P)
            act.wait_ge(xt_mm, NP_TOK // P + 1)
            evac(0, k.x[:, :, NP_TOK:T], NS_TOK)

        @block.tensor
        def _(pe):
            ident = k.c("ident")
            pe.wait_ge(const_in, 16)
            pe.wait_ge(rows_in, 16 * (len(ROWS1) + len(ROWS2)))
            pe.transpose(k.psum[0][:, 0:N1], rows1[0:N1, :], ident[0:N1, 0:N1])
            pe.transpose(k.psum[0][:, N1:N1 + N2], rows2[0:N2, :], ident[0:N2, 0:N2]).then_inc(par_mm, 1)
            pe.wait_ge(silu_done, 1)
            for c in range(KD):
                ins = pe.transpose(k.psum[1][:, 9 * c:9 * c + 9], c_silu[0:9, P * c:P * c + P], ident[0:9, 0:9])
            ins.then_inc(c_mm, 1)

            def turn(j, n):
                for c in range(KD):
                    ins = pe.transpose(k.psum[2 + 2 * j + c // 4][:, (c % 4) * n:(c % 4) * n + n],
                                       x_in[j][0:n, P * c:P * c + P], ident[0:n, 0:n])
                ins.then_inc(xt_mm, 1)

            with pe.Fori(0, NP_TOK // P // 2) as i:
                for j in range(2):
                    pe.wait_ge(x_in_done[j], 16 * i + 16)
                    pe.wait_ge(xt_free, 2 * i + j + 1)
                    turn(j, P)
            pe.wait_ge(x_in_done[0], 16 * (NP_TOK // P // 2) + 16)
            pe.wait_ge(xt_free, NP_TOK // P + 1)
            turn(0, NS_TOK)
            pe.wait_ge(c_done, 1)
            with pe.Fori(0, N_ADA) as i:
                pe.wait_ge(ada_free, i + 1)
                for q in range(NQ):
                    pe.wait_ge(ada_in[q], 16 * i + 16)
                    for h in range(2):
                        for j in range(4):
                            ins = pe.matmul(k.psum[6][32 * j:32 * j + 32, 0:256], cT[:, 2 * q + h, :],
                                            w_ada[q][:, h, 256 * j:256 * j + 256],
                                            start=(q == 0 and h == 0), stop=(q == NQ - 1 and h == 1))
                    ins.then_inc(ada_used, 1)
                pe.wait_ge(ada_rows, i + 1)
                for h in range(2):
                    ins = pe.transpose(k.psum[7][:, P * h:P * h + P], mod_rows[:, P * h:P * h + P], ident)
                ins.then_inc(ada_turned, 1)

        @block.vector
        def _(dve):
            dve.memset(cT[:], 0.0)
            dve.drain()
            dve.wait_ge(par_mm, 1)
            dve.tensor_copy(k.par1[:], k.psum[0][:, 0:N1])
            dve.tensor_copy(k.par2[:], k.psum[0][:, N1:N1 + N2]).then_inc(par_done, 1)
            dve.wait_ge(c_mm, 1)
            dve.tensor_copy(cT[:, :, 0:9], k.psum[1][:, 0:9 * KD].rearrange("p (c s) -> p c s", s=9)).then_inc(c_done, 1)
            dve.drain()
            dve.sem_inc(ada_free, 1)
            with dve.Fori(0, N_ADA) as i:
                dve.wait_ge(ada_used, NQ * i + NQ)
                dve.tensor_copy(mod_rows[:], k.psum[6][:, 0:256]).then_inc(ada_rows, 1)
                dve.wait_ge(ada_turned, i + 1)
                dve.tensor_tensor(k.mods[:, bass.ds(KD * i, KD), :].rearrange("p (j h) s -> p j h s", h=2),
                                  k.psum[7][:, 0:256].rearrange("p (h j s) -> p j h s", h=2, j=4)[:, :, :, 0:9],
                                  k.par1[:, bass.ds(KD * i, KD)].rearrange("p (j h) -> p j h", h=2).unsqueeze(3)
                                  .broadcast_to([P, 4, 2, 9]), ALU.add).then_inc(ada_free, 1)
            dve.drain()
            for i, name in ((1, "norm_ffn1"), (4, "norm_mix"), (7, "norm_ffn2")):
                g = k.par1[:, AT1[name]:AT1[name] + KD].unsqueeze(2).broadcast_to([P, KD, 9])
                dve.scalar_tensor_tensor(k.mods[:, i * KD:(i + 1) * KD, :], k.mods[:, i * KD:(i + 1) * KD, :], 1.0, g,
                                         ALU.add, ALU.mult)
            for i in (2, 8):
                ins = dve.tensor_scalar(k.mods[:, i * KD:(i + 1) * KD, :], k.mods[:, i * KD:(i + 1) * KD, :],
                                        0.5, None, ALU.mult)
            ins.then_inc(mods_done, 1)
            dve.wait_ge(mods_done, 1)


class Norm:

    def __init__(self, k, name, i_shift, at):
        self.k, self.i_shift = k, i_shift
        self.sq = [k.at(f"{name}_sq{j}", at + 4 * SLOT * j, [P, KD // 2, TW]) for j in range(2)]
        at += 8 * SLOT
        self.rstd = [k.at(f"{name}_rstd{j}", at + SLOT * j, [P, TW]) for j in range(2)]
        at += 2 * SLOT
        self.t = [k.at(f"{name}_t{j}", at + SLOT * j, [P, TW]) for j in range(4)]
        at += 4 * SLOT
        self.ts = k.at(f"{name}_ts", at, [P, KD, NS_TOK])
        (self.sq_done, self.sq_used, self.root_done, self.t_done, self.hi_done, self.lo_done) = (
            k.sem(f"{name}_{n}") for n in ("sq_done", "sq_used", "root_done", "t_done", "hi_done", "lo_done"))

    def spans(self, t):
        a, n = TILES[t]
        return a, min(n, NP_TOK - a)

    def act_squares(self, act, t):
        a, n = TILES[t]
        for j in range(2):
            if t >= 1:
                act.wait_ge(self.sq_used, 2 * t + j - 1)
            act.activation(self.sq[j][:, :, 0:n], self.k.x[:, 4 * j:4 * j + 4, a:a + n], ACT.Square
                           ).then_inc(self.sq_done, 1)

    def act_root(self, act, t):
        n = TILES[t][1]
        act.wait_ge(self.sq_used, 2 * t + 2)
        if t >= 2:
            act.wait_ge(self.t_done, KD * (t - 1))
        act.activation(self.rstd[t % 2][:, 0:n], self.k.psum[t][:, 0:n], ACT.Sqrt, bias=self.k.c("eps")
                       ).then_inc(self.root_done, 1)

    def act_heads(self, act, t):
        a, n = self.spans(t)
        for c in range(KD):
            act.wait_ge(self.t_done, KD * t + c + 1)
            act.activation(self.k.hh[:, c, a:a + n], self.t[c % 4][:, 0:n], ACT.Identity,
                           bias=self.k.mod(self.i_shift, c)).then_inc(self.hi_done, 1)

    def act(self, act):
        self.act_squares(act, 0)
        self.act_squares(act, 1)
        self.act_root(act, 0)
        self.act_squares(act, 2)
        self.act_heads(act, 0)
        self.act_root(act, 1)
        self.act_heads(act, 1)
        self.act_root(act, 2)
        self.act_heads(act, 2)

    def pe(self, pe):
        for t, (a, n) in enumerate(TILES):
            for c in range(KD):
                if c % 4 == 0:
                    pe.wait_ge(self.sq_done, 2 * t + c // 4 + 1)
                ins = pe.matmul(self.k.psum[t][:, 0:n], self.k.c("mean_all"), self.sq[c // 4][:, c % 4, 0:n],
                                start=(c == 0), stop=(c == KD - 1))
                if c % 4 == 3:
                    ins.then_inc(self.sq_used, 1)

    def pe_ready(self, pe, t):
        pe.wait_ge(self.hi_done, KD * (t + 1))
        pe.wait_ge(self.lo_done, t + 1)

    def tail(self, dve, t, c):
        a, n = self.spans(t)
        dve.wait_ge(self.hi_done, KD * t + c + 1)
        return dve.scalar_tensor_tensor(self.k.hl[:, c, a:a + n], self.t[c % 4][:, 0:n], self.k.mod(self.i_shift, c),
                                        self.k.hh[:, c, a:a + n].bitcast(F32), ALU.add, ALU.subtract)

    def dve(self, dve, t):
        k, (a, n) = self.k, self.spans(t)
        rstd = self.rstd[t % 2]
        dve.wait_ge(self.root_done, t + 1)
        dve.reciprocal(rstd[:, 0:TILES[t][1]], rstd[:, 0:TILES[t][1]])
        dve.drain()
        for c in range(KD):
            if KD * t + c >= 4:
                dve.drain()
            dve.scalar_tensor_tensor(self.t[c % 4][:, 0:n], k.x[:, c, a:a + n], k.mod(self.i_shift + 1, c), rstd[:, 0:n],
                                     ALU.mult, ALU.mult).then_inc(self.t_done, 1)
            if c >= 2:
                self.tail(dve, t, c - 2)
        self.tail(dve, t, KD - 2)
        last = self.tail(dve, t, KD - 1)
        if t == NT - 1:
            ts4 = self.ts[:].rearrange("p c (s t) -> p c s t", t=TSEQ)

            def over(i):
                return k.mods[:, i * KD:(i + 1) * KD, 1:9].unsqueeze(3).broadcast_to([P, KD, NSEQ, TSEQ])

            dve.tensor_tensor(self.ts[:], k.x[:, :, NP_TOK:T],
                              rstd[:, n:n + NS_TOK].unsqueeze(1).broadcast_to([P, KD, NS_TOK]), ALU.mult)
            dve.drain()
            dve.tensor_tensor(ts4, ts4, over(self.i_shift + 1), ALU.mult)
            dve.drain()
            dve.tensor_tensor(ts4, ts4, over(self.i_shift), ALU.add)
            dve.drain()
            dve.tensor_copy(k.hh[:, :, NP_TOK:T], self.ts[:])
            dve.drain()
            last = dve.tensor_tensor(k.hl[:, :, NP_TOK:T], self.ts[:], k.hh[:, :, NP_TOK:T].bitcast(F32), ALU.subtract)
        last.then_inc(self.lo_done, 1)

    def wait_all(self, eng):
        eng.wait_ge(self.hi_done, KD * NT)
        eng.wait_ge(self.lo_done, NT)


def norm_final(k):
    sq = [k.at(f"nf_sq{j}", ACT_AT + TB * j, [P, T]) for j in range(2)]
    rstd = k.at("nf_rstd", TMP_AT, [P, T])
    sq_done, sq_used, root_done = (k.sem(f"nf_{n}") for n in ("sq_done", "sq_used", "root_done"))
    with k.nc.Block() as block:
        @block.scalar
        def _(act):
            for c in range(KD):
                if c >= 2:
                    act.wait_ge(sq_used, c - 1)
                act.activation(sq[c % 2][:], k.x[:, c, :], ACT.Square).then_inc(sq_done, 1)
            act.wait_ge(sq_used, KD)
            for i, (a, n) in enumerate(TILES):
                act.activation(rstd[:, a:a + n], k.psum[i][:, 0:n], ACT.Sqrt, bias=k.c("eps")).then_inc(root_done, 1)

        @block.tensor
        def _(pe):
            for c in range(KD):
                pe.wait_ge(sq_done, c + 1)
                for i, (a, n) in enumerate(TILES):
                    ins = pe.matmul(k.psum[i][:, 0:n], k.c("mean_all"), sq[c % 2][:, a:a + n],
                                    start=(c == 0), stop=(c == KD - 1))
                ins.then_inc(sq_used, 1)

        @block.vector
        def _(dve):
            for i, (a, n) in enumerate(TILES):
                dve.wait_ge(root_done, i + 1)
                dve.reciprocal(rstd[:, a:a + n], rstd[:, a:a + n])
                dve.drain()
                for c in range(KD):
                    dve.scalar_tensor_tensor(k.x[:, c, a:a + n], k.x[:, c, a:a + n], k.p1("norm_final", c),
                                             rstd[:, a:a + n], ALU.mult, ALU.mult)


def three_passes(pe, out, pairs):
    last = len(pairs) - 1
    for n, (wh, wl, rh, rl) in enumerate(pairs):
        pe.matmul(out, wh, rh, start=(n == 0), stop=False)
        pe.matmul(out, wh, rl, start=False, stop=False)
        ins = pe.matmul(out, wl, rh, start=False, stop=(n == last))
    return ins


def add_gated(dve, k, i_gate, c, tile, bank, scratch):
    a, n = TILES[tile]
    np_ = min(n, NP_TOK - a)
    if isinstance(c, int):
        x, gate = k.x[:, c, :], k.mods[:, i_gate * KD + c, :]
    else:
        x = k.x[:, bass.ds(c, 1), :].rearrange("p o n -> p (o n)")
        gate = k.mods[:, bass.ds(c + i_gate * KD, 1), :].rearrange("p o s -> p (o s)")
    ins = dve.scalar_tensor_tensor(x[:, a:a + np_], bank[:, 0:np_], gate[:, 0:1], x[:, a:a + np_], ALU.mult, ALU.add)
    if np_ < n:
        ins = dve.tensor_tensor(per_seq(scratch), per_seq(bank[:, np_:n]), over_tokens(gate[:, 1:9]), ALU.mult)
        dve.drain()
        dve.tensor_tensor(x[:, NP_TOK:T], x[:, NP_TOK:T], scratch, ALU.add)
    return ins


def ffn(k, name, w_gu, w_down, i_shift):
    nc = k.nc
    i_gate = i_shift + 2
    norm = Norm(k, name, i_shift, ACT_AT)
    FC = 2
    NGRP = D_FF // P // FC
    NU = FC * NT
    ND = KD * NT
    up_raw = k.at(f"{name}_up_raw", WT_AT, [P, KD, 2, P])
    up_hi = [k.at(f"{name}_up_hi{j}", WT_AT + (8 + 16 * j) * KB, [P, KD, 2, P], F32R) for j in range(FC)]
    up_lo = [k.at(f"{name}_up_lo{j}", WT_AT + (16 + 16 * j) * KB, [P, KD, 2, P], F32R) for j in range(FC)]
    dn_raw = k.at(f"{name}_dn_raw", WT_AT + 40 * KB, [P, FC, D])
    dn_hi = k.at(f"{name}_dn_hi", WT_AT + 48 * KB, [P, FC, D], F32R)
    dn_lo = k.at(f"{name}_dn_lo", WT_AT + 56 * KB, [P, FC, D], F32R)
    a_hi = k.at(f"{name}_a_hi", ACT_AT, [P, FC, T], F32R)
    a_lo = k.at(f"{name}_a_lo", ACT_AT + 2 * TB, [P, FC, T], F32R)
    silu = [k.at(f"{name}_silu{j}", TMP_AT + SLOT * j, [P, TW]) for j in range(2)]
    prod = [k.at(f"{name}_prod{j}", TMP_AT + SLOT * (2 + j), [P, TW]) for j in range(2)]
    scratch = k.at(f"{name}_scratch", TMP_AT + 4 * SLOT, [P, 2, NS_TOK])
    up_in, up_hi_done, up_lo_done = (k.sem(f"{name}_{n}") for n in ("up_in", "up_hi_done", "up_lo_done"))
    dn_in, dn_hi_done, dn_lo_done = (k.sem(f"{name}_{n}") for n in ("dn_in", "dn_hi_done", "dn_lo_done"))
    gate_mm, up_mm, gate_free, up_free = (k.sem(f"{name}_{n}") for n in ("gate_mm", "up_mm", "gate_free", "up_free"))
    act_done, dn_mm, dn_free = (k.sem(f"{name}_{n}") for n in ("act_done", "dn_mm", "dn_free"))
    gu = w_gu[0].rearrange("(k p) (h f n) -> p f k h n", p=P, h=2, n=P)
    dn = w_down[0].rearrange("(g c p) n -> p g c n", p=P, c=FC)

    with nc.Block() as block:
        @block.sync
        def _(sp):
            def load_up(f):
                for h in range(2):
                    sp.dma_start(up_raw[:, :, h, :], gu[:, f, :, h].rearrange("p o k n -> p (o k) n") if not isinstance(f, int)
                                 else gu[:, f, :, h]).then_inc(up_in, 16)

            sp.dma_start(dn_raw[:], dn[:, 0]).then_inc(dn_in, 16)
            load_up(0)
            sp.wait_ge(up_lo_done, 1)
            load_up(1)
            with sp.Fori(0, NGRP - 1) as g:
                for j in range(FC):
                    sp.wait_ge(up_lo_done, FC * g + j + 2)
                    load_up(bass.ds(FC * g + FC + j, 1))
                sp.wait_ge(dn_lo_done, g + 1)
                sp.dma_start(dn_raw[:], dn[:, bass.ds(g + 1, 1)].rearrange("p o c n -> p (o c) n")).then_inc(dn_in, 16)

        @block.gpsimd
        def _(pool):
            def up_tail(j, count):
                pool.wait_ge(up_hi_done, count)
                pool.tensor_tensor(up_lo[j][:], up_raw[:], up_hi[j][:].bitcast(F32), ALU.subtract
                                   ).then_inc(up_lo_done, 1)

            def dn_tail(count):
                pool.wait_ge(dn_hi_done, count)
                pool.tensor_tensor(dn_lo[:], dn_raw[:], dn_hi[:].bitcast(F32), ALU.subtract).then_inc(dn_lo_done, 1)

            up_tail(0, 1)
            up_tail(1, 2)
            dn_tail(1)
            with pool.Fori(0, NGRP - 1) as g:
                up_tail(0, FC * g + 3)
                up_tail(1, FC * g + 4)
                dn_tail(g + 2)

        @block.tensor
        def _(pe):
            def group(g):
                for j in range(FC):
                    pe.wait_ge(up_lo_done, FC * g + j + 1)
                    for t, (a, n) in enumerate(TILES):
                        u = NT * j + t
                        if isinstance(g, int) and j == 0:
                            norm.pe_ready(pe, t)
                        for h, (free, done) in enumerate(((gate_free, gate_mm), (up_free, up_mm))):
                            pe.wait_ge(free, NU * g + u + 1)
                            three_passes(pe, k.psum[2 * (u % 2) + h][:, 0:n],
                                         [(up_hi[j][:, c, h, :], up_lo[j][:, c, h, :], k.hh[:, c, a:a + n],
                                           k.hl[:, c, a:a + n]) for c in range(KD)]).then_inc(done, 1)
                pe.wait_ge(dn_lo_done, g + 1)
                for t, (a, n) in enumerate(TILES):
                    pe.wait_ge(act_done, NU * g + NT * (FC - 1) + t + 1)
                    for c in range(KD):
                        v = KD * t + c
                        pe.wait_ge(dn_free, ND * g + v + 1)
                        three_passes(pe, k.psum[4 + v % 4][:, 0:n],
                                     [(dn_hi[:, f, P * c:P * c + P], dn_lo[:, f, P * c:P * c + P],
                                       a_hi[:, f, a:a + n], a_lo[:, f, a:a + n]) for f in range(FC)]
                                     ).then_inc(dn_mm, 1)

            norm.pe(pe)
            group(0)
            with pe.Fori(1, NGRP) as g:
                group(g)

        @block.scalar
        def _(act):
            norm.act(act)
            norm.wait_all(act)
            act.sem_inc(gate_free, 2)
            with act.Fori(0, NGRP) as g:
                for u in range(NU):
                    n = TILES[u % NT][1]
                    act.wait_ge(gate_mm, NU * g + u + 1)
                    act.wait_ge(up_free, NU * g + u + 1)
                    act.activation(silu[u % 2][:, 0:n], k.psum[2 * (u % 2)][:, 0:n], ACT.Silu).then_inc(gate_free, 1)

        @block.vector
        def _(dve):
            def up_head(j, count, used):
                dve.wait_ge(up_in, 32 * count)
                if used is not None:
                    dve.wait_ge(up_mm, used)
                dve.tensor_copy(up_hi[j][:], up_raw[:]).then_inc(up_hi_done, 1)

            def dn_head(count, used):
                dve.wait_ge(dn_in, 16 * count)
                if used is not None:
                    dve.wait_ge(dn_mm, used)
                dve.tensor_copy(dn_hi[:], dn_raw[:]).then_inc(dn_hi_done, 1)

            def group(g, last):
                for j in range(FC):
                    for t, (a, n) in enumerate(TILES):
                        u = NT * j + t
                        dve.wait_ge(gate_free, NU * g + u + 3)
                        dve.wait_ge(up_mm, NU * g + u + 1)
                        dve.tensor_tensor(prod[u % 2][:, 0:n], silu[u % 2][:, 0:n], k.psum[2 * (u % 2) + 1][:, 0:n],
                                          ALU.mult).then_inc(up_free, 1)
                        dve.drain()
                        dve.tensor_copy(a_hi[:, j, a:a + n], prod[u % 2][:, 0:n])
                        dve.drain()
                        dve.tensor_tensor(a_lo[:, j, a:a + n], prod[u % 2][:, 0:n], a_hi[:, j, a:a + n].bitcast(F32),
                                          ALU.subtract).then_inc(act_done, 1)
                    if not last:
                        up_head(j, FC * g + FC + j + 1, NU * g + NT * (j + 1))
                for v in range(ND):
                    t, c = v // KD, v % KD
                    dve.wait_ge(dn_mm, ND * g + v + 1)
                    add_gated(dve, k, i_gate, c, t, k.psum[4 + v % 4], scratch[:, v % 2]).then_inc(dn_free, 1)
                if not last:
                    dn_head(g + 2, ND * g + ND)

            dve.sem_inc(dn_free, 4)
            dve.sem_inc(up_free, 2)
            up_head(0, 1, None)
            dn_head(1, None)
            norm.dve(dve, 0)
            up_head(1, 2, None)
            norm.dve(dve, 1)
            norm.dve(dve, 2)
            norm.wait_all(dve)
            with dve.Fori(0, NGRP - 1) as g:
                group(g, False)
            group(NGRP - 1, True)


def each(eng, n, body, base):
    if n == 1:
        body(base, 0)
        return
    with eng.Fori(0, n) as i:
        body(i + base, i)


def stream_product(k, name, at, sections, rhs_hi, rhs_lo, evac_on_act, norm=None):
    raw = [k.at(f"{name}_raw{j}", at + 4 * KB * j, [P, KD, P]) for j in range(2)]
    hi = [k.at(f"{name}_hi{j}", at + 4 * KB * (2 + j), [P, KD, P], F32R) for j in range(2)]
    lo = [k.at(f"{name}_lo{j}", at + 4 * KB * (4 + j), [P, KD, P], F32R) for j in range(2)]
    raw_in = [k.sem(f"{name}_raw_in{j}") for j in range(2)]
    hi_done, lo_done, mm_done, bank_free = (k.sem(f"{name}_{n}") for n in ("hi_done", "lo_done", "mm_done", "bank_free"))
    dmas = sections[0][1](None, None, 0, 0, None)
    spilled = k.sem(f"{name}_spilled") if norm is not None else None

    def run(eng, body, after_first=None):
        base = 0
        for n, load, evac in sections:
            each(eng, n, lambda g, i: body(g, i, load, evac), base)
            if base == 0 and after_first is not None:
                after_first()
            base += n

    def norm_tiles(dve):
        for t in range(NT):
            norm.dve(dve, t)

    def heads(eng):
        def body(g, i, load, evac):
            for j in range(2):
                eng.wait_ge(raw_in[j], 16 * dmas * (g + 1))
                eng.wait_ge(mm_done, 6 * g + 3 * j + 3)
                copy = eng.copy if evac_on_act is False else eng.tensor_copy
                copy(hi[j][:], raw[j][:]).then_inc(hi_done, 1)
        run(eng, body, None if norm is None else lambda: norm_tiles(eng))

    def evacs(eng):
        if norm is not None:
            norm.act(eng)
            norm.wait_all(eng)
            eng.wait_ge(spilled, 16)
        eng.sem_inc(bank_free, 6)

        def body(g, i, load, evac):
            for j in range(2):
                for t in range(NT):
                    eng.wait_ge(mm_done, 6 * g + 3 * j + t + 7)
                    evac(eng, i, j, t, k.psum[3 * j + t]).then_inc(bank_free, 1)
        run(eng, body)

    with k.nc.Block() as block:
        @block.sync
        def _(sp):
            def body(g, i, load, evac):
                for j in range(2):
                    sp.wait_ge(lo_done, 2 * g + j + 1)
                    load(sp, raw[j], i, j, raw_in[j])
            run(sp, body)

        @block.gpsimd
        def _(pool):
            pool.sem_inc(lo_done, 2)
            if norm is not None:
                pool.dma_start(k.dram["x_spill"], k.x[:]).then_inc(spilled, 16)

            def body(g, i, load, evac):
                for j in range(2):
                    pool.wait_ge(hi_done, 2 * g + j + 1)
                    pool.tensor_tensor(lo[j][:], raw[j][:], hi[j][:].bitcast(F32), ALU.subtract).then_inc(lo_done, 1)
            run(pool, body)

        @block.tensor
        def _(pe):
            pe.sem_inc(mm_done, 6)
            if norm is not None:
                norm.pe(pe)

            def body(g, i, load, evac):
                for j in range(2):
                    pe.wait_ge(lo_done, 2 * g + j + 3)
                    for t, (a, n) in enumerate(TILES):
                        if norm is not None and isinstance(g, int) and g == 0 and j == 0:
                            norm.pe_ready(pe, t)
                        pe.wait_ge(bank_free, 6 * g + 3 * j + t + 1)
                        three_passes(pe, k.psum[3 * j + t][:, 0:n],
                                     [(hi[j][:, c], lo[j][:, c], rhs_hi[:, c, a:a + n], rhs_lo[:, c, a:a + n])
                                      for c in range(KD)]).then_inc(mm_done, 1)
            run(pe, body)

        @block.scalar
        def _(act):
            (evacs if evac_on_act else heads)(act)

        @block.vector
        def _(dve):
            (heads if evac_on_act else evacs)(dve)


QKV_AT = X_AT
R1_AT = X_AT + 6 * TB
U_AT = WT_AT
R2_AT = U_AT + 60 * KB
UB = W * 4


def input_projection(k):
    w = k.dram["w_in"][0]
    wu = w[:, 0:U_COLS].rearrange("(k p) (f n) -> p f k n", p=P, n=P)
    wq = w[:, U_COLS:U_COLS + RW].rearrange("(k p) (h c n) -> p c k h n", p=P, h=2, n=HD)
    wkv = w[:, U_COLS + RW:].rearrange("(k p) (f n) -> p f k n", p=P, n=P)

    def load_u(f0):
        def load(sp, raw, i, j, sem):
            if sp is not None:
                sp.dma_start(raw[:], wu[:, bass.ds(2 * i + f0 + j, 1)].rearrange("p o k n -> p (o k) n")).then_inc(sem, 32)
            return 2
        return load

    def load_q(sp, raw, i, j, sem):
        for h in range(2):
            sp.dma_start(raw[:, :, HD * h:HD * h + HD],
                         wq[:, bass.ds(2 * i + j, 1), :, h].rearrange("p o k n -> p (o k) n")).then_inc(sem, 16)
        return 2

    def load_kv(sp, raw, i, j, sem):
        sp.dma_start(raw[:], wkv[:, j]).then_inc(sem, 32)
        return 2

    def evac_u(f0):
        def evac(act, i, j, t, bank):
            a, n = TILES[t]
            np_ = min(n, NP_TOK - a)
            row = k.u[:, bass.ds(2 * i + f0 + j, 1), :].rearrange("p o n -> p (o n)")
            ins = act.copy(row[:, 1 + a:1 + a + np_], bank[:, 0:np_])
            if np_ < n:
                ins = act.copy(row[:, 1 + NP_TOK:UW].rearrange("p (s t) -> p s t", t=TSEQ + 1)[:, :, 1:],
                               per_seq(bank[:, np_:n]))
            return ins
        return evac

    def evac_qkv(c0):
        def evac(act, i, j, t, bank):
            a, n = TILES[t]
            f = c0 + 2 * i + j
            dst = k.qkv[:, f, a:a + n] if isinstance(f, int) else \
                k.qkv[:, bass.ds(f, 1), a:a + n].rearrange("p o n -> p (o n)")
            return act.copy(dst, bank[:, 0:n])
        return evac

    stream_product(k, "w_in", R2_AT, [(1, load_u(0), evac_u(0)), (UC // 2 - 1, load_u(2), evac_u(2)), (2, load_q, evac_qkv(0)), (1, load_kv, evac_qkv(4))],
                   k.hh, k.hl, True, Norm(k, "mix", 3, U_AT))


def attention_prepare(k):
    d = k.dram
    o = R1_AT
    k.cos, k.sin = k.at("cos", o, [P, T]), k.at("sin", o + TB, [P, T])
    o += 2 * TB
    k.k_bd = k.at("k_bd", o, [P, 2, WINDOW + NP_TOK]); o += 9216
    k.v_tok = k.at("v_tok", o, [P, 9, 2, 3 * HD]); o += 13824
    tmp = [k.at(f"rope_tmp{j}", o + TB * j, [P, T]) for j in range(2)]
    k.scrap = o
    o += 2 * TB
    k.q_now = k.at("q_now", o, [P, 4, P]); o += 2048
    k.v_now = k.at("v_now", o, [P, 2, 2, 3 * HD]); o += 3072
    k.prob = k.at("prob", o, [P, 4, 2, 2 * WINDOW]); o += 8192
    k.diag = k.at("diag", o, [P, 8, P]); o += 4096
    k.probT = [k.at(f"probT{j}", o + 2048 * j, [P, 4, P]) for j in range(2)]; o += 4096
    k.v_new = k.at("v_new", o, [P, NSEQ, 2, 3 * HD]); o += 12288
    k.prob_s = k.at("prob_s", o, [P, 2, 2, WINDOW + TSEQ]); o += 2176
    small_at = o
    o = R2_AT
    k.ks_bd = k.at("ks_bd", o, [P, NSEQ, 2, WINDOW + TSEQ]); o += 8704
    k.q_pad = k.at("q_pad", o, [P, NSEQ, P]); o += 4096
    k.kc = k.at("kc", o, [P, NSEQ, P]); o += 4096
    k.v_cache = k.at("v_cache", o, [P, NSEQ, 2, 3 * HD]); o += 12288
    assert o <= END
    o = small_at
    small = k.at("small", o, [P, 64]); o += 256
    k.small = small
    k.k_rows = k.at("k_rows", o, [P, 2, P]); o += 1024
    k.sink_row = k.at("sink_row", o, [1, 8]); o += 32
    k.sink4 = k.at("sink4", o, [4, 2]); o += 32
    k.sink_p = k.at("sink_p", o, [P, 4, 2]); o += 32
    k.sink_s = k.at("sink_s", o, [P, 2]); o += 32
    assert o <= X_AT + KD * TB * 3, o
    tab_in, cache_in, sink_in = k.sem("tab_in"), k.sem("cache_in"), k.sem("sink_in")
    zeroed, rot_mm, rot_used, roped, turned, turn_used, rows_done, cache_out = (
        k.sem(n) for n in ("zeroed", "rot_mm", "rot_used", "roped", "turned", "turn_used", "rows_done", "cache_out"))
    k.cache_out = cache_out

    with k.nc.Block() as block:
        @block.sync
        def _(sp):
            sp.dma_start(k.cos[:], d["cos"]).then_inc(tab_in, 16)
            sp.dma_start(k.sin[:], d["sin"]).then_inc(tab_in, 16)
            sinks = d["attn_sinks"]
            sp.dma_start(k.sink_row[:], sinks).then_inc(sink_in, 16)
            for h in range(2):
                sp.dma_start(k.sink4[:, h:h + 1], sinks[:, 4 * h:4 * h + 4].rearrange("o c -> c o")).then_inc(sink_in, 16)
            sp.dma_start(k.kc[:], d["cache_k"][0].rearrange("s w h n -> w s (h n)")).then_inc(cache_in, 16)
            sp.wait_ge(zeroed, 4)
            for h in range(2):
                sp.dma_start(k.v_cache[:, :, h, HD:2 * HD], d["cache_v"][0, :, :, h].rearrange("s w n -> w s n")
                             ).then_inc(cache_in, 16)
            for src, dst in (("cache_k", "sample_k"), ("cache_v", "sample_v")):
                sp.dma_start(d[dst][0, :, 0:WINDOW - TSEQ].rearrange("s w h n -> s (w h n)"),
                             d[src][0, :, TSEQ:WINDOW].rearrange("s w h n -> s (w h n)")).then_inc(cache_out, 16)
            sp.wait_ge(rows_done, 1)
            sp.dma_start(d["prompt_k"][0, 0].rearrange("w h n -> w (h n)"), k.k_rows[:, 0]).then_inc(cache_out, 16)
            for s in range(NSEQ):
                sp.dma_start(d["sample_k"][0, s, WINDOW - TSEQ:WINDOW].rearrange("w h n -> w (h n)"),
                             k.k_rows[TSEQ * s:TSEQ * s + TSEQ, 1]).then_inc(cache_out, 16)
            sp.wait_ge(turn_used, 6)
            sp.dma_start(d["prompt_v"][0, 0], k.v_tok[:, 8, :, HD:2 * HD]).then_inc(cache_out, 16)
            for h in range(2):
                sp.dma_start(d["sample_v"][0, :, WINDOW - TSEQ:WINDOW, h].rearrange("s w n -> w s n"),
                             k.v_new[0:TSEQ, :, h, HD:2 * HD]).then_inc(cache_out, 16)
            k.n_cache_out = 2 + 1 + NSEQ + 1 + 2

        @block.gpsimd
        def _(pool):
            for t in (k.v_cache, k.k_bd, k.v_tok, k.v_new):
                pool.memset(t[:], 0.0).then_inc(zeroed, 1)
            for t in (k.ks_bd, k.q_pad):
                pool.memset(t[:], 0.0).then_inc(zeroed, 1)

        @block.tensor
        def _(pe):
            for c in range(5):
                if c >= 2:
                    pe.wait_ge(rot_used, c - 1)
                for t, (a, n) in enumerate(TILES):
                    ins = pe.matmul(k.psum[3 * (c % 2) + t][:, 0:n], k.c("rot"), k.qkv[:, c, a:a + n], start=True, stop=True)
                ins.then_inc(rot_mm, 1)
            ident = k.c("ident")
            for g in range(2):
                for b in range(4):
                    ins = pe.transpose(k.psum[6 + g][:, P * b:P * b + P],
                                       k.qkv[:, 5, P * (4 * g + b):P * (4 * g + b) + P], ident)
                ins.then_inc(turned, 1)
            pe.wait_ge(rot_used, 4)
            for g in range(2):
                for b in range(4):
                    at = NP_TOK + TSEQ * (4 * g + b)
                    ins = pe.transpose(k.psum[3 + g][0:TSEQ, P * b:P * b + P], k.qkv[:, 5, at:at + TSEQ], ident)
                ins.then_inc(turned, 1)
            pe.wait_ge(roped, 5)
            pe.transpose(k.psum[5][:, 0:P], k.qkv[:, 4, NP_TOK - P:NP_TOK], ident)
            pe.transpose(k.psum[5][0:NS_TOK, P:2 * P], k.qkv[:, 4, NP_TOK:T], ident)
            pe.wait_ge(sink_in, 48)
            pe.matmul(k.psum[5][:, 256:264], k.c("ones")[0:1, :], k.sink_row[:], start=True, stop=True)
            pe.matmul(k.psum[5][:, 264:266], k.c("row_chunk")[0:4, :], k.sink4[:], start=True, stop=True).then_inc(turned, 1)
            pe.wait_ge(cache_in, 48)
            pe.wait_ge(turn_used, 2)
            for g in range(2):
                for b in range(4):
                    ins = pe.transpose(k.psum[6 + g][:, P * b:P * b + P], k.kc[:, 4 * g + b], ident)
                ins.then_inc(turned, 1)

        @block.vector
        def _(dve):
            dve.wait_ge(tab_in, 32)
            for c in range(5):
                dve.wait_ge(rot_mm, c + 1)
                for t, (a, n) in enumerate(TILES):
                    ins = dve.tensor_tensor(tmp[c % 2][:, a:a + n], k.psum[3 * (c % 2) + t][:, 0:n], k.sin[:, a:a + n],
                                            ALU.mult)
                ins.then_inc(rot_used, 1)
                dve.tensor_tensor(k.qkv[:, c, :], k.qkv[:, c, :], k.cos[:], ALU.mult)
                dve.drain()
                dve.tensor_tensor(k.qkv[:, c, :], k.qkv[:, c, :], tmp[c % 2][:], ALU.add).then_inc(roped, 1)
                dve.drain()
            dve.wait_ge(zeroed, 6)
            for h in range(2):
                r = slice(HD * h, HD * h + HD)
                dve.tensor_copy(k.k_bd[r, h, WINDOW:], k.qkv[r, 4, 0:NP_TOK])
                dve.tensor_copy(k.ks_bd[r, :, h, WINDOW:], per_seq(k.qkv[r, 4, NP_TOK:T]))
            for s in range(NSEQ):
                dve.tensor_copy(k.q_pad[:, s, 32 * (s % 4):32 * (s % 4) + 32].rearrange("p (c t) -> p c t", t=TSEQ),
                                k.qkv[:, 0:4, NP_TOK + TSEQ * s:NP_TOK + TSEQ * s + TSEQ])

        @block.scalar
        def _(act):
            act.wait_ge(zeroed, 4)
            for g in range(2):
                act.wait_ge(turned, g + 1)
                act.copy(k.v_tok[:, 1 + 4 * g:5 + 4 * g, :, HD:2 * HD],
                         k.psum[6 + g][:].rearrange("p (b h n) -> p b h n", b=4, h=2)).then_inc(turn_used, 1)
            for g in range(2):
                act.wait_ge(turned, g + 3)
                act.copy(k.v_new[0:TSEQ, 4 * g:4 * g + 4, :, HD:2 * HD],
                         k.psum[3 + g][0:TSEQ, :].rearrange("p (b h n) -> p b h n", b=4, h=2)).then_inc(turn_used, 1)
            act.wait_ge(turned, 5)
            act.copy(k.sink_p[:], k.psum[5][:, 256:264].rearrange("p (h c) -> p c h", h=2)).then_inc(turn_used, 1)
            act.copy(k.sink_s[:], k.psum[5][:, 264:266]).then_inc(turn_used, 1)
            act.copy(k.k_rows[:, 0], k.psum[5][:, 0:P])
            act.copy(k.k_rows[0:NS_TOK, 1], k.psum[5][0:NS_TOK, P:2 * P])
            act.drain().then_inc(rows_done, 1)
            act.wait_ge(zeroed, 6)
            for g in range(2):
                act.wait_ge(turned, g + 6)
                for h in range(2):
                    r = slice(HD * h, HD * h + HD)
                    act.copy(k.ks_bd[r, 4 * g:4 * g + 4, h, 0:WINDOW],
                             k.psum[6 + g][r, :].rearrange("p (b n) -> p b n", b=4))


def attention_prompt(k):
    NB = NP_TOK // WINDOW
    prob = [k.prob, k.at("prob1", R1_AT, [P, 4, 2, 2 * WINDOW])]
    diag = [k.diag, k.at("diag1", k.scrap, [P, 8, P])]
    q_now = [k.q_now, k.at("q_now1", k.scrap + 4096, [P, 4, P])]
    small = [k.small, k.at("small1", R1_AT + 8192, [P, 24])]
    mx, sums, es = ([t[:, 8 * i:8 * i + 8] for t in small] for i in range(3))
    q_copied, v_copied, s_mm, s_used, max_done, exp_done, diag_done, pt_mm, pt_used, o_mm, o_used = (
        k.sem(f"att_{n}") for n in ("q_copied", "v_copied", "s_mm", "s_used", "max_done", "exp_done", "diag_done",
                                    "pt_mm", "pt_used", "o_mm", "o_used"))

    def over_heads(ap):
        return ap.unsqueeze(1).broadcast_to([P, 2, 2 * WINDOW])

    def steps(eng, body):
        with eng.Fori(0, NB // 2 - 1) as i:
            for j in range(2):
                body(2 * i + j, j, True)
        body(NB - 2, 0, True)
        body(NB - 1, 1, False)

    with k.nc.Block() as block:
        @block.gpsimd
        def _(pool):
            def copy_q(b, j):
                pool.tensor_copy(q_now[j][:], k.qkv[:, 0:4, bass.ds(WINDOW * b, WINDOW)]).then_inc(q_copied, 1)

            def step(n, j, more):
                if not (isinstance(n, int) and n + 2 >= NB):
                    pool.wait_ge(s_mm, 4 * n + 8)
                    copy_q(n + 2, j)
                pool.wait_ge(o_mm, n + 1)
                pool.tensor_copy(k.v_now[:], k.v_tok[:, bass.ds(n, 2)]).then_inc(v_copied, 1)

            copy_q(0, 0)
            copy_q(1, 1)
            steps(pool, step)

        @block.tensor
        def _(pe):
            def scores(b, j):
                pe.wait_ge(q_copied, b + 1)
                for c in range(4):
                    pe.wait_ge(s_used, 4 * b + c + 1)
                    pe.matmul(k.psum[c][:].rearrange("p (h n) -> p h n", h=2), q_now[j][:, c],
                              k.k_bd[:, :, bass.ds(WINDOW * b, 2 * WINDOW)], start=True, stop=True).then_inc(s_mm, 1)

            def weighted(b, c):
                pe.wait_ge(pt_used, 4 * b + c + 3)
                for n in range(4):
                    h, w = n // 2, n % 2
                    ins = pe.matmul(k.psum[6][:, P * c:P * c + P], k.v_now[:, w, h, HD * (1 - h):HD * (1 - h) + P],
                                    k.probT[c % 2][:, n], start=(n == 0), stop=(n == 3))
                return ins

            def step(n, j, more):
                if more:
                    scores(n + 1, 1 - j)
                pe.wait_ge(diag_done, n + 1)
                pe.wait_ge(v_copied, n + 1)
                for c in range(4):
                    pe.wait_ge(pt_used, 4 * n + c + 1)
                    for i in range(4):
                        h, w = i // 2, i % 2
                        ins = pe.matmul(k.psum[4 + c % 2][:, P * i:P * i + P],
                                        prob[j][:, c, h, P * w:P * w + P], diag[j][:, 2 * c + h], start=True, stop=True)
                    ins.then_inc(pt_mm, 1)
                    if c == 0:
                        pe.wait_ge(o_used, n + 1)
                    if c >= 1:
                        weighted(n, c - 1)
                weighted(n, 3).then_inc(o_mm, 1)

            pe.sem_inc(s_mm, 4)
            pe.sem_inc(o_mm, 1)
            scores(0, 0)
            steps(pe, step)

        @block.vector
        def _(dve):
            sink = k.sink_p[:].rearrange("p c h -> p (c h)")

            def scores(b, j, mask):
                for c in range(4):
                    dve.wait_ge(s_mm, 4 * b + c + 5)
                    if c == 0 and not (isinstance(b, int) and b == 0):
                        dve.wait_ge(o_mm, b)
                    dve.scalar_tensor_tensor(prob[j][:, c], k.psum[c][:].rearrange("p (h n) -> p h n", h=2),
                                             HD ** -0.5, over_heads(k.c(mask)), ALU.mult, ALU.add).then_inc(s_used, 1)
                dve.drain()
                dve.tensor_reduce(mx[j], prob[j][:].rearrange("p c h n -> p (c h) n"), AX.X, ALU.max)
                dve.drain()
                dve.tensor_tensor(mx[j], mx[j], sink, ALU.max)
                dve.drain()
                dve.tensor_tensor(es[j], sink, mx[j], ALU.subtract)
                dve.tensor_scalar(mx[j], mx[j], -1.0, None, ALU.mult).then_inc(max_done, 1)

            def step(n, j, more):
                dve.wait_ge(exp_done, n + 1)
                dve.tensor_tensor(sums[j], sums[j], es[j], ALU.add)
                dve.drain()
                dve.reciprocal(sums[j], sums[j])
                dve.drain()
                for i in range(8):
                    ins = dve.tensor_scalar(diag[j][:, i], k.c("ident"), sums[j][:, i:i + 1], None, ALU.mult)
                ins.then_inc(diag_done, 1)
                if more:
                    scores(n + 1, 1 - j, "mask_p")

            dve.sem_inc(s_used, 4)
            scores(0, 0, "mask_p0")
            steps(dve, step)

        @block.scalar
        def _(act):
            def exps(j, first, n):
                for i in range(first, first + n):
                    act.activation(prob[j][:, i // 2, i % 2], prob[j][:, i // 2, i % 2], ACT.Exp, bias=mx[j][:, i:i + 1],
                                   accum_out=sums[j][:, i:i + 1])

            def exp_sinks(j):
                act.activation(es[j], es[j], ACT.Exp)
                act.drain().then_inc(exp_done, 1)

            def step(n, j, more):
                for c in range(4):
                    act.wait_ge(pt_mm, 4 * n + c + 1)
                    act.copy(k.probT[c % 2][:].rearrange("p c n -> p (c n)"), k.psum[4 + c % 2][:]).then_inc(pt_used, 1)
                    if more and c >= 1:
                        if c == 1:
                            act.wait_ge(max_done, n + 2)
                        exps(1 - j, 3 * (c - 1), 3 if c < 3 else 2)
                act.wait_ge(o_mm, n + 2)
                act.copy(k.qkv[:, 0:4, bass.ds(WINDOW * n, WINDOW)], k.psum[6][:].rearrange("p (c n) -> p c n", c=4)
                         ).then_inc(o_used, 1)
                if more:
                    exp_sinks(1 - j)

            act.sem_inc(pt_used, 2)
            act.sem_inc(o_used, 1)
            act.wait_ge(max_done, 1)
            exps(0, 0, 8)
            exp_sinks(0)
            steps(act, step)


def attention_sample(k):
    mx, sums, es = (k.small[:, 24 + 4 * i:28 + 4 * i] for i in range(3))
    s_mm, max_done, exp_done, diag_done, pt_mm, pt_used, o_mm = (
        k.sem(f"ats_{n}") for n in ("s_mm", "max_done", "exp_done", "diag_done", "pt_mm", "pt_used", "o_mm"))
    NK = WINDOW + TSEQ
    with k.nc.Block() as block:
        @block.tensor
        def _(pe):
            for g in range(2):
                for b in range(4):
                    ins = pe.matmul(k.psum[g][:, 0:2 * NK], k.q_pad[:, 4 * g + b],
                                    k.ks_bd[:, 4 * g + b].rearrange("p h n -> p (h n)"), start=(b == 0), stop=(b == 3))
                ins.then_inc(s_mm, 1)
            pe.wait_ge(diag_done, 1)
            for g in range(2):
                for h in range(2):
                    i = 2 * g + h
                    pe.matmul(k.psum[2][:, P * i:P * i + P], k.prob_s[:, g, h, 0:WINDOW], k.diag[:, i], start=True, stop=True)
                    ins = pe.matmul(k.psum[3][0:TSEQ, P * i:P * i + P], k.prob_s[:, g, h, WINDOW:NK], k.diag[:, i],
                                    start=True, stop=True)
            ins.then_inc(pt_mm, 1)
            pe.wait_ge(pt_used, 2)
            for s in range(NSEQ):
                for h in range(2):
                    i, col, pad = 2 * (s // 4) + h, 32 * (s % 4), HD * (1 - h)
                    pe.matmul(k.psum[4][:, 32 * s:32 * s + 32], k.v_cache[:, s, h, pad:pad + P],
                              k.probT[0][:, i, col:col + 32], start=(h == 0), stop=False)
                    ins = pe.matmul(k.psum[4][:, 32 * s:32 * s + 32], k.v_new[0:TSEQ, s, h, pad:pad + P],
                                    k.probT[1][0:TSEQ, i, col:col + 32], start=False, stop=(h == 1))
            ins.then_inc(o_mm, 1)

        @block.vector
        def _(dve):
            for g in range(2):
                dve.wait_ge(s_mm, g + 1)
                dve.scalar_tensor_tensor(k.prob_s[:, g], k.psum[g][:, 0:2 * NK].rearrange("p (h n) -> p h n", h=2), HD ** -0.5,
                                         k.c("mask_s").unsqueeze(1).broadcast_to([P, 2, NK]), ALU.mult, ALU.add)
            dve.drain()
            dve.tensor_reduce(mx, k.prob_s[:].rearrange("p g h n -> p (g h) n"), AX.X, ALU.max)
            dve.drain()
            sink = k.sink_s[:].unsqueeze(1).broadcast_to([P, 2, 2])
            mx3, es3 = (a.rearrange("p (g h) -> p g h", g=2) for a in (mx, es))
            dve.tensor_tensor(mx3, mx3, sink, ALU.max)
            dve.drain()
            dve.tensor_tensor(es3, sink, mx3, ALU.subtract)
            dve.tensor_scalar(mx, mx, -1.0, None, ALU.mult).then_inc(max_done, 1)
            dve.wait_ge(exp_done, 1)
            dve.tensor_tensor(sums, sums, es, ALU.add)
            dve.drain()
            dve.reciprocal(sums, sums)
            dve.drain()
            for i in range(4):
                ins = dve.tensor_scalar(k.diag[:, i], k.c("ident"), sums[:, i:i + 1], None, ALU.mult)
            ins.then_inc(diag_done, 1)
            dve.wait_ge(o_mm, 1)
            for c in range(4):
                dve.tensor_copy(per_seq(k.qkv[:, c, NP_TOK:T]),
                                k.psum[4][:, 0:32 * NSEQ].rearrange("p (s c t) -> p c s t", s=NSEQ, c=4)[:, c])

        @block.scalar
        def _(act):
            act.wait_ge(max_done, 1)
            for i in range(4):
                act.activation(k.prob_s[:, i // 2, i % 2], k.prob_s[:, i // 2, i % 2], ACT.Exp, bias=mx[:, i:i + 1],
                               accum_out=sums[:, i:i + 1])
            act.activation(es, es, ACT.Exp)
            act.drain().then_inc(exp_done, 1)
            act.wait_ge(pt_mm, 1)
            act.copy(k.probT[0][:].rearrange("p c n -> p (c n)"), k.psum[2][:]).then_inc(pt_used, 1)
            act.copy(k.probT[1][0:TSEQ].rearrange("p c n -> p (c n)"), k.psum[3][0:TSEQ, :]).then_inc(pt_used, 1)


UTILES = [(0, 366), (366, 366), (732, 364)]


def u_tok(ap):
    return ap[:, NP_TOK:W].rearrange("p (s t) -> p s t", t=TSEQ + 1)[:, :, 1:]


def rwkv_shift(k):
    d = k.dram
    k.dec = k.at("dec", R1_AT, [P, PAIRS, W])
    k.bb = k.at("bb", R1_AT + PAIRS * UB, [P, PAIRS, W])
    k.aa = k.at("aa", R1_AT + 2 * PAIRS * UB, [P, PAIRS, W])
    k.bon = k.at("bon", R1_AT + 3 * PAIRS * UB, [P, PAIRS, W])
    o = R2_AT
    diff = [k.at(f"diff{j}", o + UB * j, [P, W]) for j in range(2)]
    tz = k.at("tz", o + 2 * UB, [P, W])
    o += 3 * UB
    w2 = k.at("w2", o, [P, RW]); o += 2048
    a2 = k.at("a2", o, [P, RW]); o += 2048
    shift_rows = k.at("shift_rows", o, [P, P]); o += 512
    last = k.at("last", o, [P, 9, UC]); o += 512
    last_rows = k.at("last_rows", o, [P, P]); o += 512
    NR = NSEQ * UC
    zero2, lora_in, rows_in, out_done, prev_mm, u_full, last_done, last_mm, lastT_done, diff_done, z_done = (
        k.sem(f"sh_{n}") for n in ("zero2", "lora_in", "rows_in", "out_done", "prev_mm", "u_full", "last_done",
                                   "last_mm", "lastT_done", "diff_done", "z_done"))
    tz_done, lora_mm, lora_free = (k.sem(f"sh_{n}") for n in ("tz_done", "lora_mm", "lora_free"))
    order = [12, 13] + list(range(12))

    with k.nc.Block() as block:
        @block.sync
        def _(sp):
            sp.dma_start(shift_rows[0:NR, :], d["state_shift"][0].rearrange("s (c p) -> (s c) p", p=P)).then_inc(rows_in, 16)
            sp.wait_ge(zero2, 2)
            sp.dma_start(w2[0:HD, :], d["rwkv_w2"][0]).then_inc(lora_in, 16)
            sp.dma_start(a2[HD:P, :], d["rwkv_a2"][0]).then_inc(lora_in, 16)
            sp.wait_ge(lastT_done, 1)
            sp.dma_start(d["prompt_shift"][0].rearrange("o (c p) -> (o c) p", p=P), last_rows[0:UC, :]).then_inc(out_done, 16)
            sp.dma_start(d["sample_shift"][0].rearrange("s (c p) -> (s c) p", p=P), last_rows[UC:UC + NR, :]
                         ).then_inc(out_done, 16)
            sp.wait_ge(out_done, 32)

        @block.gpsimd
        def _(pool):
            pool.memset(w2[:], 0.0).then_inc(zero2, 1)
            pool.memset(a2[:], 0.0).then_inc(zero2, 1)
            pool.wait_ge(u_full, 1)
            for n, c in enumerate(order):
                if n >= 2:
                    pool.wait_ge(z_done, n - 1)
                pool.tensor_tensor(diff[n % 2][:], k.u[:, c, 0:W], k.u[:, c, 1:UW], ALU.subtract).then_inc(diff_done, 1)

        @block.vector
        def _(dve):
            dve.memset(k.u[:, :, 0:1], 0.0)
            dve.wait_ge(prev_mm, 1)
            dve.tensor_copy(k.u[:, :, 1 + NP_TOK::TSEQ + 1], k.psum[6][:, 0:NR].rearrange("p (s c) -> p c s", s=NSEQ))
            dve.tensor_copy(last[:, 0, :], k.u[:, :, NP_TOK])
            dve.tensor_copy(last[:, 1:9, :], k.u[:, :, 1 + NP_TOK + TSEQ::TSEQ + 1].rearrange("p c s -> p s c")
                            ).then_inc(last_done, 1)
            dve.drain().then_inc(u_full, 1)
            for n, c in enumerate(order):
                dve.wait_ge(diff_done, n + 1)
                dve.scalar_tensor_tensor(k.u[:, c, 1:UW], diff[n % 2][:], k.p2("mu_shift", c), k.u[:, c, 1:UW],
                                         ALU.mult, ALU.add).then_inc(z_done, 1)

        @block.tensor
        def _(pe):
            ident = k.c("ident")
            pe.wait_ge(rows_in, 16)
            pe.transpose(k.psum[6][:, 0:NR], shift_rows[0:NR, :], ident[0:NR, 0:NR]).then_inc(prev_mm, 1)
            pe.wait_ge(last_done, 1)
            pe.transpose(k.psum[7][0:9 * UC, 0:P], last[:].rearrange("p s c -> p (s c)"), ident).then_inc(last_mm, 1)
            pe.wait_ge(lora_in, 32)
            pe.wait_ge(tz_done, 1)
            for m in range(PAIRS):
                for h, w in enumerate((w2, a2)):
                    pe.wait_ge(lora_free, 2 * m + h + 1)
                    for t, (a, n) in enumerate(UTILES):
                        ins = pe.matmul(k.psum[3 * h + t][:, 0:n], w[:, P * m:P * m + P], tz[:, a:a + n],
                                        start=True, stop=True)
                    ins.then_inc(lora_mm, 1)

        @block.scalar
        def _(act):
            act.wait_ge(last_mm, 1)
            act.copy(last_rows[0:9 * UC, :], k.psum[7][0:9 * UC, 0:P]).then_inc(lastT_done, 1)
            act.sem_inc(lora_free, 2)
            act.wait_ge(z_done, 1)
            act.activation(tz[0:HD, :], k.u[0:HD, 12, 1:UW], ACT.Tanh)
            act.copy(tz[HD:P, :], k.u[HD:P, 12, 1:UW]).then_inc(tz_done, 1)
            act.wait_ge(z_done, 2)
            act.activation(k.u[:, 13, 1:UW], k.u[:, 13, 1:UW], ACT.Sigmoid)
            for m in range(PAIRS):
                for h, (dst, bias) in enumerate(((k.dec, "rwkv_w0"), (k.bb, "rwkv_a0"))):
                    act.wait_ge(lora_mm, 2 * m + h + 1)
                    for t, (a, n) in enumerate(UTILES):
                        ins = act.activation(dst[:, m, a:a + n], k.psum[3 * h + t][:, 0:n], ACT.Sigmoid, bias=k.p2(bias, m))
                    ins.then_inc(lora_free, 1)


def rwkv_keys(k):
    sq = [k.at(f"kk_sq{j}", R2_AT + UB * j, [P, W]) for j in range(2)]
    ss = [k.at(f"kk_ss{m}", R2_AT + UB * (2 + m), [P, W]) for m in range(PAIRS)]
    kk_done, sq_done, ss_mm, ss_done, root_done = (
        k.sem(f"kk_{n}") for n in ("kk_done", "sq_done", "ss_mm", "ss_done", "root_done"))
    with k.nc.Block() as block:
        @block.vector
        def _(dve):
            for m in range(PAIRS):
                dve.tensor_scalar(k.aa[:, m], k.u[:, 4 + m, 1:UW], k.p2("rwkv_k_k", m), None, ALU.mult).then_inc(kk_done, 1)
            for m in range(PAIRS):
                dve.wait_ge(ss_mm, m + 1)
                for t, (a, n) in enumerate(UTILES):
                    ins = dve.tensor_scalar(ss[m][:, a:a + n], k.psum[3 * (m % 2) + t][:, 0:n], 1e-24, None, ALU.max)
                ins.then_inc(ss_done, 1)
            for m in range(PAIRS):
                dve.wait_ge(root_done, m + 1)
                dve.reciprocal(ss[m][:], ss[m][:])
                dve.drain()
                dve.tensor_tensor(k.aa[:, m], k.aa[:, m], ss[m][:], ALU.mult)

        @block.scalar
        def _(act):
            for m in range(PAIRS):
                act.wait_ge(kk_done, m + 1)
                if m >= 2:
                    act.wait_ge(ss_mm, m - 1)
                act.activation(sq[m % 2][:], k.aa[:, m], ACT.Square).then_inc(sq_done, 1)
            for m in range(PAIRS):
                act.wait_ge(ss_done, m + 1)
                act.activation(ss[m][:], ss[m][:], ACT.Sqrt).then_inc(root_done, 1)

        @block.tensor
        def _(pe):
            for m in range(PAIRS):
                pe.wait_ge(sq_done, m + 1)
                if m >= 2:
                    pe.wait_ge(ss_done, m - 1)
                for t, (a, n) in enumerate(UTILES):
                    ins = pe.matmul(k.psum[3 * (m % 2) + t][:, 0:n], k.c("head_sum"), sq[m % 2][:, a:a + n],
                                    start=True, stop=True)
                ins.then_inc(ss_mm, 1)


def rwkv_decay(k):
    C = float(np.exp(-0.5))
    keep = k.at("keep", R2_AT, [P, W])
    log_sum, inv, prd = (k.at(n, R2_AT + UB * (1 + j), [P, W]) for j, n in enumerate(("log_sum", "inv", "prd")))
    keep_in, sum_done, exp_done, b_done, r_done, bon_in, bon_mm, scaled, used = (
        k.sem(f"dc_{n}") for n in ("keep_in", "sum_done", "exp_done", "b_done", "r_done", "bon_in", "bon_mm", "scaled", "used"))
    with k.nc.Block() as block:
        @block.sync
        def _(sp):
            sp.dma_start(keep[:], k.dram["scan_keep"]).then_inc(keep_in, 16)

        @block.vector
        def _(dve):
            dve.wait_ge(keep_in, 16)
            for m in range(PAIRS):
                if m >= 1:
                    dve.wait_ge(exp_done, m)
                dve.tensor_tensor_scan(log_sum[:], keep[:], k.dec[:, m], 0.0, ALU.mult, ALU.add)
                dve.drain()
                dve.tensor_tensor(k.dec[:, m], log_sum[:], k.dec[:, m], ALU.subtract).then_inc(sum_done, 1)
                kz, rz = k.u[:, 4 + m, 1:UW], k.u[:, m, 1:UW]
                dve.tensor_scalar(k.bon[:, m], k.bb[:, m], -1.0, k.p2("rwkv_k_a", m), ALU.add, ALU.mult)
                dve.tensor_tensor(k.bb[:, m], k.bb[:, m], k.aa[:, m], ALU.mult)
                dve.drain()
                dve.scalar_tensor_tensor(kz, k.bon[:, m], 1.0, kz, ALU.add, ALU.mult).then_inc(b_done, 1)
                dve.drain()
                dve.scalar_tensor_tensor(k.bon[:, m], rz, k.p2("rwkv_r_k", m), kz, ALU.mult, ALU.mult).then_inc(bon_in, 1)
                dve.wait_ge(exp_done, m + 1)
                dve.scalar_tensor_tensor(k.aa[:, m], k.aa[:, m], -1.0, k.dec[:, m], ALU.mult, ALU.mult)
                dve.tensor_copy(k.p_end[:, m, 0:NP_TOK // HD], prd[:, HD - 1:NP_TOK:HD])
                dve.tensor_copy(k.p_end[:, m, NP_TOK // HD:], prd[:, NP_TOK + TSEQ::TSEQ + 1]).then_inc(used, 1)
                dve.wait_ge(bon_mm, m + 1)
                for t, (a, n) in enumerate(UTILES):
                    dve.tensor_tensor(k.bon[:, m, a:a + n], k.psum[t][:, 0:n], k.u[:, 8 + m, 1 + a:1 + a + n], ALU.mult)
                dve.drain().then_inc(r_done, 1)

        @block.scalar
        def _(act):
            for m in range(PAIRS):
                act.wait_ge(sum_done, m + 1)
                if m >= 1:
                    act.wait_ge(scaled, m)
                    act.wait_ge(used, m)
                act.activation(k.dec[:, m], k.dec[:, m], ACT.Exp, scale=-C)
                act.activation(inv[:], log_sum[:], ACT.Exp, scale=C)
                act.activation(prd[:], log_sum[:], ACT.Exp, scale=-C).then_inc(exp_done, 1)

        @block.tensor
        def _(pe):
            for m in range(PAIRS):
                pe.wait_ge(bon_in, m + 1)
                if m >= 1:
                    pe.wait_ge(r_done, m)
                for t, (a, n) in enumerate(UTILES):
                    ins = pe.matmul(k.psum[t][:, 0:n], k.c("head_sum"), k.bon[:, m, a:a + n], start=True, stop=True)
                ins.then_inc(bon_mm, 1)

        @block.gpsimd
        def _(pool):
            for m in range(PAIRS):
                kz, rz = k.u[:, 4 + m, 1:UW], k.u[:, m, 1:UW]
                pool.wait_ge(exp_done, m + 1)
                pool.wait_ge(bon_in, m + 1)
                pool.tensor_tensor(k.bb[:, m], k.bb[:, m], inv[:], ALU.mult)
                pool.tensor_tensor(kz, kz, inv[:], ALU.mult)
                pool.tensor_tensor(rz, rz, prd[:], ALU.mult).then_inc(scaled, 1)


TILE = 4 * PAIRS * P
STREAM = ("ar", "a_bd", "b_bd", "k_bd", "x", "lt", "t", "tt", "lak", "mb", "mk", "v_tok", "b_tok", "k_tok")
PE_STEPS = ["gram_b", "gram_k", "gram_a", "v_tok", "b_tok", "k_tok"] + [
    f"{s}{m}" for m in LEVELS[1:] for s in ("x", "inc")] + ["w", "u", "s", "o"]
DVE_STEPS = ["mask_b", "mask_k", "level1"] + [f"{s}{m}" for m in LEVELS[1:] for s in ("x", "inc")] + ["state"]
ACT_STEPS = ["gather", "v_tok", "lt", "lak", "b_tok", "k_tok", "w", "u", "o"]


def at_step(steps, i, name):
    return i * len(steps) + (steps.index(name) + 2)


def pair4(ap):
    return ap.rearrange("p (m n) -> p m n", m=PAIRS)


def over_pairs(ap):
    return ap.unsqueeze(1).broadcast_to([P, PAIRS, ap.shape[1]])


class Stream:

    def __init__(self, k, s, places):
        self.k, self.s = k, s
        tiles = [k.at(f"{name}_{s}", at, [P, PAIRS, P]) for name, at in zip(STREAM, places)]
        (self.ar, self.a_bd, self.b_bd, self.k_bd, self.x, self.lt, self.t, self.tt, self.lak, self.mb, self.mk,
         self.v_tok, self.b_tok, self.k_tok) = tiles
        self.bank = [k.psum[4 * s + n] for n in range(4)]
        self.pe, self.dve, self.act = (k.sem(f"rwkv_{e}_steps{s}") for e in ("pe", "dve", "act"))


def chunk_views(k, c):
    if c is None:
        def view(t, m0, off):
            return t[:, m0:m0 + PAIRS, off + NP_TOK:off + W].rearrange("p m (s t) -> p m s t", t=TSEQ + 1)[:, :, :, 1:]
    else:
        def view(t, m0, off):
            return t[:, m0:m0 + PAIRS, bass.ds(c * HD + off, HD)]
    return view(k.aa, 0, 0), view(k.u, 0, 1), view(k.bb, 0, 0), view(k.u, 4, 1), view(k.u, 8, 1)


def gather(act, st, views, sample):
    def like(ap):
        return ap.rearrange("p m (s t) -> p m s t", t=TSEQ) if sample else ap

    a, r, b, kk, v = views
    act.copy(like(st.ar[:, :, 0:HD]), a)
    act.copy(like(st.ar[:, :, HD:P]), r)
    for dst, src in ((st.a_bd, a), (st.b_bd, b), (st.k_bd, kk), (st.x, v)):
        for h in range(2):
            rows = slice(HD * h, HD * h + HD)
            ins = act.copy(like(dst[:, :, HD * h:HD * h + HD])[rows], src[rows])
    return ins


def head_blocks(act, dst, src):
    for h in range(2):
        rows = slice(HD * h, HD * h + HD)
        ins = act.copy(dst[rows, :, HD * h:HD * h + HD], src[rows])
    return ins


def pe_local(pe, st, i, part, levels):
    k = st.k

    def four(bank, lhs, rhs):
        for m in range(PAIRS):
            ins = pe.matmul(bank[:, P * m:P * m + P], lhs[:, m], rhs[:, m], start=True, stop=True)
        return ins

    def turn(bank, src):
        for m in range(PAIRS):
            ins = pe.transpose(bank[:, P * m:P * m + P], src[:, m], k.c("ident"))
        return ins

    if part == 0:
        pe.wait_ge(st.act, at_step(ACT_STEPS, i, "gather"))
        pe.wait_ge(st.dve, len(DVE_STEPS) * i + 1)
        four(st.bank[0], st.b_bd, st.ar).then_inc(st.pe, 1)
        four(st.bank[1], st.k_bd, st.ar).then_inc(st.pe, 1)
        four(st.bank[2], st.a_bd, st.b_bd).then_inc(st.pe, 1)
        turn(st.bank[3], st.x).then_inc(st.pe, 1)
        pe.wait_ge(st.dve, at_step(DVE_STEPS, i, "mask_b"))
        turn(st.bank[0], st.b_bd).then_inc(st.pe, 1)
        pe.wait_ge(st.dve, at_step(DVE_STEPS, i, "mask_k"))
        turn(st.bank[1], st.k_bd).then_inc(st.pe, 1)
        return
    m, what = part
    if what == "x":
        pe.wait_ge(st.dve, at_step(DVE_STEPS, i, "level1" if m == 2 else f"inc{m // 2}"))
        if m == 2:
            pe.wait_ge(st.act, at_step(ACT_STEPS, i, "lt"))
        four(st.bank[2], st.lt, st.t).then_inc(st.pe, 1)
    else:
        pe.wait_ge(st.dve, at_step(DVE_STEPS, i, f"x{m}"))
        if m == 2:
            pe.wait_ge(st.act, at_step(ACT_STEPS, i, "k_tok"))
        ins = four(st.bank[0], st.x, st.tt)
        if m != levels[-1]:
            ins = four(st.bank[1], st.tt, st.x)
        ins.then_inc(st.pe, 1)


def dve_local(dve, st, i, part, levels, causal):
    k = st.k
    if part == 0:
        for n, (dst, gram) in enumerate(((st.mb, "gram_b"), (st.mk, "gram_k"))):
            dve.wait_ge(st.pe, at_step(PE_STEPS, i, gram))
            dve.tensor_tensor(dst[:], pair4(st.bank[n][:]), over_pairs(causal), ALU.mult).then_inc(st.dve, 1)
        dve.wait_ge(st.pe, at_step(PE_STEPS, i, "gram_a"))
        dve.tensor_tensor(st.t[:], pair4(st.bank[2][:]), over_pairs(k.c("lev1")), ALU.mult)
        dve.drain()
        for m in range(PAIRS):
            dve.tensor_tensor(st.tt[:, m].rearrange("p (h t) -> p h t", h=2),
                              st.mb[:, m, 0:HD].unsqueeze(1).broadcast_to([P, 2, HD]),
                              k.c("lev1T").rearrange("p (h t) -> p h t", h=2), ALU.mult)
        dve.tensor_tensor(st.t[:], st.t[:], over_pairs(k.c("ident")), ALU.add)
        dve.drain()
        dve.tensor_tensor(st.tt[:], st.tt[:], over_pairs(k.c("ident")), ALU.add).then_inc(st.dve, 1)
        return
    m, what = part
    if what == "x":
        dve.wait_ge(st.pe, at_step(PE_STEPS, i, f"x{m}"))
        dve.tensor_tensor(st.x[:], pair4(st.bank[2][:]), over_pairs(k.c(f"lev{m}")), ALU.mult).then_inc(st.dve, 1)
    else:
        dve.wait_ge(st.pe, at_step(PE_STEPS, i, f"inc{m}"))
        ins = dve.tensor_tensor(st.tt[:], st.tt[:], pair4(st.bank[0][:]), ALU.add)
        if m != levels[-1]:
            ins = dve.tensor_tensor(st.t[:], st.t[:], pair4(st.bank[1][:]), ALU.add)
        ins.then_inc(st.dve, 1)


def act_local(act, st, i):
    for step, n, dst in (("v_tok", 3, st.v_tok), ("lt", None, None), ("lak", None, None), ("b_tok", 0, st.b_tok),
                         ("k_tok", 1, st.k_tok)):
        if n is not None:
            act.wait_ge(st.pe, at_step(PE_STEPS, i, step))
            act.copy(dst[:], pair4(st.bank[n][:])).then_inc(st.act, 1)
        elif step == "lt":
            act.wait_ge(st.dve, at_step(DVE_STEPS, i, "mask_b"))
            head_blocks(act, st.lt, st.mb[:, :, 0:HD]).then_inc(st.act, 1)
        else:
            act.wait_ge(st.dve, at_step(DVE_STEPS, i, "mask_k"))
            head_blocks(act, st.lak, st.mk[:, :, 0:HD]).then_inc(st.act, 1)


def rwkv_prompt(k):
    region_a = QKV_AT + 4 * TB
    region_b = R1_AT + 4 * PAIRS * UB
    u12 = up32(U_AT + 12 * UW * 4)
    k.streams = [Stream(k, 0, [region_a + TILE * n for n in range(12)] + [region_b, region_b + TILE]),
                 Stream(k, 1, [R2_AT + TILE * n for n in range(14)])]
    k.w_now = k.at("w_now", region_b + 2 * TILE, [P, PAIRS, P])
    k.u_now = k.at("u_now", region_b + 3 * TILE, [P, PAIRS, P])
    k.state = k.at("state", u12, [P, PAIRS, P])
    zeroed = k.sem("rwkv_zeroed")
    NI = NP_TOK // HD // 2
    levels = LEVELS[1:]
    parts = [0] + [(m, what) for m in levels for what in ("x", "inc")]
    wkv_turned, wkv_rows, wkv_out = k.sem("wkv_turned"), k.sem("wkv_rows"), k.sem("wkv_out")

    with k.nc.Block() as block:
        @block.gpsimd
        def _(pool):
            for st in k.streams:
                for t in (st.a_bd, st.b_bd, st.k_bd, st.x, st.lt, st.lak):
                    pool.memset(t[:], 0.0).then_inc(zeroed, 1)
            pool.memset(k.state[:], 0.0).then_inc(zeroed, 1)

        @block.scalar
        def _(act):
            act.wait_ge(zeroed, 13)
            for st in k.streams:
                act.sem_inc(st.act, 1)
            with act.Fori(0, NI) as i:
                act.drain()
                for st in k.streams:
                    act.wait_ge(st.pe, len(PE_STEPS) * i + 1)
                    gather(act, st, chunk_views(k, 2 * i + st.s), False).then_inc(st.act, 1)
                for st in k.streams:
                    act_local(act, st, i)
                for st in k.streams:
                    act.wait_ge(st.pe, at_step(PE_STEPS, i, "w"))
                    act.copy(k.w_now[:], pair4(st.bank[3][:])).then_inc(st.act, 1)
                    act.wait_ge(st.pe, at_step(PE_STEPS, i, "u"))
                    act.copy(k.u_now[:], pair4(st.bank[2][:])).then_inc(st.act, 1)
                    act.wait_ge(st.pe, at_step(PE_STEPS, i, "o"))
                    act.copy(st.ar[:, :, HD:P], pair4(st.bank[1][:])[:, :, HD:P])
                    act.drain()
                    act.copy(chunk_views(k, 2 * i + st.s)[1], st.ar[:, :, HD:P]).then_inc(st.act, 1)

        @block.tensor
        def _(pe):
            for st in k.streams:
                pe.sem_inc(st.pe, 1)
            with pe.Fori(0, NI) as i:
                for part in parts:
                    for st in k.streams:
                        pe_local(pe, st, i, part, levels)
                for st in k.streams:
                    other = k.streams[1 - st.s]
                    for m in range(PAIRS):
                        pe.matmul(st.bank[3][:, P * m:P * m + P], st.lak[:, m], st.v_tok[:, m], start=True, stop=False)
                        if m == 0:
                            pe.wait_ge(other.dve, at_step(DVE_STEPS, i, "state") if st.s else len(DVE_STEPS) * i + 1)
                        ins = pe.matmul(st.bank[3][:, P * m:P * m + P], st.a_bd[:, m], k.state[:, m], start=False, stop=True)
                    ins.then_inc(st.pe, 1)
                    pe.wait_ge(st.act, at_step(ACT_STEPS, i, "w"))
                    pe.wait_ge(st.dve, at_step(DVE_STEPS, i, f"inc{levels[-1]}"))
                    for m in range(PAIRS):
                        ins = pe.matmul(st.bank[2][:, P * m:P * m + P], st.tt[:, m], k.w_now[:, m], start=True, stop=True)
                    ins.then_inc(st.pe, 1)
                    pe.wait_ge(st.act, at_step(ACT_STEPS, i, "u"))
                    for m in range(PAIRS):
                        col = slice(P * m, P * m + P)
                        pe.matmul(st.bank[1][:, col], k.state[:, m], st.ar[:, m], start=True, stop=False)
                        pe.matmul(st.bank[1][:, col], st.v_tok[:, m], st.mk[:, m], start=False, stop=False)
                        pe.matmul(st.bank[1][:, col], k.u_now[:, m], st.mb[:, m], start=False, stop=True)
                        pe.matmul(st.bank[0][:, col], st.k_tok[:, m], st.v_tok[:, m], start=True, stop=False)
                        ins = pe.matmul(st.bank[0][:, col], st.b_tok[:, m], k.u_now[:, m], start=False, stop=True)
                    ins.then_inc(st.pe, 2)
            pe.wait_ge(k.streams[1].dve, len(DVE_STEPS) * NI + 1)
            pe.wait_ge(k.streams[0].act, len(ACT_STEPS) * NI + 1)
            for m in range(PAIRS):
                ins = pe.transpose(k.psum[0][:, P * m:P * m + P], k.state[:, m], k.c("ident"))
            ins.then_inc(wkv_turned, 1)

        @block.vector
        def _(dve):
            for st in k.streams:
                dve.sem_inc(st.dve, 1)
            with dve.Fori(0, NI) as i:
                for part in parts:
                    for st in k.streams:
                        dve_local(dve, st, i, part, levels, k.c("causal"))
                for st in k.streams:
                    dve.wait_ge(st.pe, at_step(PE_STEPS, i, "o"))
                    dve.tensor_tensor(k.state[:], k.state[:], pair4(st.bank[0][:]), ALU.add)
                    dve.drain()
                    dve.tensor_tensor(k.state[:], k.state[:],
                                      k.p_end[:, :, bass.ds(2 * i + st.s, 1)].broadcast_to([P, PAIRS, P]),
                                      ALU.mult).then_inc(st.dve, 1)
            dve.wait_ge(wkv_turned, 1)
            dve.tensor_copy(k.w_now[:], pair4(k.psum[0][:])).then_inc(wkv_rows, 1)

        @block.sync
        def _(sp):
            sp.wait_ge(wkv_rows, 1)
            for h in range(2):
                sp.dma_start(k.dram["prompt_wkv"][0, 0].rearrange("(m h) i j -> h i m j", h=2)[h],
                             k.w_now[HD * h:HD * h + HD, :, HD * h:HD * h + HD]).then_inc(wkv_out, 16)
            sp.wait_ge(wkv_out, 32)


def rwkv_sample(k):
    st = k.streams[0]
    st.pe, st.dve, st.act = (k.sem(f"rwkv_s_{e}_steps") for e in ("pe", "dve", "act"))
    levels = (2, 4)
    parts = [0] + [(m, what) for m in levels for what in ("x", "inc")]
    o = R2_AT
    rows = k.at("s_rows", o, [P, NSEQ, P]); o += 4096
    sq = k.at("s_state", o, [P, NSEQ, P]); o += 4096
    a_seq = k.at("a_seq", o, [P, NSEQ * (P + TSEQ)]); o += 4 * NSEQ * (P + TSEQ)
    u_seq = k.at("u_seq", o, [P, NSEQ, P]); o += 4096
    v_seq = k.at("v_seq", o, [P, NSEQ, P]); o += 4096
    out_rows = k.at("out_rows", o, [P, NSEQ, P]); o += 4096
    zeroed, rows_in, sq_mm, sq_done, a_done, w_mm, w_done, u_mm, u_done, o_mm, o_done, up_mm, up_done, back_mm, back_done, out_sem = (
        k.sem(f"ss_{n}") for n in ("zeroed", "rows_in", "sq_mm", "sq_done", "a_done", "w_mm", "w_done", "u_mm", "u_done",
                                   "o_mm", "o_done", "up_mm", "up_done", "back_mm", "back_done", "out"))
    state_v = k.dram["state_wkv"][0].rearrange("s (m h) i j -> m h i s j", h=2)
    out_v = k.dram["sample_wkv"][0].rearrange("s (m h) i j -> m h i s j", h=2)
    NE = NP_TOK // HD

    def store(sp, m):
        sp.wait_ge(back_done, m + 1)
        for h in range(2):
            sp.dma_start(out_v[m, h], out_rows[HD * h:HD * h + HD, :, HD * h:HD * h + HD]).then_inc(out_sem, 16)

    with k.nc.Block() as block:
        @block.sync
        def _(sp):
            sp.wait_ge(zeroed, 2)
            for m in range(PAIRS):
                if m >= 1:
                    sp.wait_ge(sq_mm, m)
                for h in range(2):
                    sp.dma_start(rows[HD * h:HD * h + HD, :, HD * h:HD * h + HD], state_v[m, h]).then_inc(rows_in, 16)
                if m >= 1:
                    store(sp, m - 1)
            store(sp, PAIRS - 1)
            sp.wait_ge(out_sem, 32 * PAIRS)

        @block.gpsimd
        def _(pool):
            for t in (rows, a_seq):
                pool.memset(t[:], 0.0).then_inc(zeroed, 1)

        @block.scalar
        def _(act):
            act.sem_inc(st.act, 1)
            gather(act, st, chunk_views(k, None), True).then_inc(st.act, 1)
            act_local(act, st, 0)
            act.wait_ge(zeroed, 2)
            for m in range(PAIRS):
                act.wait_ge(sq_mm, m + 1)
                for h in range(2):
                    act.copy(sq[:, 4 * h:4 * h + 4], pair4(k.psum[4 + h][:]))
                act.drain().then_inc(sq_done, 1)
                for h in range(2):
                    ins = act.copy(a_seq[:].rearrange("p (q n) -> p q n", n=P + TSEQ)[:, :, HD * h:HD * h + TSEQ],
                                   per_seq(st.a_bd[:, m, HD * h:HD * h + HD]))
                ins.then_inc(a_done, 1)
                act.wait_ge(w_mm, m + 1)
                act.copy(k.w_now[:, m], st.bank[3][:, P * m:P * m + P]).then_inc(w_done, 1)
                act.wait_ge(u_mm, m + 1)
                act.copy(k.u_now[:, m], st.bank[2][:, P * m:P * m + P]).then_inc(u_done, 1)
                act.wait_ge(o_mm, m + 1)
                act.copy(u_tok(k.u[:, m, 1:UW]), per_seq(st.bank[1][:, P * m + HD:P * m + P])).then_inc(o_done, 1)
                act.wait_ge(back_mm, m + 1)
                if m >= 1:
                    act.wait_ge(out_sem, 32 * m)
                for h in range(2):
                    ins = act.copy(out_rows[:, 4 * h:4 * h + 4], pair4(k.psum[4 + h][:]))
                ins.then_inc(back_done, 1)

        @block.tensor
        def _(pe):
            pe.sem_inc(st.pe, 1)
            for part in parts:
                pe_local(pe, st, 0, part, levels)
            ident = k.c("ident")
            for m in range(PAIRS):
                pe.wait_ge(rows_in, 32 * m + 32)
                if m >= 1:
                    pe.wait_ge(back_done, m)
                for q in range(NSEQ):
                    ins = pe.transpose(k.psum[4 + q // 4][:, P * (q % 4):P * (q % 4) + P], rows[:, q], ident)
                ins.then_inc(sq_mm, 1)
                col = slice(P * m, P * m + P)
                pe.wait_ge(a_done, m + 1)
                if m >= 1:
                    pe.wait_ge(w_done, m)
                pe.matmul(st.bank[3][:, col], st.lak[:, m], st.v_tok[:, m], start=True, stop=False)
                for q in range(NSEQ):
                    ins = pe.matmul(st.bank[3][:, col], a_seq[:, P * q:P * q + P], sq[:, q], start=False, stop=(q == NSEQ - 1))
                ins.then_inc(w_mm, 1)
                pe.wait_ge(w_done, m + 1)
                pe.wait_ge(st.dve, at_step(DVE_STEPS, 0, f"inc{levels[-1]}"))
                pe.matmul(st.bank[2][:, col], st.tt[:, m], k.w_now[:, m], start=True, stop=True).then_inc(u_mm, 1)
                pe.wait_ge(u_done, m + 1)
                if m >= 1:
                    pe.wait_ge(o_done, m)
                pe.matmul(st.bank[1][:, col], st.v_tok[:, m], st.mk[:, m], start=True, stop=False)
                pe.matmul(st.bank[1][:, col], k.u_now[:, m], st.mb[:, m], start=False, stop=False)
                for q in range(NSEQ):
                    at = P * m + HD + TSEQ * q
                    ins = pe.matmul(st.bank[1][:, at:at + TSEQ], sq[:, q],
                                    st.ar[:, m, HD + TSEQ * q:HD + TSEQ * q + TSEQ], start=False, stop=(q == NSEQ - 1))
                ins.then_inc(o_mm, 1)
                pe.wait_ge(up_done, 2 * m + 1)
                for h in range(2):
                    pe.matmul(k.psum[6 + h][:], st.b_tok[:, m], u_seq[:, 4 * h:4 * h + 4].rearrange("p q n -> p (q n)"),
                              start=True, stop=False)
                    ins = pe.matmul(k.psum[6 + h][:], st.k_tok[:, m], v_seq[:, 4 * h:4 * h + 4].rearrange("p q n -> p (q n)"),
                                    start=False, stop=True)
                ins.then_inc(up_mm, 1)
                pe.wait_ge(up_done, 2 * m + 2)
                for q in range(NSEQ):
                    ins = pe.transpose(k.psum[4 + q // 4][:, P * (q % 4):P * (q % 4) + P], sq[:, q], ident)
                ins.then_inc(back_mm, 1)

        @block.vector
        def _(dve):
            dve.sem_inc(st.dve, 1)
            for part in parts:
                dve_local(dve, st, 0, part, levels, k.c("causal_s"))
            seq = k.c("seq_of").unsqueeze(2).broadcast_to([P, NSEQ, P])
            for m in range(PAIRS):
                dve.wait_ge(u_done, m + 1)
                dve.wait_ge(st.act, at_step(ACT_STEPS, 0, "v_tok"))
                dve.tensor_tensor(v_seq[:], st.v_tok[:, m].unsqueeze(1).broadcast_to([P, NSEQ, P]), seq, ALU.mult)
                dve.tensor_tensor(u_seq[:], k.u_now[:, m].unsqueeze(1).broadcast_to([P, NSEQ, P]), seq, ALU.mult
                                  ).then_inc(up_done, 1)
                dve.wait_ge(up_mm, m + 1)
                for h in range(2):
                    dve.tensor_tensor(sq[:, 4 * h:4 * h + 4], sq[:, 4 * h:4 * h + 4], pair4(k.psum[6 + h][:]), ALU.add)
                dve.drain()
                dve.tensor_tensor(sq[:], sq[:], k.p_end[:, m, NE:].unsqueeze(2).broadcast_to([P, NSEQ, P]),
                                  ALU.mult).then_inc(up_done, 1)


def rwkv_finish(k):
    o = R2_AT
    dev = [k.at(f"dev{j}", o + UB * j, [P, W]) for j in range(2)]; o += 2 * UB
    sqd = k.at("dev_sq", o, [P, W]); o += UB
    rstd = [k.at(f"gn_rstd{j}", o + UB * j, [P, W]) for j in range(2)]; o += 2 * UB
    g2 = k.at("g2", o, [P, RW]); o += 2048
    g2_in, mean_mm, dev_done, sq_done, var_mm, var_done, root_done, g_mm, out_done = (
        k.sem(f"gn_{n}") for n in ("g2_in", "mean_mm", "dev_done", "sq_done", "var_mm", "var_done", "root_done", "g_mm", "out_done"))
    with k.nc.Block() as block:
        @block.sync
        def _(sp):
            sp.dma_start(g2[:], k.dram["rwkv_g2"][0]).then_inc(g2_in, 16)

        @block.tensor
        def _(pe):
            def mean(m):
                if m >= 1:
                    pe.wait_ge(dev_done, m)
                for t, (a, n) in enumerate(UTILES):
                    ins = pe.matmul(k.psum[t][:, 0:n], k.c("head_mean"), k.u[:, m, 1 + a:1 + a + n], start=True, stop=True)
                ins.then_inc(mean_mm, 1)

            mean(0)
            pe.wait_ge(g2_in, 16)
            for m in range(PAIRS):
                if m + 1 < PAIRS:
                    mean(m + 1)
                pe.wait_ge(sq_done, m + 1)
                if m >= 1:
                    pe.wait_ge(var_done, m)
                for t, (a, n) in enumerate(UTILES[:2]):
                    pe.matmul(k.psum[3 + t][:, 0:n], k.c("head_mean"), sqd[:, a:a + n], start=True, stop=True)
                a, n = UTILES[2]
                pe.matmul(k.psum[5][:, 0:n], k.c("head_mean"), sqd[:, a:a + n], start=True, stop=True).then_inc(var_mm, 1)
                for t, (a, n) in enumerate(UTILES):
                    v = 3 * m + t
                    if v >= 2:
                        pe.wait_ge(out_done, v - 1)
                    pe.matmul(k.psum[6 + v % 2][:, 0:n], g2[:, P * m:P * m + P], k.u[:, 13, 1 + a:1 + a + n],
                              start=True, stop=True).then_inc(g_mm, 1)

        @block.vector
        def _(dve):
            def deviation(m):
                dve.wait_ge(mean_mm, m + 1)
                for t, (a, n) in enumerate(UTILES):
                    ins = dve.tensor_tensor(dev[m % 2][:, a:a + n], k.u[:, m, 1 + a:1 + a + n], k.psum[t][:, 0:n], ALU.subtract)
                ins.then_inc(dev_done, 1)

            def variance(m):
                dve.wait_ge(var_mm, m + 1)
                for t, (a, n) in enumerate(UTILES):
                    ins = dve.tensor_scalar(rstd[m % 2][:, a:a + n], k.psum[3 + t][:, 0:n], LNX_EPS, None, ALU.add)
                ins.then_inc(var_done, 1)

            deviation(0)
            variance(0)
            for m in range(PAIRS):
                if m + 1 < PAIRS:
                    dve.drain()
                    deviation(m + 1)
                dve.wait_ge(root_done, m + 1)
                dve.reciprocal(rstd[m % 2][:], rstd[m % 2][:])
                dve.drain()
                dve.tensor_tensor(dev[m % 2][:], dev[m % 2][:], rstd[m % 2][:], ALU.mult)
                dve.drain()
                dve.tensor_scalar(dev[m % 2][:], dev[m % 2][:], k.p2("ln_x_w", m), k.p2("ln_x_b", m), ALU.mult, ALU.add)
                dve.drain()
                dve.tensor_tensor(dev[m % 2][:], dev[m % 2][:], k.bon[:, m], ALU.add)
                dve.drain()
                for t, (a, n) in enumerate(UTILES):
                    v = 3 * m + t
                    dve.wait_ge(g_mm, v + 1)
                    dve.tensor_tensor(k.u[:, m, 1 + a:1 + a + n], dev[m % 2][:, a:a + n], k.psum[6 + v % 2][:, 0:n],
                                      ALU.mult).then_inc(out_done, 1)
                if m + 1 < PAIRS:
                    variance(m + 1)

        @block.scalar
        def _(act):
            for m in range(PAIRS):
                act.wait_ge(dev_done, m + 1)
                if m >= 1:
                    act.wait_ge(var_mm, m)
                act.activation(sqd[:], dev[m % 2][:], ACT.Square).then_inc(sq_done, 1)
                act.wait_ge(var_done, m + 1)
                act.activation(rstd[m % 2][:], rstd[m % 2][:], ACT.Sqrt).then_inc(root_done, 1)


def output_projection(k):
    split_hi, split_lo, x_back = k.sem("split_hi"), k.sem("split_lo"), k.sem("x_back")
    with k.nc.Block() as block:
        @block.vector
        def _(dve):
            for m in range(PAIRS):
                dve.tensor_copy(k.hh[:, m, 0:NP_TOK], k.u[:, m, 1:1 + NP_TOK])
                dve.tensor_copy(per_seq(k.hh[:, m, NP_TOK:T]), u_tok(k.u[:, m, 1:UW])).then_inc(split_hi, 1)
            for m in range(PAIRS):
                dve.tensor_copy(k.hh[:, 4 + m, :], k.qkv[:, m, :]).then_inc(split_hi, 1)
            for m in range(2, PAIRS):
                dve.wait_ge(split_hi, 4 + m + 1)
                dve.tensor_tensor(k.hl[:, 4 + m, :], k.qkv[:, m, :], k.hh[:, 4 + m, :].bitcast(F32), ALU.subtract)
            dve.drain().then_inc(split_lo, 1)

        @block.gpsimd
        def _(pool):
            for m in range(PAIRS):
                pool.wait_ge(split_hi, m + 1)
                pool.tensor_tensor(k.hl[:, m, 0:NP_TOK], k.u[:, m, 1:1 + NP_TOK], k.hh[:, m, 0:NP_TOK].bitcast(F32), ALU.subtract)
                pool.tensor_tensor(per_seq(k.hl[:, m, NP_TOK:T]), u_tok(k.u[:, m, 1:UW]),
                                   per_seq(k.hh[:, m, NP_TOK:T].bitcast(F32)), ALU.subtract)
            for m in range(2):
                pool.wait_ge(split_hi, 4 + m + 1)
                ins = pool.tensor_tensor(k.hl[:, 4 + m, :], k.qkv[:, m, :], k.hh[:, 4 + m, :].bitcast(F32), ALU.subtract)
            ins.then_inc(split_lo, 1)

        @block.sync
        def _(sp):
            sp.wait_ge(split_lo, 2)
            sp.dma_start(k.x[:], k.dram["x_spill"]).then_inc(x_back, 16)
            sp.wait_ge(x_back, 16)

    w = k.dram["w_out"][0]
    wr = w[0:RW].rearrange("(k p) (f n) -> p f k n", p=P, n=P)
    wa = w[RW:].rearrange("(h c p) (f n) -> h p f c n", h=2, p=HD, n=P)
    scratch = k.at("w_out_scratch", R2_AT + 24 * KB, [P, 2, NS_TOK])

    def load(sp, raw, i, j, sem):
        if sp is not None:
            f = bass.ds(2 * i + j, 1)
            sp.dma_start(raw[:, 0:4], wr[:, f].rearrange("p o k n -> p (o k) n")).then_inc(sem, 16)
            for h in range(2):
                sp.dma_start(raw[HD * h:HD * h + HD, 4:8], wa[h][:, f].rearrange("p o c n -> p (o c) n")).then_inc(sem, 16)
        return 3

    def evac(dve, i, j, t, bank):
        return add_gated(dve, k, 5, 2 * i + j, t, bank, scratch[:, j])

    stream_product(k, "w_out", R2_AT, [(KD // 2, load, evac)], k.hh, k.hl, False)


def store_output(k):
    x_now = [k.at(f"x_now{j}", WT_AT + 4096 * j, [P, KD, P]) for j in range(2)]
    rows = [k.at(f"y_rows{j}", WT_AT + 4096 * (2 + j), [P, D]) for j in range(2)]
    now_done, turned, rows_done = (k.sem(f"y_{n}") for n in ("now_done", "turned", "rows_done"))
    y_out = [k.sem(f"y_out{j}") for j in range(2)]
    NTT = NP_TOK // P
    yv = k.dram["y_prompt"][0].rearrange("(i j p) n -> j p i n", p=P, j=2)
    with k.nc.Block() as block:
        @block.scalar
        def _(act):
            def take(count, j, x, n):
                act.wait_ge(turned, count + 1)
                act.copy(x_now[j][:, :, 0:n], x).then_inc(now_done, 1)

            with act.Fori(0, NTT // 2) as i:
                for j in range(2):
                    take(2 * i + j, j, k.x[:, :, bass.ds(256 * i + 128 * j, P)], P)
            take(NTT, 0, k.x[:, :, NP_TOK:T], NS_TOK)

        @block.tensor
        def _(pe):
            pe.sem_inc(turned, 2)

            def turn(count, j, n):
                pe.wait_ge(now_done, count + 1)
                pe.wait_ge(rows_done, count + 1)
                for c in range(KD):
                    ins = pe.transpose(k.psum[2 * j + c // 4][0:n, P * (c % 4):P * (c % 4) + P], x_now[j][:, c, 0:n],
                                       k.c("ident"))
                ins.then_inc(turned, 1)

            with pe.Fori(0, NTT // 2) as i:
                for j in range(2):
                    turn(2 * i + j, j, P)
            turn(NTT, 0, NS_TOK)

        @block.vector
        def _(dve):
            dve.sem_inc(rows_done, 2)

            def collect(i, j, n):
                dve.wait_ge(turned, 2 * i + j + 3)
                dve.wait_ge(y_out[j], 16 * i + 16)
                for h in range(2):
                    ins = dve.tensor_copy(rows[j][0:n, 512 * h:512 * h + 512], k.psum[2 * j + h][0:n, :])
                ins.then_inc(rows_done, 1)

            with dve.Fori(0, NTT // 2) as i:
                for j in range(2):
                    collect(i, j, P)
            collect(NTT // 2, 0, NS_TOK)

        @block.sync
        def _(sp):
            for j in range(2):
                sp.sem_inc(y_out[j], 16)
            with sp.Fori(0, NTT // 2) as i:
                for j in range(2):
                    sp.wait_ge(rows_done, 2 * i + j + 3)
                    sp.dma_start(yv[j][:, bass.ds(i, 1)].rearrange("p o n -> p (o n)"), rows[j][:]).then_inc(y_out[j], 16)
            sp.wait_ge(rows_done, NTT + 3)
            sp.dma_start(k.dram["y_sample"].rearrange("s t n -> (s t) n"), rows[0][0:NS_TOK, :]).then_inc(y_out[0], 16)
            sp.wait_ge(y_out[0], 16 * (NTT // 2 + 2))
            sp.wait_ge(y_out[1], 16 * (NTT // 2 + 1))
            sp.wait_ge(k.cache_out, 16 * k.n_cache_out)


OUTS = [("y_prompt", [1, NP_TOK, D]), ("y_sample", [NSEQ, TSEQ, D]), ("prompt_wkv", [1, 1, 8, HD, HD]),
        ("prompt_shift", [1, 1, U_COLS]), ("prompt_k", [1, 1, WINDOW, 2, HD]), ("prompt_v", [1, 1, WINDOW, 2, HD]),
        ("sample_wkv", [1, NSEQ, 8, HD, HD]), ("sample_shift", [1, NSEQ, U_COLS]),
        ("sample_k", [1, NSEQ, WINDOW, 2, HD]), ("sample_v", [1, NSEQ, WINDOW, 2, HD])]


def build(nc, dram):
    with ExitStack() as ctx:
        k = Core(nc, dram, ctx)
        load_and_modulate(k)
        ffn(k, "f1", dram["ffn1_w_gu"], dram["ffn1_w_down"], 0)
        input_projection(k)
        attention_prepare(k)
        attention_prompt(k)
        attention_sample(k)
        k.release(keep=(k.cache_out,))
        rwkv_shift(k)
        rwkv_keys(k)
        rwkv_decay(k)
        rwkv_prompt(k)
        rwkv_sample(k)
        rwkv_finish(k)
        output_projection(k)
        k.release(keep=(k.cache_out,))
        ffn(k, "f2", dram["ffn2_w_gu"], dram["ffn2_w_down"], 6)
        norm_final(k)
        store_output(k)


def kernel(**inputs):
    import concourse.bacc as bacc
    from concourse.bass_utils import run_bass_kernel_spmd

    cos, sin = rope_tables()
    given = dict(inputs, consts=np.concatenate(list(CONST.values()), axis=1), scan_keep=scan_keep(), cos=cos, sin=sin)
    nc = bacc.Bacc("TRN2", target_bir_lowering=False, num_devices=1)
    arrays, dram = {}, {}
    for name, value in given.items():
        a = np.ascontiguousarray(value)
        arrays[f"in_{name}"] = a
        dram[name] = nc.dram_tensor(f"in_{name}", a.shape, mybir.dt.from_np(a.dtype), kind="ExternalInput").ap()
    for name, shape in OUTS:
        dram[name] = nc.dram_tensor(f"out_{name}", shape, F32, kind="ExternalOutput").ap()
    dram["x_spill"] = nc.dram_tensor("x_spill", [P, KD, T], F32, kind="Internal").ap()
    build(nc, dram)
    r = run_bass_kernel_spmd(nc, [arrays], core_ids=[0])
    return tuple(r.results[0][f"out_{name}"] for name, _ in OUTS)
```

```python
from contextlib import ExitStack

import numpy as np

import concourse.bass as bass
from concourse import mybir

F32 = mybir.dt.float32
F32R = mybir.dt.float32r
ALU = mybir.AluOpType
ACT = mybir.ActivationFunctionType
AX = mybir.AxisListType

P = 128
D = 1024
KD = D // P
NP_TOK = 1024
NSEQ = 8
TSEQ = 8
NS_TOK = NSEQ * TSEQ
T = NP_TOK + NS_TOK
D_FF = 2816
N_ADA = 9
HD = 64
RW = 512
PAIRS = RW // P
U_COLS = 1792
UC = U_COLS // P
WINDOW = 128
EPS = 1e-5
LNX_EPS = 64e-5

TILES = [(0, 364), (364, 364), (728, 360)]
TW = 364
NT = len(TILES)

LEVELS = (1, 2, 4, 8, 16, 32)
UW = 1 + NP_TOK + NSEQ * (TSEQ + 1)
W = UW - 1

ROWS1 = [("b_ada", N_ADA * KD), ("norm_ffn1", KD), ("norm_mix", KD), ("norm_ffn2", KD)]
ROWS2 = [("mu_shift", UC), ("rwkv_w0", PAIRS), ("rwkv_a0", PAIRS), ("rwkv_k_k", PAIRS), ("rwkv_k_a", PAIRS),
         ("rwkv_r_k", PAIRS), ("ln_x_w", PAIRS), ("ln_x_b", PAIRS)]


def row_starts(rows):
    at, out = 0, {}
    for name, n in rows:
        out[name] = at
        at += n
    return out, at


AT1, N1 = row_starts(ROWS1)
AT2, N2 = row_starts(ROWS2)

BASE = 16512
KB = 1024
TB = T * 4
CONST_AT = BASE
X_AT = BASE + 17 * KB
HH_AT = X_AT + KD * TB
HL_AT = HH_AT + KD * TB
WT_AT = HL_AT + KD * TB
ACT_AT = WT_AT + 64 * KB
TMP_AT = ACT_AT + 4 * TB
END = 229368
SLOT = 1472


def up32(n):
    return (n + 31) // 32 * 32


def make_constants():
    p = np.arange(P)
    blk = (p[:, None] // HD) == (p[None, :] // HD)
    lo, lc = p % HD, np.arange(HD)
    out = {
        "ident": np.eye(P),
        "mean_all": np.full((P, P), 1.0 / D),
        "head_sum": blk * 1.0,
        "head_mean": blk / HD,
    }
    rot = np.zeros((P, P))
    for h in range(2):
        for j in range(8):
            rot[h * HD + 8 + j, h * HD + j] = -1.0
            rot[h * HD + j, h * HD + 8 + j] = 1.0
    out["rot"] = rot
    same = (lo[:, None] // TSEQ) == (lc[None, :] // TSEQ)
    before, upto = lo[:, None] < lc[None, :], lo[:, None] <= lc[None, :]
    out["causal"] = np.concatenate([before, upto], axis=1)
    out["causal_s"] = np.concatenate([before & same, upto & same], axis=1)
    for m in LEVELS:
        t, s = lo[:, None] // m, lo[None, :] // m
        out[f"lev{m}"] = blk & (t % 2 == 1) & (s == t - 1)
    out["lev1T"] = out["lev1"].T
    out["seq_of"] = (lo[:, None] // TSEQ) == np.arange(NSEQ)[None, :]
    q, k = p[:, None], np.arange(2 * WINDOW)[None, :]
    ok = (k - WINDOW <= q) & (q - (k - WINDOW) < WINDOW)
    out["mask_p"] = np.where(ok, 0.0, -1e30)
    out["mask_p0"] = np.where(ok & (k >= WINDOW), 0.0, -1e30)
    t, k = p[:, None] % TSEQ, np.arange(WINDOW + TSEQ)[None, :]
    out["ones"] = np.ones((P, P))
    out["eps"] = np.full((P, 1), EPS)
    row = 2 * np.arange(PAIRS)[:, None] + (p // HD)[None, :]
    out["to_rows"] = (row[:, :, None] == np.arange(8)).transpose(1, 0, 2).reshape(P, 8 * PAIRS)
    out["from_rows"] = ((p % 32)[:, None, None] == row[None, :, :]).reshape(P, PAIRS * P)
    out["row_chunk"] = np.zeros((P, P))
    out["row_chunk"][0:4] = np.arange(4)[:, None] == (p[None, :] % 32) // TSEQ
    out["mask_s"] = np.where((k > t) & (k - WINDOW <= t), 0.0, -1e30)
    return {n: np.ascontiguousarray(a, np.float32) for n, a in out.items()}


def scan_keep():
    keep = np.ones((P, W), np.float32)
    keep[:, 0:NP_TOK:HD] = 0.0
    keep[:, NP_TOK + 1::TSEQ + 1] = 0.0
    return keep


def rope_tables():
    pos = np.concatenate([np.arange(NP_TOK), np.tile(2048 + np.arange(TSEQ), NSEQ)]).astype(np.float32)
    inv = np.float32(500000.0) ** (-np.arange(0, 16, 2, dtype=np.float32) / np.float32(16))
    ang = (pos[None, :] * inv[:, None].astype(np.float32)).astype(np.float32)
    cos, sin = np.ones((P, T), np.float32), np.zeros((P, T), np.float32)
    for h in range(2):
        for part in range(2):
            at = h * HD + 8 * part
            cos[at:at + 8], sin[at:at + 8] = np.cos(ang), np.sin(ang)
    return cos, sin


CONST = make_constants()
CONST_COL = {}
_at = 0
for _n, _a in CONST.items():
    CONST_COL[_n] = (_at, _a.shape[1])
    _at += _a.shape[1]
NCONST = _at


class Core:

    def __init__(self, nc, dram, ctx):
        self.nc, self.dram, self.ctx = nc, dram, ctx
        self.phase_sems = []
        self.psum = [ctx.enter_context(nc.psum_tensor(f"bank{i}", [P, 512], F32)) for i in range(8)]
        self.const = self.at("const", CONST_AT, [P, NCONST])
        o = up32(CONST_AT + 4 * NCONST)
        self.mods = self.at("mods", o, [P, N_ADA * KD, 9])
        o = up32(o + 4 * N_ADA * KD * 9)
        self.par1 = self.at("par1", o, [P, N1])
        o = up32(o + 4 * N1)
        self.par2 = self.at("par2", o, [P, N2])
        o = up32(o + 4 * N2)
        self.p_end = self.at("p_end", o, [P, PAIRS, NP_TOK // HD + NSEQ])
        o = up32(o + 4 * PAIRS * (NP_TOK // HD + NSEQ))
        assert o <= X_AT, o - CONST_AT
        self.x = self.at("x", X_AT, [P, KD, T])
        self.hh = self.at("hh", HH_AT, [P, KD, T], F32R)
        self.hl = self.at("hl", HL_AT, [P, KD, T], F32R)
        self.u = self.at("u", U_AT, [P, UC, UW])
        self.qkv = self.at("qkv", QKV_AT, [P, 6, T])

    def at(self, name, off, shape, dt=F32):
        assert off % 4 == 0 and off + 4 * int(np.prod(shape[1:])) <= END, name
        return self.nc.alloc_sbuf_tensor_at(name, shape, dt, offset=off)

    def c(self, name):
        a, n = CONST_COL[name]
        return self.const[:, a:a + n]

    def sem(self, name):
        sem = self.nc.alloc_semaphore(name)
        self.phase_sems.append(sem)
        return sem

    def release(self, keep=()):
        self.nc.clear_and_free_semaphores([s for s in self.phase_sems if s not in keep])
        self.nc.all_engine_barrier()
        self.phase_sems = list(keep)

    def p1(self, name, i):
        return self.par1[:, AT1[name] + i:AT1[name] + i + 1]

    def p2(self, name, i):
        return self.par2[:, AT2[name] + i:AT2[name] + i + 1]

    def mod(self, i, k, s0=0, n=1):
        return self.mods[:, i * KD + k, s0:s0 + n]


def per_seq(ap):
    return ap.rearrange("p (s t) -> p s t", t=TSEQ)


def over_tokens(ap):
    return ap.unsqueeze(2).broadcast_to([P, NSEQ, TSEQ])


def load_and_modulate(k):
    d = k.dram
    rows1 = k.at("rows1", TMP_AT, [P, P])
    rows2 = k.at("rows2", TMP_AT + 512, [P, P])
    c_rows = k.at("c_rows", ACT_AT, [9, D])
    c_silu = k.at("c_silu", ACT_AT + 4096, [9, D])
    x_in = [k.at(f"x_in{j}", ACT_AT + 8192 + 4096 * j, [P, D]) for j in range(2)]
    cT = k.at("cT", TMP_AT + 1024, [P, KD, 32])
    mod_rows = k.at("mod_rows", TMP_AT + 2048, [P, 2 * P])
    NQ = KD // 2
    w_ada = [k.at(f"w_ada{q}", WT_AT + 8 * KB * q, [P, 2, D]) for q in range(NQ)]

    const_in, rows_in, c_in = k.sem("const_in"), k.sem("rows_in"), k.sem("c_in")
    silu_done, par_mm, par_done, c_mm, c_done = (k.sem(n) for n in ("silu_done", "par_mm", "par_done", "c_mm", "c_done"))
    x_in_done = [k.sem(f"x_in_done{j}") for j in range(2)]
    xt_mm, xt_free = k.sem("xt_mm"), k.sem("xt_free")
    ada_in = [k.sem(f"ada_in{q}") for q in range(NQ)]
    ada_used, ada_mm, ada_rows, ada_turned, ada_free = (
        k.sem(n) for n in ("ada_used", "ada_mm", "ada_rows", "ada_turned", "ada_free"))
    mods_done = k.sem("mods_done")
    w_ada_view = d["w_ada"][0].rearrange("(q k p) (i n) -> q p i k n", p=P, k=2, n=D)

    with k.nc.Block() as block:
        @block.sync
        def _(sp):
            sp.dma_start(c_rows[0:1, :], d["c_prompt"]).then_inc(c_in, 16)
            sp.dma_start(c_rows[1:9, :], d["c_sample"]).then_inc(c_in, 16)
            sp.dma_start(k.const[:], d["consts"]).then_inc(const_in, 16)
            for names, tile, at in ((ROWS1, rows1, AT1), (ROWS2, rows2, AT2)):
                for name, n in names:
                    src = d[name]
                    flat = src.rearrange("(n p) -> n p", p=P) if len(src.shape) == 1 else (
                        src[0].rearrange("(n p) -> n p", p=P) if len(src.shape) == 2 else
                        src[0].rearrange("(n h) i -> n (h i)", h=2))
                    sp.dma_start(tile[at[name]:at[name] + n, :], flat).then_inc(rows_in, 16)
            for q in range(NQ):
                sp.dma_start(w_ada[q][:], w_ada_view[q][:, 0]).then_inc(ada_in[q], 16)
            with sp.Fori(0, N_ADA - 1) as i:
                for q in range(NQ):
                    sp.wait_ge(ada_used, NQ * i + q + 1)
                    sp.dma_start(w_ada[q][:], w_ada_view[q][:, bass.ds(i + 1, 1)].rearrange("p o k n -> p (o k) n")
                                 ).then_inc(ada_in[q], 16)

        @block.gpsimd
        def _(pool):
            xv = d["x_prompt"][0].rearrange("(i j p) n -> j p i n", p=P, j=2)
            for j in range(2):
                pool.dma_start(x_in[j][:], xv[j][:, 0]).then_inc(x_in_done[j], 16)
            with pool.Fori(1, NP_TOK // P // 2) as i:
                for j in range(2):
                    pool.wait_ge(xt_mm, 2 * i + j - 1)
                    pool.dma_start(x_in[j][:], xv[j][:, bass.ds(i, 1)].rearrange("p o n -> p (o n)")
                                   ).then_inc(x_in_done[j], 16)
            pool.wait_ge(xt_mm, NP_TOK // P - 1)
            pool.dma_start(x_in[0][0:NS_TOK, :], d["x_sample"].rearrange("s t n -> (s t) n")).then_inc(x_in_done[0], 16)

        @block.scalar
        def _(act):
            act.wait_ge(c_in, 32)
            act.activation(c_silu[:], c_rows[:], ACT.Silu).then_inc(silu_done, 1)
            act.sem_inc(xt_free, 2)

            def evac(j, dst, n):
                for h in range(2):
                    ins = act.copy(dst[:, 4 * h:4 * h + 4, :], k.psum[2 + 2 * j + h][:, 0:4 * n].rearrange(
                        "p (c t) -> p c t", t=n))
                ins.then_inc(xt_free, 1)

            with act.Fori(0, NP_TOK // P // 2) as i:
                for j in range(2):
                    act.wait_ge(xt_mm, 2 * i + j + 1)
                    evac(j, k.x[:, :, bass.ds(256 * i + 128 * j, P)], P)
            act.wait_ge(xt_mm, NP_TOK // P + 1)
            evac(0, k.x[:, :, NP_TOK:T], NS_TOK)

        @block.tensor
        def _(pe):
            ident = k.c("ident")
            pe.wait_ge(const_in, 16)
            pe.wait_ge(rows_in, 16 * (len(ROWS1) + len(ROWS2)))
            pe.transpose(k.psum[0][:, 0:N1], rows1[0:N1, :], ident[0:N1, 0:N1])
            pe.transpose(k.psum[0][:, N1:N1 + N2], rows2[0:N2, :], ident[0:N2, 0:N2]).then_inc(par_mm, 1)
            pe.wait_ge(silu_done, 1)
            for c in range(KD):
                ins = pe.transpose(k.psum[1][:, 9 * c:9 * c + 9], c_silu[0:9, P * c:P * c + P], ident[0:9, 0:9])
            ins.then_inc(c_mm, 1)

            def turn(j, n):
                for c in range(KD):
                    ins = pe.transpose(k.psum[2 + 2 * j + c // 4][:, (c % 4) * n:(c % 4) * n + n],
                                       x_in[j][0:n, P * c:P * c + P], ident[0:n, 0:n])
                ins.then_inc(xt_mm, 1)

            with pe.Fori(0, NP_TOK // P // 2) as i:
                for j in range(2):
                    pe.wait_ge(x_in_done[j], 16 * i + 16)
                    pe.wait_ge(xt_free, 2 * i + j + 1)
                    turn(j, P)
            pe.wait_ge(x_in_done[0], 16 * (NP_TOK // P // 2) + 16)
            pe.wait_ge(xt_free, NP_TOK // P + 1)
            turn(0, NS_TOK)
            pe.wait_ge(c_done, 1)
            with pe.Fori(0, N_ADA) as i:
                pe.wait_ge(ada_free, i + 1)
                for q in range(NQ):
                    pe.wait_ge(ada_in[q], 16 * i + 16)
                    for h in range(2):
                        for j in range(4):
                            ins = pe.matmul(k.psum[6][32 * j:32 * j + 32, 0:256], cT[:, 2 * q + h, :],
                                            w_ada[q][:, h, 256 * j:256 * j + 256],
                                            start=(q == 0 and h == 0), stop=(q == NQ - 1 and h == 1))
                    ins.then_inc(ada_used, 1)
                pe.wait_ge(ada_rows, i + 1)
                for h in range(2):
                    ins = pe.transpose(k.psum[7][:, P * h:P * h + P], mod_rows[:, P * h:P * h + P], ident)
                ins.then_inc(ada_turned, 1)

        @block.vector
        def _(dve):
            dve.memset(cT[:], 0.0)
            dve.drain()
            dve.wait_ge(par_mm, 1)
            dve.tensor_copy(k.par1[:], k.psum[0][:, 0:N1])
            dve.tensor_copy(k.par2[:], k.psum[0][:, N1:N1 + N2]).then_inc(par_done, 1)
            dve.wait_ge(c_mm, 1)
            dve.tensor_copy(cT[:, :, 0:9], k.psum[1][:, 0:9 * KD].rearrange("p (c s) -> p c s", s=9)).then_inc(c_done, 1)
            dve.drain()
            dve.sem_inc(ada_free, 1)
            with dve.Fori(0, N_ADA) as i:
                dve.wait_ge(ada_used, NQ * i + NQ)
                dve.tensor_copy(mod_rows[:], k.psum[6][:, 0:256]).then_inc(ada_rows, 1)
                dve.wait_ge(ada_turned, i + 1)
                dve.tensor_tensor(k.mods[:, bass.ds(KD * i, KD), :].rearrange("p (j h) s -> p j h s", h=2),
                                  k.psum[7][:, 0:256].rearrange("p (h j s) -> p j h s", h=2, j=4)[:, :, :, 0:9],
                                  k.par1[:, bass.ds(KD * i, KD)].rearrange("p (j h) -> p j h", h=2).unsqueeze(3)
                                  .broadcast_to([P, 4, 2, 9]), ALU.add).then_inc(ada_free, 1)
            dve.drain()
            for i, name in ((1, "norm_ffn1"), (4, "norm_mix"), (7, "norm_ffn2")):
                g = k.par1[:, AT1[name]:AT1[name] + KD].unsqueeze(2).broadcast_to([P, KD, 9])
                dve.scalar_tensor_tensor(k.mods[:, i * KD:(i + 1) * KD, :], k.mods[:, i * KD:(i + 1) * KD, :], 1.0, g,
                                         ALU.add, ALU.mult)
            for i in (2, 8):
                ins = dve.tensor_scalar(k.mods[:, i * KD:(i + 1) * KD, :], k.mods[:, i * KD:(i + 1) * KD, :],
                                        0.5, None, ALU.mult)
            ins.then_inc(mods_done, 1)
            dve.wait_ge(mods_done, 1)


class Norm:

    def __init__(self, k, name, i_shift, at, bank):
        self.k, self.i_shift = k, i_shift
        self.bank = k.psum[bank:bank + NT]
        self.sq = [k.at(f"{name}_sq{j}", at + 4 * SLOT * j, [P, KD // 2, TW]) for j in range(2)]
        at += 8 * SLOT
        self.rstd = [k.at(f"{name}_rstd{j}", at + SLOT * j, [P, TW]) for j in range(2)]
        at += 2 * SLOT
        self.t = [k.at(f"{name}_t{j}", at + SLOT * j, [P, TW]) for j in range(4)]
        at += 4 * SLOT
        self.ts = k.at(f"{name}_ts", at, [P, KD, NS_TOK])
        (self.sq_done, self.sq_used, self.root_done, self.t_done, self.hi_done, self.lo_done) = (
            k.sem(f"{name}_{n}") for n in ("sq_done", "sq_used", "root_done", "t_done", "hi_done", "lo_done"))

    def spans(self, t):
        a, n = TILES[t]
        return a, min(n, NP_TOK - a)

    def act_squares(self, act, t):
        a, n = TILES[t]
        for j in range(2):
            if t >= 1:
                act.wait_ge(self.sq_used, 2 * t + j - 1)
            act.activation(self.sq[j][:, :, 0:n], self.k.x[:, 4 * j:4 * j + 4, a:a + n], ACT.Square
                           ).then_inc(self.sq_done, 1)

    def act_root(self, act, t):
        n = TILES[t][1]
        act.wait_ge(self.sq_used, 2 * t + 2)
        if t >= 2:
            act.wait_ge(self.t_done, KD * (t - 1))
        act.activation(self.rstd[t % 2][:, 0:n], self.bank[t][:, 0:n], ACT.Sqrt, bias=self.k.c("eps")
                       ).then_inc(self.root_done, 1)

    def act_heads(self, act, t):
        a, n = self.spans(t)
        for c in range(KD):
            act.wait_ge(self.t_done, KD * t + c + 1)
            act.activation(self.k.hh[:, c, a:a + n], self.t[c % 4][:, 0:n], ACT.Identity,
                           bias=self.k.mod(self.i_shift, c)).then_inc(self.hi_done, 1)

    def act(self, act):
        self.act_squares(act, 0)
        self.act_squares(act, 1)
        self.act_root(act, 0)
        self.act_squares(act, 2)
        self.act_heads(act, 0)
        self.act_root(act, 1)
        self.act_heads(act, 1)
        self.act_root(act, 2)
        self.act_heads(act, 2)

    def pe(self, pe):
        for t, (a, n) in enumerate(TILES):
            for c in range(KD):
                if c % 4 == 0:
                    pe.wait_ge(self.sq_done, 2 * t + c // 4 + 1)
                ins = pe.matmul(self.bank[t][:, 0:n], self.k.c("mean_all"), self.sq[c // 4][:, c % 4, 0:n],
                                start=(c == 0), stop=(c == KD - 1))
                if c % 4 == 3:
                    ins.then_inc(self.sq_used, 1)

    def pe_ready(self, pe, t):
        pe.wait_ge(self.hi_done, KD * (t + 1))
        pe.wait_ge(self.lo_done, t + 1)

    def tail(self, dve, t, c):
        a, n = self.spans(t)
        dve.wait_ge(self.hi_done, KD * t + c + 1)
        return dve.scalar_tensor_tensor(self.k.hl[:, c, a:a + n], self.t[c % 4][:, 0:n], self.k.mod(self.i_shift, c),
                                        self.k.hh[:, c, a:a + n].bitcast(F32), ALU.add, ALU.subtract)

    def dve(self, dve, t):
        k, (a, n) = self.k, self.spans(t)
        rstd = self.rstd[t % 2]
        dve.wait_ge(self.root_done, t + 1)
        dve.reciprocal(rstd[:, 0:TILES[t][1]], rstd[:, 0:TILES[t][1]])
        dve.drain()
        for c in range(KD):
            if KD * t + c >= 4:
                dve.drain()
            dve.scalar_tensor_tensor(self.t[c % 4][:, 0:n], k.x[:, c, a:a + n], k.mod(self.i_shift + 1, c), rstd[:, 0:n],
                                     ALU.mult, ALU.mult).then_inc(self.t_done, 1)
            if c >= 2:
                self.tail(dve, t, c - 2)
        self.tail(dve, t, KD - 2)
        last = self.tail(dve, t, KD - 1)
        if t == NT - 1:
            ts4 = self.ts[:].rearrange("p c (s t) -> p c s t", t=TSEQ)

            def over(i):
                return k.mods[:, i * KD:(i + 1) * KD, 1:9].unsqueeze(3).broadcast_to([P, KD, NSEQ, TSEQ])

            dve.tensor_tensor(self.ts[:], k.x[:, :, NP_TOK:T],
                              rstd[:, n:n + NS_TOK].unsqueeze(1).broadcast_to([P, KD, NS_TOK]), ALU.mult)
            dve.drain()
            dve.tensor_tensor(ts4, ts4, over(self.i_shift + 1), ALU.mult)
            dve.drain()
            dve.tensor_tensor(ts4, ts4, over(self.i_shift), ALU.add)
            dve.drain()
            dve.tensor_copy(k.hh[:, :, NP_TOK:T], self.ts[:])
            dve.drain()
            last = dve.tensor_tensor(k.hl[:, :, NP_TOK:T], self.ts[:], k.hh[:, :, NP_TOK:T].bitcast(F32), ALU.subtract)
        last.then_inc(self.lo_done, 1)

    def wait_all(self, eng):
        eng.wait_ge(self.hi_done, KD * NT)
        eng.wait_ge(self.lo_done, NT)


def three_passes(pe, out, pairs):
    last = len(pairs) - 1
    for n, (wh, wl, rh, rl) in enumerate(pairs):
        pe.matmul(out, wh, rh, start=(n == 0), stop=False)
        pe.matmul(out, wh, rl, start=False, stop=False)
        ins = pe.matmul(out, wl, rh, start=False, stop=(n == last))
    return ins


def add_gated(dve, k, i_gate, c, tile, bank, scratch):
    a, n = TILES[tile]
    np_ = min(n, NP_TOK - a)
    if isinstance(c, int):
        x, gate = k.x[:, c, :], k.mods[:, i_gate * KD + c, :]
    else:
        x = k.x[:, bass.ds(c, 1), :].rearrange("p o n -> p (o n)")
        gate = k.mods[:, bass.ds(c + i_gate * KD, 1), :].rearrange("p o s -> p (o s)")
    ins = dve.scalar_tensor_tensor(x[:, a:a + np_], bank[:, 0:np_], gate[:, 0:1], x[:, a:a + np_], ALU.mult, ALU.add)
    if np_ < n:
        ins = dve.tensor_tensor(per_seq(scratch), per_seq(bank[:, np_:n]), over_tokens(gate[:, 1:9]), ALU.mult)
        dve.drain()
        dve.tensor_tensor(x[:, NP_TOK:T], x[:, NP_TOK:T], scratch, ALU.add)
    return ins


def ffn(k, name, w_gu, w_down, i_shift):
    nc = k.nc
    i_gate = i_shift + 2
    norm = Norm(k, name, i_shift, ACT_AT, 4)
    FC = 2
    NGRP = D_FF // P // FC
    NU = FC * NT
    ND = KD * NT
    up_raw = k.at(f"{name}_up_raw", WT_AT, [P, KD, 2, P])
    up_hi = [k.at(f"{name}_up_hi{j}", WT_AT + (8 + 16 * j) * KB, [P, KD, 2, P], F32R) for j in range(FC)]
    up_lo = [k.at(f"{name}_up_lo{j}", WT_AT + (16 + 16 * j) * KB, [P, KD, 2, P], F32R) for j in range(FC)]
    dn_raw = k.at(f"{name}_dn_raw", WT_AT + 40 * KB, [P, FC, D])
    dn_hi = k.at(f"{name}_dn_hi", WT_AT + 48 * KB, [P, FC, D], F32R)
    dn_lo = k.at(f"{name}_dn_lo", WT_AT + 56 * KB, [P, FC, D], F32R)
    a_hi = k.at(f"{name}_a_hi", ACT_AT, [P, FC, T], F32R)
    a_lo = k.at(f"{name}_a_lo", ACT_AT + 2 * TB, [P, FC, T], F32R)
    silu = [k.at(f"{name}_silu{j}", TMP_AT + SLOT * j, [P, TW]) for j in range(2)]
    prod = [k.at(f"{name}_prod{j}", TMP_AT + SLOT * (2 + j), [P, TW]) for j in range(2)]
    scratch = k.at(f"{name}_scratch", TMP_AT + 4 * SLOT, [P, 2, NS_TOK])
    up_in, up_hi_done, up_lo_done = (k.sem(f"{name}_{n}") for n in ("up_in", "up_hi_done", "up_lo_done"))
    dn_in, dn_hi_done, dn_lo_done = (k.sem(f"{name}_{n}") for n in ("dn_in", "dn_hi_done", "dn_lo_done"))
    gate_mm, up_mm, gate_free, up_free = (k.sem(f"{name}_{n}") for n in ("gate_mm", "up_mm", "gate_free", "up_free"))
    act_done, dn_mm, dn_free = (k.sem(f"{name}_{n}") for n in ("act_done", "dn_mm", "dn_free"))
    gu = w_gu[0].rearrange("(k p) (h f n) -> p f k h n", p=P, h=2, n=P)
    dn = w_down[0].rearrange("(g c p) n -> p g c n", p=P, c=FC)

    with nc.Block() as block:
        @block.sync
        def _(sp):
            def load_up(f):
                for h in range(2):
                    sp.dma_start(up_raw[:, :, h, :], gu[:, f, :, h].rearrange("p o k n -> p (o k) n") if not isinstance(f, int)
                                 else gu[:, f, :, h]).then_inc(up_in, 16)

            sp.dma_start(dn_raw[:], dn[:, 0]).then_inc(dn_in, 16)
            load_up(0)
            sp.wait_ge(up_lo_done, 1)
            load_up(1)
            with sp.Fori(0, NGRP - 1) as g:
                for j in range(FC):
                    sp.wait_ge(up_lo_done, FC * g + j + 2)
                    load_up(bass.ds(FC * g + FC + j, 1))
                sp.wait_ge(dn_lo_done, g + 1)
                sp.dma_start(dn_raw[:], dn[:, bass.ds(g + 1, 1)].rearrange("p o c n -> p (o c) n")).then_inc(dn_in, 16)

        @block.gpsimd
        def _(pool):
            def up_tail(j, count):
                pool.wait_ge(up_hi_done, count)
                pool.tensor_tensor(up_lo[j][:], up_raw[:], up_hi[j][:].bitcast(F32), ALU.subtract
                                   ).then_inc(up_lo_done, 1)

            def dn_tail(count):
                pool.wait_ge(dn_hi_done, count)
                pool.tensor_tensor(dn_lo[:], dn_raw[:], dn_hi[:].bitcast(F32), ALU.subtract).then_inc(dn_lo_done, 1)

            up_tail(0, 1)
            up_tail(1, 2)
            dn_tail(1)
            with pool.Fori(0, NGRP - 1) as g:
                up_tail(0, FC * g + 3)
                up_tail(1, FC * g + 4)
                dn_tail(g + 2)

        @block.tensor
        def _(pe):
            def group(g):
                for j in range(FC):
                    pe.wait_ge(up_lo_done, FC * g + j + 1)
                    for t, (a, n) in enumerate(TILES):
                        u = NT * j + t
                        if isinstance(g, int) and j == 0:
                            norm.pe_ready(pe, t)
                        for h, (free, done) in enumerate(((gate_free, gate_mm), (up_free, up_mm))):
                            pe.wait_ge(free, NU * g + u + 1)
                            three_passes(pe, k.psum[2 * (u % 2) + h][:, 0:n],
                                         [(up_hi[j][:, c, h, :], up_lo[j][:, c, h, :], k.hh[:, c, a:a + n],
                                           k.hl[:, c, a:a + n]) for c in range(KD)]).then_inc(done, 1)
                pe.wait_ge(dn_lo_done, g + 1)
                for t, (a, n) in enumerate(TILES):
                    pe.wait_ge(act_done, NU * g + NT * (FC - 1) + t + 1)
                    for c in range(KD):
                        v = KD * t + c
                        pe.wait_ge(dn_free, ND * g + v + 1)
                        three_passes(pe, k.psum[4 + v % 4][:, 0:n],
                                     [(dn_hi[:, f, P * c:P * c + P], dn_lo[:, f, P * c:P * c + P],
                                       a_hi[:, f, a:a + n], a_lo[:, f, a:a + n]) for f in range(FC)]
                                     ).then_inc(dn_mm, 1)

            norm.pe(pe)
            group(0)
            with pe.Fori(1, NGRP) as g:
                group(g)

        @block.scalar
        def _(act):
            act.sem_inc(gate_free, 2)
            norm.act(act)
            norm.wait_all(act)
            with act.Fori(0, NGRP) as g:
                for u in range(NU):
                    n = TILES[u % NT][1]
                    act.wait_ge(gate_mm, NU * g + u + 1)
                    act.wait_ge(up_free, NU * g + u + 1)
                    act.activation(silu[u % 2][:, 0:n], k.psum[2 * (u % 2)][:, 0:n], ACT.Silu).then_inc(gate_free, 1)

        @block.vector
        def _(dve):
            def up_head(j, count, used):
                dve.wait_ge(up_in, 32 * count)
                if used is not None:
                    dve.wait_ge(up_mm, used)
                dve.tensor_copy(up_hi[j][:], up_raw[:]).then_inc(up_hi_done, 1)

            def dn_head(count, used):
                dve.wait_ge(dn_in, 16 * count)
                if used is not None:
                    dve.wait_ge(dn_mm, used)
                dve.tensor_copy(dn_hi[:], dn_raw[:]).then_inc(dn_hi_done, 1)

            def group(g, last):
                for j in range(FC):
                    for t, (a, n) in enumerate(TILES):
                        u = NT * j + t
                        dve.wait_ge(gate_free, NU * g + u + 3)
                        dve.wait_ge(up_mm, NU * g + u + 1)
                        dve.tensor_tensor(prod[u % 2][:, 0:n], silu[u % 2][:, 0:n], k.psum[2 * (u % 2) + 1][:, 0:n],
                                          ALU.mult).then_inc(up_free, 1)
                        dve.drain()
                        dve.tensor_copy(a_hi[:, j, a:a + n], prod[u % 2][:, 0:n])
                        dve.drain()
                        dve.tensor_tensor(a_lo[:, j, a:a + n], prod[u % 2][:, 0:n], a_hi[:, j, a:a + n].bitcast(F32),
                                          ALU.subtract).then_inc(act_done, 1)
                    if not last:
                        up_head(j, FC * g + FC + j + 1, NU * g + NT * (j + 1))
                for v in range(ND):
                    t, c = v // KD, v % KD
                    dve.wait_ge(dn_mm, ND * g + v + 1)
                    add_gated(dve, k, i_gate, c, t, k.psum[4 + v % 4], scratch[:, v % 2]).then_inc(dn_free, 1)
                if not last:
                    dn_head(g + 2, ND * g + ND)

            dve.sem_inc(dn_free, 4)
            dve.sem_inc(up_free, 2)
            up_head(0, 1, None)
            dn_head(1, None)
            norm.dve(dve, 0)
            up_head(1, 2, None)
            norm.dve(dve, 1)
            norm.dve(dve, 2)
            norm.wait_all(dve)
            with dve.Fori(0, NGRP - 1) as g:
                group(g, False)
            group(NGRP - 1, True)


def each(eng, n, body, base):
    if n == 1:
        body(base, 0)
        return
    with eng.Fori(0, n) as i:
        body(i + base, i)


def stream_product(k, name, at, sections, rhs_hi, rhs_lo, evac_on_act, norm=None, split=None):
    raw = [k.at(f"{name}_raw{j}", at + 4 * KB * j, [P, KD, P]) for j in range(2)]
    hi = [k.at(f"{name}_hi{j}", at + 4 * KB * (2 + j), [P, KD, P], F32R) for j in range(2)]
    lo = [k.at(f"{name}_lo{j}", at + 4 * KB * (4 + j), [P, KD, P], F32R) for j in range(2)]
    raw_in = [k.sem(f"{name}_raw_in{j}") for j in range(2)]
    hi_done, lo_done, mm_done, bank_free = (k.sem(f"{name}_{n}") for n in ("hi_done", "lo_done", "mm_done", "bank_free"))
    dmas = sections[0][1](None, None, 0, 0, None)
    spilled = k.sem(f"{name}_spilled") if norm is not None else None

    def run(eng, body, after_first=None):
        base = 0
        for n, load, evac in sections:
            each(eng, n, lambda g, i: body(g, i, load, evac), base)
            if base == 0 and after_first is not None:
                after_first()
            base += n

    def norm_tiles(dve):
        for t in range(NT):
            norm.dve(dve, t)

    def heads(eng):
        def body(g, i, load, evac):
            for j in range(2):
                eng.wait_ge(raw_in[j], 16 * dmas * (g + 1))
                eng.wait_ge(mm_done, 6 * g + 3 * j + 3)
                copy = eng.copy if evac_on_act is False else eng.tensor_copy
                copy(hi[j][:], raw[j][:]).then_inc(hi_done, 1)
        run(eng, body, lambda: norm_tiles(eng) if norm is not None else split.restore_x(eng))

    def evacs(eng):
        eng.sem_inc(bank_free, 6)
        if norm is not None:
            norm.act(eng)
            norm.wait_all(eng)
            eng.wait_ge(spilled, 16)
        if split is not None:
            split.dve(eng)
            eng.wait_ge(split.x_back, 16)

        def body(g, i, load, evac):
            for j in range(2):
                for t in range(NT):
                    eng.wait_ge(mm_done, 6 * g + 3 * j + t + 7)
                    evac(eng, i, j, t, k.psum[3 * j + t]).then_inc(bank_free, 1)
        run(eng, body)

    with k.nc.Block() as block:
        @block.sync
        def _(sp):
            def body(g, i, load, evac):
                for j in range(2):
                    sp.wait_ge(lo_done, 2 * g + j + 1)
                    load(sp, raw[j], i, j, raw_in[j])
            run(sp, body)

        @block.gpsimd
        def _(pool):
            pool.sem_inc(lo_done, 2)
            if norm is not None:
                pool.dma_start(k.dram["x_spill"], k.x[:]).then_inc(spilled, 16)

            def body(g, i, load, evac):
                for j in range(2):
                    pool.wait_ge(hi_done, 2 * g + j + 1)
                    pool.tensor_tensor(lo[j][:], raw[j][:], hi[j][:].bitcast(F32), ALU.subtract).then_inc(lo_done, 1)
            run(pool, body, None if split is None else lambda: split.pool(pool))

        @block.tensor
        def _(pe):
            pe.sem_inc(mm_done, 6)
            if norm is not None:
                norm.pe(pe)

            def body(g, i, load, evac):
                for j in range(2):
                    pe.wait_ge(lo_done, 2 * g + j + 3)
                    for t, (a, n) in enumerate(TILES):
                        if isinstance(g, int) and g == 0 and j == 0:
                            (norm or split).pe_ready(pe, t)
                        pe.wait_ge(bank_free, 6 * g + 3 * j + t + 1)
                        three_passes(pe, k.psum[3 * j + t][:, 0:n],
                                     [(hi[j][:, c], lo[j][:, c], rhs_hi[:, c, a:a + n], rhs_lo[:, c, a:a + n])
                                      for c in range(KD)]).then_inc(mm_done, 1)
            run(pe, body)

        @block.scalar
        def _(act):
            (evacs if evac_on_act else heads)(act)

        @block.vector
        def _(dve):
            (heads if evac_on_act else evacs)(dve)


QKV_AT = X_AT
R1_AT = X_AT + 6 * TB
U_AT = WT_AT
R2_AT = U_AT + 60 * KB
UB = W * 4


def input_projection(k):
    w = k.dram["w_in"][0]
    wu = w[:, 0:U_COLS].rearrange("(k p) (f n) -> p f k n", p=P, n=P)
    wq = w[:, U_COLS:U_COLS + RW].rearrange("(k p) (h c n) -> p c k h n", p=P, h=2, n=HD)
    wkv = w[:, U_COLS + RW:].rearrange("(k p) (f n) -> p f k n", p=P, n=P)

    def load_u(f0):
        def load(sp, raw, i, j, sem):
            if sp is not None:
                sp.dma_start(raw[:], wu[:, bass.ds(2 * i + f0 + j, 1)].rearrange("p o k n -> p (o k) n")).then_inc(sem, 32)
            return 2
        return load

    def load_q(sp, raw, i, j, sem):
        for h in range(2):
            sp.dma_start(raw[:, :, HD * h:HD * h + HD],
                         wq[:, bass.ds(2 * i + j, 1), :, h].rearrange("p o k n -> p (o k) n")).then_inc(sem, 16)
        return 2

    def load_kv(sp, raw, i, j, sem):
        sp.dma_start(raw[:], wkv[:, j]).then_inc(sem, 32)
        return 2

    def evac_u(f0):
        def evac(act, i, j, t, bank):
            a, n = TILES[t]
            np_ = min(n, NP_TOK - a)
            row = k.u[:, bass.ds(2 * i + f0 + j, 1), :].rearrange("p o n -> p (o n)")
            ins = act.copy(row[:, 1 + a:1 + a + np_], bank[:, 0:np_])
            if np_ < n:
                ins = act.copy(row[:, 1 + NP_TOK:UW].rearrange("p (s t) -> p s t", t=TSEQ + 1)[:, :, 1:],
                               per_seq(bank[:, np_:n]))
            return ins
        return evac

    def evac_qkv(c0):
        def evac(act, i, j, t, bank):
            a, n = TILES[t]
            f = c0 + 2 * i + j
            dst = k.qkv[:, f, a:a + n] if isinstance(f, int) else \
                k.qkv[:, bass.ds(f, 1), a:a + n].rearrange("p o n -> p (o n)")
            return act.copy(dst, bank[:, 0:n])
        return evac

    stream_product(k, "w_in", R2_AT, [(1, load_u(0), evac_u(0)), (UC // 2 - 1, load_u(2), evac_u(2)), (2, load_q, evac_qkv(0)), (1, load_kv, evac_qkv(4))],
                   k.hh, k.hl, True, Norm(k, "mix", 3, U_AT, 0))


def attention_prepare(k):
    d = k.dram
    o = R1_AT
    k.cos, k.sin = k.at("cos", o, [P, T]), k.at("sin", o + TB, [P, T])
    o += 2 * TB
    k.k_bd = k.at("k_bd", o, [P, 2, WINDOW + NP_TOK]); o += 9216
    k.v_tok = k.at("v_tok", o, [P, 9, 2, 3 * HD]); o += 13824
    tmp = [k.at(f"rope_tmp{j}", o + TB * j, [P, T]) for j in range(2)]
    k.scrap = o
    o += 2 * TB
    k.q_now = k.at("q_now", o, [P, 4, P]); o += 2048
    k.v_now = k.at("v_now", o, [P, 2, 2, 3 * HD]); o += 3072
    k.prob = k.at("prob", o, [P, 4, 2, 2 * WINDOW]); o += 8192
    k.diag = k.at("diag", o, [P, 8, P]); o += 4096
    k.probT = [k.at(f"probT{j}", o + 2048 * j, [P, 4, P]) for j in range(2)]; o += 4096
    k.v_new = k.at("v_new", o, [P, NSEQ, 2, 3 * HD]); o += 12288
    k.prob_s = k.at("prob_s", o, [P, 2, 2, WINDOW + TSEQ]); o += 2176
    small_at = o
    o = R2_AT
    k.ks_bd = k.at("ks_bd", o, [P, NSEQ, 2, WINDOW + TSEQ]); o += 8704
    k.q_pad = k.at("q_pad", o, [P, NSEQ, P]); o += 4096
    k.kc = k.at("kc", o, [P, NSEQ, P]); o += 4096
    k.v_cache = k.at("v_cache", o, [P, NSEQ, 2, 3 * HD]); o += 12288
    assert o <= END
    o = small_at
    small = k.at("small", o, [P, 64]); o += 256
    k.small = small
    k.k_rows = k.at("k_rows", o, [P, 2, P]); o += 1024
    k.sink_row = k.at("sink_row", o, [1, 8]); o += 32
    k.sink4 = k.at("sink4", o, [4, 2]); o += 32
    k.sink_p = k.at("sink_p", o, [P, 4, 2]); o += 32
    k.sink_s = k.at("sink_s", o, [P, 2]); o += 32
    assert o <= X_AT + KD * TB * 3, o
    tab_in, cache_in, sink_in = k.sem("tab_in"), k.sem("cache_in"), k.sem("sink_in")
    zeroed, rot_mm, rot_used, roped, turned, turn_used, rows_done, cache_out = (
        k.sem(n) for n in ("zeroed", "rot_mm", "rot_used", "roped", "turned", "turn_used", "rows_done", "cache_out"))
    k.cache_out = cache_out

    with k.nc.Block() as block:
        @block.sync
        def _(sp):
            sp.dma_start(k.cos[:], d["cos"]).then_inc(tab_in, 16)
            sp.dma_start(k.sin[:], d["sin"]).then_inc(tab_in, 16)
            sinks = d["attn_sinks"]
            sp.dma_start(k.sink_row[:], sinks).then_inc(sink_in, 16)
            for h in range(2):
                sp.dma_start(k.sink4[:, h:h + 1], sinks[:, 4 * h:4 * h + 4].rearrange("o c -> c o")).then_inc(sink_in, 16)
            sp.dma_start(k.kc[:], d["cache_k"][0].rearrange("s w h n -> w s (h n)")).then_inc(cache_in, 16)
            sp.wait_ge(zeroed, 4)
            for h in range(2):
                sp.dma_start(k.v_cache[:, :, h, HD:2 * HD], d["cache_v"][0, :, :, h].rearrange("s w n -> w s n")
                             ).then_inc(cache_in, 16)
            for src, dst in (("cache_k", "sample_k"), ("cache_v", "sample_v")):
                sp.dma_start(d[dst][0, :, 0:WINDOW - TSEQ].rearrange("s w h n -> s (w h n)"),
                             d[src][0, :, TSEQ:WINDOW].rearrange("s w h n -> s (w h n)")).then_inc(cache_out, 16)
            sp.wait_ge(rows_done, 1)
            sp.dma_start(d["prompt_k"][0, 0].rearrange("w h n -> w (h n)"), k.k_rows[:, 0]).then_inc(cache_out, 16)
            for s in range(NSEQ):
                sp.dma_start(d["sample_k"][0, s, WINDOW - TSEQ:WINDOW].rearrange("w h n -> w (h n)"),
                             k.k_rows[TSEQ * s:TSEQ * s + TSEQ, 1]).then_inc(cache_out, 16)
            sp.wait_ge(turn_used, 6)
            sp.dma_start(d["prompt_v"][0, 0], k.v_tok[:, 8, :, HD:2 * HD]).then_inc(cache_out, 16)
            for h in range(2):
                sp.dma_start(d["sample_v"][0, :, WINDOW - TSEQ:WINDOW, h].rearrange("s w n -> w s n"),
                             k.v_new[0:TSEQ, :, h, HD:2 * HD]).then_inc(cache_out, 16)
            k.n_cache_out = 2 + 1 + NSEQ + 1 + 2

        @block.gpsimd
        def _(pool):
            for t in (k.v_cache, k.k_bd, k.v_tok, k.v_new):
                pool.memset(t[:], 0.0).then_inc(zeroed, 1)
            for t in (k.ks_bd, k.q_pad):
                pool.memset(t[:], 0.0).then_inc(zeroed, 1)

        @block.tensor
        def _(pe):
            for c in range(5):
                if c >= 2:
                    pe.wait_ge(rot_used, c - 1)
                for t, (a, n) in enumerate(TILES):
                    ins = pe.matmul(k.psum[3 * (c % 2) + t][:, 0:n], k.c("rot"), k.qkv[:, c, a:a + n], start=True, stop=True)
                ins.then_inc(rot_mm, 1)
            ident = k.c("ident")
            for g in range(2):
                for b in range(4):
                    ins = pe.transpose(k.psum[6 + g][:, P * b:P * b + P],
                                       k.qkv[:, 5, P * (4 * g + b):P * (4 * g + b) + P], ident)
                ins.then_inc(turned, 1)
            pe.wait_ge(rot_used, 4)
            for g in range(2):
                for b in range(4):
                    at = NP_TOK + TSEQ * (4 * g + b)
                    ins = pe.transpose(k.psum[3 + g][0:TSEQ, P * b:P * b + P], k.qkv[:, 5, at:at + TSEQ], ident)
                ins.then_inc(turned, 1)
            pe.wait_ge(roped, 5)
            pe.transpose(k.psum[5][:, 0:P], k.qkv[:, 4, NP_TOK - P:NP_TOK], ident)
            pe.transpose(k.psum[5][0:NS_TOK, P:2 * P], k.qkv[:, 4, NP_TOK:T], ident)
            pe.wait_ge(sink_in, 48)
            pe.matmul(k.psum[5][:, 256:264], k.c("ones")[0:1, :], k.sink_row[:], start=True, stop=True)
            pe.matmul(k.psum[5][:, 264:266], k.c("row_chunk")[0:4, :], k.sink4[:], start=True, stop=True).then_inc(turned, 1)
            pe.wait_ge(cache_in, 48)
            pe.wait_ge(turn_used, 2)
            for g in range(2):
                for b in range(4):
                    ins = pe.transpose(k.psum[6 + g][:, P * b:P * b + P], k.kc[:, 4 * g + b], ident)
                ins.then_inc(turned, 1)

        @block.vector
        def _(dve):
            dve.wait_ge(tab_in, 32)
            for c in range(5):
                dve.wait_ge(rot_mm, c + 1)
                for t, (a, n) in enumerate(TILES):
                    ins = dve.tensor_tensor(tmp[c % 2][:, a:a + n], k.psum[3 * (c % 2) + t][:, 0:n], k.sin[:, a:a + n],
                                            ALU.mult)
                ins.then_inc(rot_used, 1)
                dve.tensor_tensor(k.qkv[:, c, :], k.qkv[:, c, :], k.cos[:], ALU.mult)
                dve.drain()
                dve.tensor_tensor(k.qkv[:, c, :], k.qkv[:, c, :], tmp[c % 2][:], ALU.add).then_inc(roped, 1)
                dve.drain()
            dve.wait_ge(zeroed, 6)
            for h in range(2):
                r = slice(HD * h, HD * h + HD)
                dve.tensor_copy(k.k_bd[r, h, WINDOW:], k.qkv[r, 4, 0:NP_TOK])
                dve.tensor_copy(k.ks_bd[r, :, h, WINDOW:], per_seq(k.qkv[r, 4, NP_TOK:T]))
            for s in range(NSEQ):
                dve.tensor_copy(k.q_pad[:, s, 32 * (s % 4):32 * (s % 4) + 32].rearrange("p (c t) -> p c t", t=TSEQ),
                                k.qkv[:, 0:4, NP_TOK + TSEQ * s:NP_TOK + TSEQ * s + TSEQ])

        @block.scalar
        def _(act):
            act.wait_ge(zeroed, 4)
            for g in range(2):
                act.wait_ge(turned, g + 1)
                act.copy(k.v_tok[:, 1 + 4 * g:5 + 4 * g, :, HD:2 * HD],
                         k.psum[6 + g][:].rearrange("p (b h n) -> p b h n", b=4, h=2)).then_inc(turn_used, 1)
            for g in range(2):
                act.wait_ge(turned, g + 3)
                act.copy(k.v_new[0:TSEQ, 4 * g:4 * g + 4, :, HD:2 * HD],
                         k.psum[3 + g][0:TSEQ, :].rearrange("p (b h n) -> p b h n", b=4, h=2)).then_inc(turn_used, 1)
            act.wait_ge(turned, 5)
            act.copy(k.sink_p[:], k.psum[5][:, 256:264].rearrange("p (h c) -> p c h", h=2)).then_inc(turn_used, 1)
            act.copy(k.sink_s[:], k.psum[5][:, 264:266]).then_inc(turn_used, 1)
            act.copy(k.k_rows[:, 0], k.psum[5][:, 0:P])
            act.copy(k.k_rows[0:NS_TOK, 1], k.psum[5][0:NS_TOK, P:2 * P])
            act.drain().then_inc(rows_done, 1)
            act.wait_ge(zeroed, 6)
            for g in range(2):
                act.wait_ge(turned, g + 6)
                for h in range(2):
                    r = slice(HD * h, HD * h + HD)
                    act.copy(k.ks_bd[r, 4 * g:4 * g + 4, h, 0:WINDOW],
                             k.psum[6 + g][r, :].rearrange("p (b n) -> p b n", b=4))


def attention_prompt(k):
    NB = NP_TOK // WINDOW
    prob = [k.prob, k.at("prob1", R1_AT, [P, 4, 2, 2 * WINDOW])]
    diag = [k.diag, k.at("diag1", k.scrap, [P, 8, P])]
    q_now = [k.q_now, k.at("q_now1", k.scrap + 4096, [P, 4, P])]
    small = [k.small, k.at("small1", R1_AT + 8192, [P, 24])]
    mx, sums, es = ([t[:, 8 * i:8 * i + 8] for t in small] for i in range(3))
    q_copied, v_copied, s_mm, s_used, max_done, exp_done, diag_done, pt_mm, pt_used, o_mm, o_used = (
        k.sem(f"att_{n}") for n in ("q_copied", "v_copied", "s_mm", "s_used", "max_done", "exp_done", "diag_done",
                                    "pt_mm", "pt_used", "o_mm", "o_used"))

    def over_heads(ap):
        return ap.unsqueeze(1).broadcast_to([P, 2, 2 * WINDOW])

    def steps(eng, body):
        with eng.Fori(0, NB // 2 - 1) as i:
            for j in range(2):
                body(2 * i + j, j, True)
        body(NB - 2, 0, True)
        body(NB - 1, 1, False)

    with k.nc.Block() as block:
        @block.gpsimd
        def _(pool):
            def copy_q(b, j):
                pool.tensor_copy(q_now[j][:], k.qkv[:, 0:4, bass.ds(WINDOW * b, WINDOW)]).then_inc(q_copied, 1)

            def step(n, j, more):
                if not (isinstance(n, int) and n + 2 >= NB):
                    pool.wait_ge(s_mm, 4 * n + 8)
                    copy_q(n + 2, j)
                pool.wait_ge(o_mm, n + 1)
                pool.tensor_copy(k.v_now[:], k.v_tok[:, bass.ds(n, 2)]).then_inc(v_copied, 1)

            copy_q(0, 0)
            copy_q(1, 1)
            steps(pool, step)

        @block.tensor
        def _(pe):
            def scores(b, j):
                pe.wait_ge(q_copied, b + 1)
                for c in range(4):
                    pe.wait_ge(s_used, 4 * b + c + 1)
                    pe.matmul(k.psum[c][:].rearrange("p (h n) -> p h n", h=2), q_now[j][:, c],
                              k.k_bd[:, :, bass.ds(WINDOW * b, 2 * WINDOW)], start=True, stop=True).then_inc(s_mm, 1)

            def weighted(b, c):
                pe.wait_ge(pt_used, 4 * b + c + 3)
                for n in range(4):
                    h, w = n // 2, n % 2
                    ins = pe.matmul(k.psum[6][:, P * c:P * c + P], k.v_now[:, w, h, HD * (1 - h):HD * (1 - h) + P],
                                    k.probT[c % 2][:, n], start=(n == 0), stop=(n == 3))
                return ins

            def step(n, j, more):
                if more:
                    scores(n + 1, 1 - j)
                pe.wait_ge(diag_done, n + 1)
                pe.wait_ge(v_copied, n + 1)
                for c in range(4):
                    pe.wait_ge(pt_used, 4 * n + c + 1)
                    for i in range(4):
                        h, w = i // 2, i % 2
                        ins = pe.matmul(k.psum[4 + c % 2][:, P * i:P * i + P],
                                        prob[j][:, c, h, P * w:P * w + P], diag[j][:, 2 * c + h], start=True, stop=True)
                    ins.then_inc(pt_mm, 1)
                    if c == 0:
                        pe.wait_ge(o_used, n + 1)
                    if c >= 1:
                        weighted(n, c - 1)
                weighted(n, 3).then_inc(o_mm, 1)

            pe.sem_inc(s_mm, 4)
            pe.sem_inc(o_mm, 1)
            scores(0, 0)
            steps(pe, step)

        @block.vector
        def _(dve):
            sink = k.sink_p[:].rearrange("p c h -> p (c h)")

            def scores(b, j, mask):
                for c in range(4):
                    dve.wait_ge(s_mm, 4 * b + c + 5)
                    if c == 0 and not (isinstance(b, int) and b == 0):
                        dve.wait_ge(o_mm, b)
                    dve.scalar_tensor_tensor(prob[j][:, c], k.psum[c][:].rearrange("p (h n) -> p h n", h=2),
                                             HD ** -0.5, over_heads(k.c(mask)), ALU.mult, ALU.add).then_inc(s_used, 1)
                dve.drain()
                dve.tensor_reduce(mx[j], prob[j][:].rearrange("p c h n -> p (c h) n"), AX.X, ALU.max)
                dve.drain()
                dve.tensor_tensor(mx[j], mx[j], sink, ALU.max)
                dve.drain()
                dve.tensor_tensor(es[j], sink, mx[j], ALU.subtract)
                dve.tensor_scalar(mx[j], mx[j], -1.0, None, ALU.mult).then_inc(max_done, 1)

            def step(n, j, more):
                dve.wait_ge(exp_done, n + 1)
                dve.tensor_tensor(sums[j], sums[j], es[j], ALU.add)
                dve.drain()
                dve.reciprocal(sums[j], sums[j])
                dve.drain()
                for i in range(8):
                    ins = dve.tensor_scalar(diag[j][:, i], k.c("ident"), sums[j][:, i:i + 1], None, ALU.mult)
                ins.then_inc(diag_done, 1)
                if more:
                    scores(n + 1, 1 - j, "mask_p")

            dve.sem_inc(s_used, 4)
            scores(0, 0, "mask_p0")
            steps(dve, step)

        @block.scalar
        def _(act):
            def exps(j, first, n):
                for i in range(first, first + n):
                    act.activation(prob[j][:, i // 2, i % 2], prob[j][:, i // 2, i % 2], ACT.Exp, bias=mx[j][:, i:i + 1],
                                   accum_out=sums[j][:, i:i + 1])

            def exp_sinks(j):
                act.activation(es[j], es[j], ACT.Exp)
                act.drain().then_inc(exp_done, 1)

            def step(n, j, more):
                for c in range(4):
                    act.wait_ge(pt_mm, 4 * n + c + 1)
                    act.copy(k.probT[c % 2][:].rearrange("p c n -> p (c n)"), k.psum[4 + c % 2][:]).then_inc(pt_used, 1)
                    if more and c >= 1:
                        if c == 1:
                            act.wait_ge(max_done, n + 2)
                        exps(1 - j, 3 * (c - 1), 3 if c < 3 else 2)
                act.wait_ge(o_mm, n + 2)
                act.copy(k.qkv[:, 0:4, bass.ds(WINDOW * n, WINDOW)], k.psum[6][:].rearrange("p (c n) -> p c n", c=4)
                         ).then_inc(o_used, 1)
                if more:
                    exp_sinks(1 - j)

            act.sem_inc(pt_used, 2)
            act.sem_inc(o_used, 1)
            act.wait_ge(max_done, 1)
            exps(0, 0, 8)
            exp_sinks(0)
            steps(act, step)


def attention_sample(k):
    mx, sums, es = (k.small[:, 24 + 4 * i:28 + 4 * i] for i in range(3))
    s_mm, max_done, exp_done, diag_done, pt_mm, pt_used, o_mm = (
        k.sem(f"ats_{n}") for n in ("s_mm", "max_done", "exp_done", "diag_done", "pt_mm", "pt_used", "o_mm"))
    NK = WINDOW + TSEQ
    with k.nc.Block() as block:
        @block.tensor
        def _(pe):
            for g in range(2):
                for b in range(4):
                    ins = pe.matmul(k.psum[g][:, 0:2 * NK], k.q_pad[:, 4 * g + b],
                                    k.ks_bd[:, 4 * g + b].rearrange("p h n -> p (h n)"), start=(b == 0), stop=(b == 3))
                ins.then_inc(s_mm, 1)
            pe.wait_ge(diag_done, 1)
            for g in range(2):
                for h in range(2):
                    i = 2 * g + h
                    pe.matmul(k.psum[2][:, P * i:P * i + P], k.prob_s[:, g, h, 0:WINDOW], k.diag[:, i], start=True, stop=True)
                    ins = pe.matmul(k.psum[3][0:TSEQ, P * i:P * i + P], k.prob_s[:, g, h, WINDOW:NK], k.diag[:, i],
                                    start=True, stop=True)
            ins.then_inc(pt_mm, 1)
            pe.wait_ge(pt_used, 2)
            for s in range(NSEQ):
                for h in range(2):
                    i, col, pad = 2 * (s // 4) + h, 32 * (s % 4), HD * (1 - h)
                    pe.matmul(k.psum[4][:, 32 * s:32 * s + 32], k.v_cache[:, s, h, pad:pad + P],
                              k.probT[0][:, i, col:col + 32], start=(h == 0), stop=False)
                    ins = pe.matmul(k.psum[4][:, 32 * s:32 * s + 32], k.v_new[0:TSEQ, s, h, pad:pad + P],
                                    k.probT[1][0:TSEQ, i, col:col + 32], start=False, stop=(h == 1))
            ins.then_inc(o_mm, 1)

        @block.vector
        def _(dve):
            for g in range(2):
                dve.wait_ge(s_mm, g + 1)
                dve.scalar_tensor_tensor(k.prob_s[:, g], k.psum[g][:, 0:2 * NK].rearrange("p (h n) -> p h n", h=2), HD ** -0.5,
                                         k.c("mask_s").unsqueeze(1).broadcast_to([P, 2, NK]), ALU.mult, ALU.add)
            dve.drain()
            dve.tensor_reduce(mx, k.prob_s[:].rearrange("p g h n -> p (g h) n"), AX.X, ALU.max)
            dve.drain()
            sink = k.sink_s[:].unsqueeze(1).broadcast_to([P, 2, 2])
            mx3, es3 = (a.rearrange("p (g h) -> p g h", g=2) for a in (mx, es))
            dve.tensor_tensor(mx3, mx3, sink, ALU.max)
            dve.drain()
            dve.tensor_tensor(es3, sink, mx3, ALU.subtract)
            dve.tensor_scalar(mx, mx, -1.0, None, ALU.mult).then_inc(max_done, 1)
            dve.wait_ge(exp_done, 1)
            dve.tensor_tensor(sums, sums, es, ALU.add)
            dve.drain()
            dve.reciprocal(sums, sums)
            dve.drain()
            for i in range(4):
                ins = dve.tensor_scalar(k.diag[:, i], k.c("ident"), sums[:, i:i + 1], None, ALU.mult)
            ins.then_inc(diag_done, 1)
            dve.wait_ge(o_mm, 1)
            for c in range(4):
                dve.tensor_copy(per_seq(k.qkv[:, c, NP_TOK:T]),
                                k.psum[4][:, 0:32 * NSEQ].rearrange("p (s c t) -> p c s t", s=NSEQ, c=4)[:, c])

        @block.scalar
        def _(act):
            act.wait_ge(max_done, 1)
            for i in range(4):
                act.activation(k.prob_s[:, i // 2, i % 2], k.prob_s[:, i // 2, i % 2], ACT.Exp, bias=mx[:, i:i + 1],
                               accum_out=sums[:, i:i + 1])
            act.activation(es, es, ACT.Exp)
            act.drain().then_inc(exp_done, 1)
            act.wait_ge(pt_mm, 1)
            act.copy(k.probT[0][:].rearrange("p c n -> p (c n)"), k.psum[2][:]).then_inc(pt_used, 1)
            act.copy(k.probT[1][0:TSEQ].rearrange("p c n -> p (c n)"), k.psum[3][0:TSEQ, :]).then_inc(pt_used, 1)


UTILES = [(0, 366), (366, 366), (732, 364)]


def u_tok(ap):
    return ap[:, NP_TOK:W].rearrange("p (s t) -> p s t", t=TSEQ + 1)[:, :, 1:]


def rwkv_shift(k):
    d = k.dram
    k.dec = k.at("dec", R1_AT, [P, PAIRS, W])
    k.bb = k.at("bb", R1_AT + PAIRS * UB, [P, PAIRS, W])
    k.aa = k.at("aa", R1_AT + 2 * PAIRS * UB, [P, PAIRS, W])
    k.bon = k.at("bon", R1_AT + 3 * PAIRS * UB, [P, PAIRS, W])
    o = R2_AT
    diff = [k.at(f"diff{j}", o + UB * j, [P, W]) for j in range(2)]
    tz = k.at("tz", o + 2 * UB, [P, W])
    o += 3 * UB
    w2 = k.at("w2", o, [P, RW]); o += 2048
    a2 = k.at("a2", o, [P, RW]); o += 2048
    shift_rows = k.at("shift_rows", o, [P, P]); o += 512
    last = k.at("last", o, [P, 9, UC]); o += 512
    last_rows = k.at("last_rows", o, [P, P]); o += 512
    NR = NSEQ * UC
    zero2, lora_in, rows_in, out_done, prev_mm, u_full, last_done, last_mm, lastT_done, diff_done, z_done = (
        k.sem(f"sh_{n}") for n in ("zero2", "lora_in", "rows_in", "out_done", "prev_mm", "u_full", "last_done",
                                   "last_mm", "lastT_done", "diff_done", "z_done"))
    tz_done, lora_mm, lora_free = (k.sem(f"sh_{n}") for n in ("tz_done", "lora_mm", "lora_free"))
    order = [12, 13] + list(range(12))

    with k.nc.Block() as block:
        @block.sync
        def _(sp):
            sp.dma_start(shift_rows[0:NR, :], d["state_shift"][0].rearrange("s (c p) -> (s c) p", p=P)).then_inc(rows_in, 16)
            sp.wait_ge(zero2, 2)
            sp.dma_start(w2[0:HD, :], d["rwkv_w2"][0]).then_inc(lora_in, 16)
            sp.dma_start(a2[HD:P, :], d["rwkv_a2"][0]).then_inc(lora_in, 16)
            sp.wait_ge(lastT_done, 1)
            sp.dma_start(d["prompt_shift"][0].rearrange("o (c p) -> (o c) p", p=P), last_rows[0:UC, :]).then_inc(out_done, 16)
            sp.dma_start(d["sample_shift"][0].rearrange("s (c p) -> (s c) p", p=P), last_rows[UC:UC + NR, :]
                         ).then_inc(out_done, 16)
            sp.wait_ge(out_done, 32)

        @block.gpsimd
        def _(pool):
            pool.memset(w2[:], 0.0).then_inc(zero2, 1)
            pool.memset(a2[:], 0.0).then_inc(zero2, 1)
            pool.wait_ge(u_full, 1)
            for n, c in enumerate(order):
                if n >= 2:
                    pool.wait_ge(z_done, n - 1)
                pool.tensor_tensor(diff[n % 2][:], k.u[:, c, 0:W], k.u[:, c, 1:UW], ALU.subtract).then_inc(diff_done, 1)

        @block.vector
        def _(dve):
            dve.memset(k.u[:, :, 0:1], 0.0)
            dve.wait_ge(prev_mm, 1)
            dve.tensor_copy(k.u[:, :, 1 + NP_TOK::TSEQ + 1], k.psum[6][:, 0:NR].rearrange("p (s c) -> p c s", s=NSEQ))
            dve.tensor_copy(last[:, 0, :], k.u[:, :, NP_TOK])
            dve.tensor_copy(last[:, 1:9, :], k.u[:, :, 1 + NP_TOK + TSEQ::TSEQ + 1].rearrange("p c s -> p s c")
                            ).then_inc(last_done, 1)
            dve.drain().then_inc(u_full, 1)
            for n, c in enumerate(order):
                dve.wait_ge(diff_done, n + 1)
                dve.scalar_tensor_tensor(k.u[:, c, 1:UW], diff[n % 2][:], k.p2("mu_shift", c), k.u[:, c, 1:UW],
                                         ALU.mult, ALU.add).then_inc(z_done, 1)

        @block.tensor
        def _(pe):
            ident = k.c("ident")
            pe.wait_ge(rows_in, 16)
            pe.transpose(k.psum[6][:, 0:NR], shift_rows[0:NR, :], ident[0:NR, 0:NR]).then_inc(prev_mm, 1)
            pe.wait_ge(last_done, 1)
            pe.transpose(k.psum[7][0:9 * UC, 0:P], last[:].rearrange("p s c -> p (s c)"), ident).then_inc(last_mm, 1)
            pe.wait_ge(lora_in, 32)
            pe.wait_ge(tz_done, 1)
            for m in range(PAIRS):
                for h, w in enumerate((w2, a2)):
                    pe.wait_ge(lora_free, 2 * m + h + 1)
                    for t, (a, n) in enumerate(UTILES):
                        ins = pe.matmul(k.psum[3 * h + t][:, 0:n], w[:, P * m:P * m + P], tz[:, a:a + n],
                                        start=True, stop=True)
                    ins.then_inc(lora_mm, 1)

        @block.scalar
        def _(act):
            act.wait_ge(last_mm, 1)
            act.copy(last_rows[0:9 * UC, :], k.psum[7][0:9 * UC, 0:P]).then_inc(lastT_done, 1)
            act.sem_inc(lora_free, 2)
            act.wait_ge(z_done, 1)
            act.activation(tz[0:HD, :], k.u[0:HD, 12, 1:UW], ACT.Tanh)
            act.copy(tz[HD:P, :], k.u[HD:P, 12, 1:UW]).then_inc(tz_done, 1)
            act.wait_ge(z_done, 2)
            act.activation(k.u[:, 13, 1:UW], k.u[:, 13, 1:UW], ACT.Sigmoid)
            for m in range(PAIRS):
                for h, (dst, bias) in enumerate(((k.dec, "rwkv_w0"), (k.bb, "rwkv_a0"))):
                    act.wait_ge(lora_mm, 2 * m + h + 1)
                    for t, (a, n) in enumerate(UTILES):
                        ins = act.activation(dst[:, m, a:a + n], k.psum[3 * h + t][:, 0:n], ACT.Sigmoid, bias=k.p2(bias, m))
                    ins.then_inc(lora_free, 1)


def sums_to_rows(k, pe, bank, m, sq):
    for t, (a, n) in enumerate(UTILES):
        ins = pe.matmul(bank[32 * t:32 * t + 8, 0:n], k.c("to_rows")[:, 8 * m:8 * m + 8], sq[:, a:a + n],
                        start=(m == 0), stop=(m == PAIRS - 1))
    return ins


def rows_to_heads(k, pe, banks, m, rows):
    for t, (a, n) in enumerate(UTILES):
        r = slice(32 * t, 32 * t + 8)
        ins = pe.matmul(banks[t][:, 0:n], k.c("from_rows")[r, P * m:P * m + P], rows[r, 0:n], start=True, stop=True)
    return ins


def rwkv_keys(k):
    sq = [k.at(f"kk_sq{j}", R2_AT + UB * j, [P, W]) for j in range(2)]
    rows = k.at("kk_rows", R2_AT + 2 * UB, [P, 366])
    kk_done, sq_done, ss_mm, ss_done, root_done, inv_done, back_mm, back_used = (
        k.sem(f"kk_{n}") for n in ("kk_done", "sq_done", "ss_mm", "ss_done", "root_done", "inv_done", "back_mm", "back_used"))
    with k.nc.Block() as block:
        @block.vector
        def _(dve):
            for m in range(PAIRS):
                dve.tensor_scalar(k.aa[:, m], k.u[:, 4 + m, 1:UW], k.p2("rwkv_k_k", m), None, ALU.mult).then_inc(kk_done, 1)
            dve.memset(rows[:], 1.0)
            dve.drain()
            dve.wait_ge(ss_mm, PAIRS)
            for t, (a, n) in enumerate(UTILES):
                r = slice(32 * t, 32 * t + 8)
                ins = dve.tensor_scalar(rows[r, 0:n], k.psum[6][r, 0:n], 1e-24, None, ALU.max)
            ins.then_inc(ss_done, 1)
            dve.wait_ge(root_done, 1)
            dve.reciprocal(rows[0:72, :], rows[0:72, :]).then_inc(inv_done, 1)
            for m in range(PAIRS):
                dve.wait_ge(back_mm, m + 1)
                for t, (a, n) in enumerate(UTILES):
                    ins = dve.tensor_tensor(k.aa[:, m, a:a + n], k.aa[:, m, a:a + n], k.psum[3 * (m % 2) + t][:, 0:n], ALU.mult)
                ins.then_inc(back_used, 1)

        @block.scalar
        def _(act):
            for m in range(PAIRS):
                act.wait_ge(kk_done, m + 1)
                if m >= 2:
                    act.wait_ge(ss_mm, m - 1)
                act.activation(sq[m % 2][:], k.aa[:, m], ACT.Square).then_inc(sq_done, 1)
            act.wait_ge(ss_done, 1)
            act.activation(rows[0:72, :], rows[0:72, :], ACT.Sqrt).then_inc(root_done, 1)

        @block.tensor
        def _(pe):
            for m in range(PAIRS):
                pe.wait_ge(sq_done, m + 1)
                sums_to_rows(k, pe, k.psum[6], m, sq[m % 2]).then_inc(ss_mm, 1)
            pe.wait_ge(inv_done, 1)
            for m in range(PAIRS):
                if m >= 2:
                    pe.wait_ge(back_used, m - 1)
                rows_to_heads(k, pe, k.psum[3 * (m % 2):3 * (m % 2) + 3], m, rows).then_inc(back_mm, 1)


def rwkv_decay(k):
    C = float(np.exp(-0.5))
    keep = k.at("keep", R2_AT, [P, W])
    log_sum, inv, prd = (k.at(n, R2_AT + UB * (1 + j), [P, W]) for j, n in enumerate(("log_sum", "inv", "prd")))
    keep_in, sum_done, exp_done, b_done, r_done, bon_in, bon_mm, scaled, used = (
        k.sem(f"dc_{n}") for n in ("keep_in", "sum_done", "exp_done", "b_done", "r_done", "bon_in", "bon_mm", "scaled", "used"))
    with k.nc.Block() as block:
        @block.sync
        def _(sp):
            sp.dma_start(keep[:], k.dram["scan_keep"]).then_inc(keep_in, 16)

        @block.vector
        def _(dve):
            dve.wait_ge(keep_in, 16)
            for m in range(PAIRS):
                if m >= 1:
                    dve.wait_ge(exp_done, m)
                dve.tensor_tensor_scan(log_sum[:], keep[:], k.dec[:, m], 0.0, ALU.mult, ALU.add)
                dve.drain()
                dve.tensor_tensor(k.dec[:, m], log_sum[:], k.dec[:, m], ALU.subtract).then_inc(sum_done, 1)
                kz, rz = k.u[:, 4 + m, 1:UW], k.u[:, m, 1:UW]
                dve.tensor_scalar(k.bon[:, m], k.bb[:, m], -1.0, k.p2("rwkv_k_a", m), ALU.add, ALU.mult)
                dve.tensor_tensor(k.bb[:, m], k.bb[:, m], k.aa[:, m], ALU.mult)
                dve.drain()
                dve.scalar_tensor_tensor(kz, k.bon[:, m], 1.0, kz, ALU.add, ALU.mult).then_inc(b_done, 1)
                dve.drain()
                dve.scalar_tensor_tensor(k.bon[:, m], rz, k.p2("rwkv_r_k", m), kz, ALU.mult, ALU.mult).then_inc(bon_in, 1)
                dve.wait_ge(exp_done, m + 1)
                dve.scalar_tensor_tensor(k.aa[:, m], k.aa[:, m], -1.0, k.dec[:, m], ALU.mult, ALU.mult)
                dve.tensor_copy(k.p_end[:, m, 0:NP_TOK // HD], prd[:, HD - 1:NP_TOK:HD])
                dve.tensor_copy(k.p_end[:, m, NP_TOK // HD:], prd[:, NP_TOK + TSEQ::TSEQ + 1]).then_inc(used, 1)
                dve.wait_ge(bon_mm, m + 1)
                for t, (a, n) in enumerate(UTILES):
                    dve.tensor_tensor(k.bon[:, m, a:a + n], k.psum[t][:, 0:n], k.u[:, 8 + m, 1 + a:1 + a + n], ALU.mult)
                dve.drain().then_inc(r_done, 1)

        @block.scalar
        def _(act):
            for m in range(PAIRS):
                act.wait_ge(sum_done, m + 1)
                if m >= 1:
                    act.wait_ge(scaled, m)
                    act.wait_ge(used, m)
                act.activation(k.dec[:, m], k.dec[:, m], ACT.Exp, scale=-C)
                act.activation(inv[:], log_sum[:], ACT.Exp, scale=C)
                act.activation(prd[:], log_sum[:], ACT.Exp, scale=-C).then_inc(exp_done, 1)

        @block.tensor
        def _(pe):
            for m in range(PAIRS):
                pe.wait_ge(bon_in, m + 1)
                if m >= 1:
                    pe.wait_ge(r_done, m)
                for t, (a, n) in enumerate(UTILES):
                    ins = pe.matmul(k.psum[t][:, 0:n], k.c("head_sum"), k.bon[:, m, a:a + n], start=True, stop=True)
                ins.then_inc(bon_mm, 1)

        @block.gpsimd
        def _(pool):
            for m in range(PAIRS):
                kz, rz = k.u[:, 4 + m, 1:UW], k.u[:, m, 1:UW]
                pool.wait_ge(exp_done, m + 1)
                pool.wait_ge(bon_in, m + 1)
                pool.tensor_tensor(k.bb[:, m], k.bb[:, m], inv[:], ALU.mult)
                pool.tensor_tensor(kz, kz, inv[:], ALU.mult)
                pool.tensor_tensor(rz, rz, prd[:], ALU.mult).then_inc(scaled, 1)


TILE = 4 * PAIRS * P
STREAM = ("ar", "a_bd", "b_bd", "k_bd", "x", "lt", "t", "tt", "lak", "mb", "mk", "v_tok", "b_tok", "k_tok")
PE_STEPS = ["gram_b", "gram_k", "gram_a", "v_tok", "b_tok", "k_tok"] + [
    f"{s}{m}" for m in LEVELS[1:] for s in ("x", "inc")] + ["w", "u", "s", "o"]
DVE_STEPS = ["mask_b", "mask_k", "level1"] + [f"{s}{m}" for m in LEVELS[1:] for s in ("x", "inc")] + ["state"]
ACT_STEPS = ["gather", "v_tok", "lt", "lak", "b_tok", "k_tok", "w", "u", "o"]


def at_step(steps, i, name):
    return i * len(steps) + (steps.index(name) + 2)


def pair4(ap):
    return ap.rearrange("p (m n) -> p m n", m=PAIRS)


def over_pairs(ap):
    return ap.unsqueeze(1).broadcast_to([P, PAIRS, ap.shape[1]])


class Stream:

    def __init__(self, k, s, places):
        self.k, self.s = k, s
        tiles = [k.at(f"{name}_{s}", at, [P, PAIRS, P]) for name, at in zip(STREAM, places)]
        (self.ar, self.a_bd, self.b_bd, self.k_bd, self.x, self.lt, self.t, self.tt, self.lak, self.mb, self.mk,
         self.v_tok, self.b_tok, self.k_tok) = tiles
        self.bank = [k.psum[4 * s + n] for n in range(4)]
        self.pe, self.dve, self.act = (k.sem(f"rwkv_{e}_steps{s}") for e in ("pe", "dve", "act"))
        self.kv_in = k.sem(f"rwkv_kv_in{s}")


def chunk_views(k, c):
    if c is None:
        def view(t, m0, off):
            return t[:, m0:m0 + PAIRS, off + NP_TOK:off + W].rearrange("p m (s t) -> p m s t", t=TSEQ + 1)[:, :, :, 1:]
    else:
        def view(t, m0, off):
            return t[:, m0:m0 + PAIRS, bass.ds(c * HD + off, HD)]
    return view(k.aa, 0, 0), view(k.u, 0, 1), view(k.bb, 0, 0), view(k.u, 4, 1), view(k.u, 8, 1)


def gather(act, st, views, sample):
    def like(ap):
        return ap.rearrange("p m (s t) -> p m s t", t=TSEQ) if sample else ap

    a, r, b, _, _ = views
    act.copy(like(st.ar[:, :, 0:HD]), a)
    act.copy(like(st.ar[:, :, HD:P]), r)
    for dst, src in ((st.a_bd, a), (st.b_bd, b)):
        for h in range(2):
            rows = slice(HD * h, HD * h + HD)
            ins = act.copy(like(dst[:, :, HD * h:HD * h + HD])[rows], src[rows])
    return ins


def gather_kv(pool, st, views, sample):
    for dst, src in ((st.k_bd, views[3]), (st.x, views[4])):
        for h in range(2):
            rows = slice(HD * h, HD * h + HD)
            out = dst[rows, :, HD * h:HD * h + HD]
            if sample:
                out = out.rearrange("p m (s t) -> p m s t", t=TSEQ)
            ins = pool.tensor_copy(out, src[rows])
    ins.then_inc(st.kv_in, 1)


def head_blocks(act, dst, src):
    for h in range(2):
        rows = slice(HD * h, HD * h + HD)
        ins = act.copy(dst[rows, :, HD * h:HD * h + HD], src[rows])
    return ins


def pe_local(pe, st, i, part, levels):
    k = st.k

    def four(bank, lhs, rhs):
        for m in range(PAIRS):
            ins = pe.matmul(bank[:, P * m:P * m + P], lhs[:, m], rhs[:, m], start=True, stop=True)
        return ins

    def turn(bank, src):
        for m in range(PAIRS):
            ins = pe.transpose(bank[:, P * m:P * m + P], src[:, m], k.c("ident"))
        return ins

    if part == 0:
        pe.wait_ge(st.act, at_step(ACT_STEPS, i, "gather"))
        pe.wait_ge(st.dve, len(DVE_STEPS) * i + 1)
        four(st.bank[0], st.b_bd, st.ar).then_inc(st.pe, 1)
        pe.wait_ge(st.kv_in, i + 1)
        four(st.bank[1], st.k_bd, st.ar).then_inc(st.pe, 1)
        four(st.bank[2], st.a_bd, st.b_bd).then_inc(st.pe, 1)
        turn(st.bank[3], st.x).then_inc(st.pe, 1)
        pe.wait_ge(st.dve, at_step(DVE_STEPS, i, "mask_b"))
        turn(st.bank[0], st.b_bd).then_inc(st.pe, 1)
        pe.wait_ge(st.dve, at_step(DVE_STEPS, i, "mask_k"))
        turn(st.bank[1], st.k_bd).then_inc(st.pe, 1)
        return
    m, what = part
    if what == "x":
        pe.wait_ge(st.dve, at_step(DVE_STEPS, i, "level1" if m == 2 else f"inc{m // 2}"))
        if m == 2:
            pe.wait_ge(st.act, at_step(ACT_STEPS, i, "lt"))
        four(st.bank[2], st.lt, st.t).then_inc(st.pe, 1)
    else:
        pe.wait_ge(st.dve, at_step(DVE_STEPS, i, f"x{m}"))
        if m == 2:
            pe.wait_ge(st.act, at_step(ACT_STEPS, i, "k_tok"))
        ins = four(st.bank[0], st.x, st.tt)
        if m != levels[-1]:
            ins = four(st.bank[1], st.tt, st.x)
        ins.then_inc(st.pe, 1)


def dve_local(dve, st, i, part, levels, causal):
    k = st.k
    if part == 0:
        for n, (dst, gram) in enumerate(((st.mb, "gram_b"), (st.mk, "gram_k"))):
            dve.wait_ge(st.pe, at_step(PE_STEPS, i, gram))
            dve.tensor_tensor(dst[:], pair4(st.bank[n][:]), over_pairs(causal), ALU.mult).then_inc(st.dve, 1)
        dve.wait_ge(st.pe, at_step(PE_STEPS, i, "gram_a"))
        dve.tensor_tensor(st.t[:], pair4(st.bank[2][:]), over_pairs(k.c("lev1")), ALU.mult)
        dve.drain()
        for m in range(PAIRS):
            dve.tensor_tensor(st.tt[:, m].rearrange("p (h t) -> p h t", h=2),
                              st.mb[:, m, 0:HD].unsqueeze(1).broadcast_to([P, 2, HD]),
                              k.c("lev1T").rearrange("p (h t) -> p h t", h=2), ALU.mult)
        dve.tensor_tensor(st.t[:], st.t[:], over_pairs(k.c("ident")), ALU.add)
        dve.drain()
        dve.tensor_tensor(st.tt[:], st.tt[:], over_pairs(k.c("ident")), ALU.add).then_inc(st.dve, 1)
        return
    m, what = part
    if what == "x":
        dve.wait_ge(st.pe, at_step(PE_STEPS, i, f"x{m}"))
        dve.tensor_tensor(st.x[:], pair4(st.bank[2][:]), over_pairs(k.c(f"lev{m}")), ALU.mult).then_inc(st.dve, 1)
    else:
        dve.wait_ge(st.pe, at_step(PE_STEPS, i, f"inc{m}"))
        ins = dve.tensor_tensor(st.tt[:], st.tt[:], pair4(st.bank[0][:]), ALU.add)
        if m != levels[-1]:
            ins = dve.tensor_tensor(st.t[:], st.t[:], pair4(st.bank[1][:]), ALU.add)
        ins.then_inc(st.dve, 1)


def act_local(act, st, i):
    for step, n, dst in (("v_tok", 3, st.v_tok), ("lt", None, None), ("lak", None, None), ("b_tok", 0, st.b_tok),
                         ("k_tok", 1, st.k_tok)):
        if n is not None:
            act.wait_ge(st.pe, at_step(PE_STEPS, i, step))
            act.copy(dst[:], pair4(st.bank[n][:])).then_inc(st.act, 1)
        elif step == "lt":
            act.wait_ge(st.dve, at_step(DVE_STEPS, i, "mask_b"))
            head_blocks(act, st.lt, st.mb[:, :, 0:HD]).then_inc(st.act, 1)
        else:
            act.wait_ge(st.dve, at_step(DVE_STEPS, i, "mask_k"))
            head_blocks(act, st.lak, st.mk[:, :, 0:HD]).then_inc(st.act, 1)


def rwkv_prompt(k):
    region_a = QKV_AT + 4 * TB
    region_b = R1_AT + 4 * PAIRS * UB
    u12 = up32(U_AT + 12 * UW * 4)
    k.streams = [Stream(k, 0, [region_a + TILE * n for n in range(12)] + [region_b, region_b + TILE]),
                 Stream(k, 1, [R2_AT + TILE * n for n in range(14)])]
    k.w_now = k.at("w_now", region_b + 2 * TILE, [P, PAIRS, P])
    k.u_now = k.at("u_now", region_b + 3 * TILE, [P, PAIRS, P])
    k.state = k.at("state", u12, [P, PAIRS, P])
    zeroed = k.sem("rwkv_zeroed")
    NI = NP_TOK // HD // 2
    levels = LEVELS[1:]
    parts = [0] + [(m, what) for m in levels for what in ("x", "inc")]
    wkv_turned, wkv_rows, wkv_out = k.sem("wkv_turned"), k.sem("wkv_rows"), k.sem("wkv_out")

    with k.nc.Block() as block:
        @block.gpsimd
        def _(pool):
            for st in k.streams:
                for t in (st.a_bd, st.b_bd, st.k_bd, st.x, st.lt, st.lak):
                    pool.memset(t[:], 0.0).then_inc(zeroed, 1)
            pool.memset(k.state[:], 0.0).then_inc(zeroed, 1)
            pool.drain()
            for st in k.streams:
                gather_kv(pool, st, chunk_views(k, st.s), False)
            with pool.Fori(0, NI - 1) as i:
                for st in k.streams:
                    pool.wait_ge(st.pe, at_step(PE_STEPS, i, f"inc{levels[-1]}"))
                    gather_kv(pool, st, chunk_views(k, 2 * i + 2 + st.s), False)

        @block.scalar
        def _(act):
            act.wait_ge(zeroed, 13)
            for st in k.streams:
                act.sem_inc(st.act, 1)
            for st in k.streams:
                gather(act, st, chunk_views(k, st.s), False).then_inc(st.act, 1)

            def round_(i, more):
                s0, s1 = k.streams
                for st in k.streams:
                    act_local(act, st, i)

                def w_and_u(st):
                    act.wait_ge(st.pe, at_step(PE_STEPS, i, "w"))
                    act.copy(k.w_now[:], pair4(st.bank[3][:])).then_inc(st.act, 1)
                    act.wait_ge(st.pe, at_step(PE_STEPS, i, "u"))
                    act.copy(k.u_now[:], pair4(st.bank[2][:])).then_inc(st.act, 1)

                def output(st):
                    act.wait_ge(st.pe, at_step(PE_STEPS, i, "o"))
                    act.copy(st.ar[:, :, HD:P], pair4(st.bank[1][:])[:, :, HD:P])
                    act.drain()
                    act.copy(chunk_views(k, 2 * i + st.s)[1], st.ar[:, :, HD:P]).then_inc(st.act, 1)

                def next_chunk(st):
                    if more:
                        act.drain()
                        gather(act, st, chunk_views(k, 2 * i + 2 + st.s), False).then_inc(st.act, 1)

                w_and_u(s0)
                output(s0)
                w_and_u(s1)
                next_chunk(s0)
                output(s1)
                next_chunk(s1)

            with act.Fori(0, NI - 1) as i:
                round_(i, True)
            round_(NI - 1, False)

        @block.tensor
        def _(pe):
            for st in k.streams:
                pe.sem_inc(st.pe, 1)
            with pe.Fori(0, NI) as i:
                s0, s1 = k.streams

                def four(bank, lhs, rhs, start, stop):
                    for m in range(PAIRS):
                        ins = pe.matmul(bank[:, P * m:P * m + P], lhs[:, m], rhs[:, m],
                                        start=start and m == 0, stop=stop and m == PAIRS - 1)
                    return ins

                def alone(st):
                    pe.wait_ge(st.dve, at_step(DVE_STEPS, i, f"inc{levels[-1]}"))
                    four(st.bank[1], st.v_tok, st.mk, True, False)
                    four(st.bank[0], st.k_tok, st.v_tok, True, False)

                def with_state(st):
                    four(st.bank[3], st.a_bd, k.state, False, True).then_inc(st.pe, 1)
                    four(st.bank[1], k.state, st.ar, False, False)
                    pe.wait_ge(st.act, at_step(ACT_STEPS, i, "w"))
                    four(st.bank[2], st.tt, k.w_now, True, True).then_inc(st.pe, 1)

                def with_u(st):
                    pe.wait_ge(st.act, at_step(ACT_STEPS, i, "u"))
                    four(st.bank[0], st.b_tok, k.u_now, False, True).then_inc(st.pe, 1)
                    four(st.bank[1], k.u_now, st.mb, False, True).then_inc(st.pe, 1)

                for part in parts:
                    for st in k.streams:
                        if part == parts[-1]:
                            four(st.bank[3], st.lak, st.v_tok, True, False)
                        pe_local(pe, st, i, part, levels)
                alone(s0)
                pe.wait_ge(s1.dve, len(DVE_STEPS) * i + 1)
                with_state(s0)
                alone(s1)
                with_u(s0)
                pe.wait_ge(s0.dve, at_step(DVE_STEPS, i, "state"))
                with_state(s1)
                with_u(s1)
            pe.wait_ge(k.streams[1].dve, len(DVE_STEPS) * NI + 1)
            pe.wait_ge(k.streams[0].act, len(ACT_STEPS) * NI + 1)
            for m in range(PAIRS):
                ins = pe.transpose(k.psum[0][:, P * m:P * m + P], k.state[:, m], k.c("ident"))
            ins.then_inc(wkv_turned, 1)

        @block.vector
        def _(dve):
            for st in k.streams:
                dve.sem_inc(st.dve, 1)
            with dve.Fori(0, NI) as i:
                for part in parts:
                    for st in k.streams:
                        dve_local(dve, st, i, part, levels, k.c("causal"))
                for st in k.streams:
                    dve.wait_ge(st.pe, at_step(PE_STEPS, i, "s"))
                    dve.tensor_tensor(k.state[:], k.state[:], pair4(st.bank[0][:]), ALU.add)
                    dve.drain()
                    dve.tensor_tensor(k.state[:], k.state[:],
                                      k.p_end[:, :, bass.ds(2 * i + st.s, 1)].broadcast_to([P, PAIRS, P]),
                                      ALU.mult).then_inc(st.dve, 1)
            dve.wait_ge(wkv_turned, 1)
            dve.tensor_copy(k.w_now[:], pair4(k.psum[0][:])).then_inc(wkv_rows, 1)

        @block.sync
        def _(sp):
            sp.wait_ge(wkv_rows, 1)
            for h in range(2):
                sp.dma_start(k.dram["prompt_wkv"][0, 0].rearrange("(m h) i j -> h i m j", h=2)[h],
                             k.w_now[HD * h:HD * h + HD, :, HD * h:HD * h + HD]).then_inc(wkv_out, 16)
            sp.wait_ge(wkv_out, 32)


def rwkv_sample(k):
    st = k.streams[0]
    st.pe, st.dve, st.act, st.kv_in = (k.sem(f"rwkv_s_{e}") for e in ("pe_steps", "dve_steps", "act_steps", "kv_in"))
    levels = (2, 4)
    parts = [0] + [(m, what) for m in levels for what in ("x", "inc")]
    o = R2_AT
    rows = k.at("s_rows", o, [P, NSEQ, P]); o += 4096
    sq2 = [k.at(f"s_state{j}", o + 4096 * j, [P, NSEQ, P]) for j in range(2)]; o += 8192
    a_seq = k.at("a_seq", o, [P, NSEQ * (P + TSEQ)]); o += 4 * NSEQ * (P + TSEQ)
    u_seq = k.at("u_seq", o, [P, NSEQ, P]); o += 4096
    v_seq = k.at("v_seq", o, [P, NSEQ, P]); o += 4096
    out_rows = k.at("out_rows", o, [P, NSEQ, P]); o += 4096
    zeroed, rows_in, sq_mm, sq_done, a_done, w_mm, w_done, u_mm, u_done, o_mm, o_done, up_mm, up_done, back_mm, back_done, out_sem = (
        k.sem(f"ss_{n}") for n in ("zeroed", "rows_in", "sq_mm", "sq_done", "a_done", "w_mm", "w_done", "u_mm", "u_done",
                                   "o_mm", "o_done", "up_mm", "up_done", "back_mm", "back_done", "out"))
    state_v = k.dram["state_wkv"][0].rearrange("s (m h) i j -> m h i s j", h=2)
    out_v = k.dram["sample_wkv"][0].rearrange("s (m h) i j -> m h i s j", h=2)
    NE = NP_TOK // HD

    def store(sp, m):
        sp.wait_ge(back_done, m + 1)
        for h in range(2):
            sp.dma_start(out_v[m, h], out_rows[HD * h:HD * h + HD, :, HD * h:HD * h + HD]).then_inc(out_sem, 16)

    with k.nc.Block() as block:
        @block.sync
        def _(sp):
            sp.wait_ge(zeroed, 2)
            for m in range(PAIRS):
                if m >= 1:
                    sp.wait_ge(sq_mm, m)
                for h in range(2):
                    sp.dma_start(rows[HD * h:HD * h + HD, :, HD * h:HD * h + HD], state_v[m, h]).then_inc(rows_in, 16)
                if m >= 2:
                    store(sp, m - 2)
            store(sp, PAIRS - 2)
            store(sp, PAIRS - 1)
            sp.wait_ge(out_sem, 32 * PAIRS)

        @block.gpsimd
        def _(pool):
            for t in (rows, a_seq):
                pool.memset(t[:], 0.0).then_inc(zeroed, 1)
            pool.drain()
            gather_kv(pool, st, chunk_views(k, None), True)

        @block.scalar
        def _(act):
            act.sem_inc(st.act, 1)
            gather(act, st, chunk_views(k, None), True).then_inc(st.act, 1)
            act_local(act, st, 0)
            act.wait_ge(zeroed, 2)

            def take(m):
                act.wait_ge(sq_mm, m + 1)
                for h in range(2):
                    act.copy(sq2[m % 2][:, 4 * h:4 * h + 4], pair4(k.psum[4 + h][:]))
                act.drain().then_inc(sq_done, 1)
                for h in range(2):
                    ins = act.copy(a_seq[:].rearrange("p (q n) -> p q n", n=P + TSEQ)[:, :, HD * h:HD * h + TSEQ],
                                   per_seq(st.a_bd[:, m, HD * h:HD * h + HD]))
                ins.then_inc(a_done, 1)

            def give(m):
                act.wait_ge(back_mm, m + 1)
                if m >= 1:
                    act.wait_ge(out_sem, 32 * m)
                for h in range(2):
                    ins = act.copy(out_rows[:, 4 * h:4 * h + 4], pair4(k.psum[4 + h][:]))
                ins.then_inc(back_done, 1)

            take(0)
            for m in range(PAIRS):
                act.wait_ge(w_mm, m + 1)
                act.copy(k.w_now[:, m], st.bank[3][:, P * m:P * m + P]).then_inc(w_done, 1)
                act.wait_ge(u_mm, m + 1)
                act.copy(k.u_now[:, m], st.bank[2][:, P * m:P * m + P]).then_inc(u_done, 1)
                act.wait_ge(o_mm, m + 1)
                act.copy(u_tok(k.u[:, m, 1:UW]), per_seq(st.bank[1][:, P * m + HD:P * m + P])).then_inc(o_done, 1)
                if m >= 1:
                    give(m - 1)
                if m + 1 < PAIRS:
                    take(m + 1)
            give(PAIRS - 1)

        @block.tensor
        def _(pe):
            pe.sem_inc(st.pe, 1)
            for part in parts:
                pe_local(pe, st, 0, part, levels)
            ident = k.c("ident")

            def turn(m):
                pe.wait_ge(rows_in, 32 * m + 32)
                if m >= 2:
                    pe.wait_ge(back_done, m - 1)
                for q in range(NSEQ):
                    ins = pe.transpose(k.psum[4 + q // 4][:, P * (q % 4):P * (q % 4) + P], rows[:, q], ident)
                ins.then_inc(sq_mm, 1)

            def turn_back(m):
                pe.wait_ge(up_done, 2 * m + 2)
                if m == PAIRS - 1:
                    pe.wait_ge(back_done, m)
                for q in range(NSEQ):
                    ins = pe.transpose(k.psum[4 + q // 4][:, P * (q % 4):P * (q % 4) + P], sq2[m % 2][:, q], ident)
                ins.then_inc(back_mm, 1)

            turn(0)
            for m in range(PAIRS):
                sq = sq2[m % 2]
                col = slice(P * m, P * m + P)
                pe.wait_ge(a_done, m + 1)
                if m >= 1:
                    pe.wait_ge(w_done, m)
                pe.matmul(st.bank[3][:, col], st.lak[:, m], st.v_tok[:, m], start=True, stop=False)
                for q in range(NSEQ):
                    ins = pe.matmul(st.bank[3][:, col], a_seq[:, P * q:P * q + P], sq[:, q], start=False, stop=(q == NSEQ - 1))
                ins.then_inc(w_mm, 1)
                pe.wait_ge(w_done, m + 1)
                pe.wait_ge(st.dve, at_step(DVE_STEPS, 0, f"inc{levels[-1]}"))
                pe.matmul(st.bank[2][:, col], st.tt[:, m], k.w_now[:, m], start=True, stop=True).then_inc(u_mm, 1)
                pe.wait_ge(u_done, m + 1)
                if m >= 1:
                    pe.wait_ge(o_done, m)
                pe.matmul(st.bank[1][:, col], st.v_tok[:, m], st.mk[:, m], start=True, stop=False)
                pe.matmul(st.bank[1][:, col], k.u_now[:, m], st.mb[:, m], start=False, stop=False)
                for q in range(NSEQ):
                    at = P * m + HD + TSEQ * q
                    ins = pe.matmul(st.bank[1][:, at:at + TSEQ], sq[:, q],
                                    st.ar[:, m, HD + TSEQ * q:HD + TSEQ * q + TSEQ], start=False, stop=(q == NSEQ - 1))
                ins.then_inc(o_mm, 1)
                if m >= 1:
                    turn_back(m - 1)
                if m + 1 < PAIRS:
                    turn(m + 1)
                pe.wait_ge(up_done, 2 * m + 1)
                for h in range(2):
                    pe.matmul(k.psum[6 + h][:], st.b_tok[:, m], u_seq[:, 4 * h:4 * h + 4].rearrange("p q n -> p (q n)"),
                              start=True, stop=False)
                    ins = pe.matmul(k.psum[6 + h][:], st.k_tok[:, m], v_seq[:, 4 * h:4 * h + 4].rearrange("p q n -> p (q n)"),
                                    start=False, stop=True)
                ins.then_inc(up_mm, 1)
            turn_back(PAIRS - 1)

        @block.vector
        def _(dve):
            dve.sem_inc(st.dve, 1)
            for part in parts:
                dve_local(dve, st, 0, part, levels, k.c("causal_s"))
            seq = k.c("seq_of").unsqueeze(2).broadcast_to([P, NSEQ, P])
            for m in range(PAIRS):
                sq = sq2[m % 2]
                dve.wait_ge(u_done, m + 1)
                dve.wait_ge(st.act, at_step(ACT_STEPS, 0, "v_tok"))
                dve.tensor_tensor(v_seq[:], st.v_tok[:, m].unsqueeze(1).broadcast_to([P, NSEQ, P]), seq, ALU.mult)
                dve.tensor_tensor(u_seq[:], k.u_now[:, m].unsqueeze(1).broadcast_to([P, NSEQ, P]), seq, ALU.mult
                                  ).then_inc(up_done, 1)
                dve.wait_ge(up_mm, m + 1)
                for h in range(2):
                    dve.tensor_tensor(sq[:, 4 * h:4 * h + 4], sq[:, 4 * h:4 * h + 4], pair4(k.psum[6 + h][:]), ALU.add)
                dve.drain()
                dve.tensor_tensor(sq[:], sq[:], k.p_end[:, m, NE:].unsqueeze(2).broadcast_to([P, NSEQ, P]),
                                  ALU.mult).then_inc(up_done, 1)


def rwkv_finish(k):
    sq = [k.at(f"dev_sq{j}", R2_AT + UB * j, [P, W]) for j in range(2)]
    rows = k.at("gn_rows", R2_AT + 2 * UB, [P, 366])
    g2 = k.at("g2", R2_AT + 3 * UB, [P, RW])
    g2_in, mean_mm, dev_done, sq_done, var_mm, var_done, root_done, inv_done, back_mm, scaled, affine_done, bonus_done, g_mm, out_done = (
        k.sem(f"gn_{n}") for n in ("g2_in", "mean_mm", "dev_done", "sq_done", "var_mm", "var_done", "root_done", "inv_done",
                                   "back_mm", "scaled", "affine_done", "bonus_done", "g_mm", "out_done"))

    def o(m, a=0, n=W):
        return k.u[:, m, 1 + a:1 + a + n]

    with k.nc.Block() as block:
        @block.sync
        def _(sp):
            sp.dma_start(g2[:], k.dram["rwkv_g2"][0]).then_inc(g2_in, 16)

        @block.tensor
        def _(pe):
            def means(m):
                if m >= 2:
                    pe.wait_ge(dev_done, m - 1)
                for t, (a, n) in enumerate(UTILES):
                    ins = pe.matmul(k.psum[3 * (m % 2) + t][:, 0:n], k.c("head_mean"), o(m, a, n), start=True, stop=True)
                ins.then_inc(mean_mm, 1)

            means(0)
            for m in range(PAIRS):
                if m + 1 < PAIRS:
                    means(m + 1)
                pe.wait_ge(sq_done, m + 1)
                sums_to_rows(k, pe, k.psum[6], m, sq[m % 2]).then_inc(var_mm, 1)
            pe.wait_ge(g2_in, 16)
            pe.wait_ge(dev_done, PAIRS)

            def gate(m):
                if m >= 1:
                    pe.wait_ge(out_done, m)
                for t, (a, n) in enumerate(UTILES):
                    ins = pe.matmul(k.psum[3 + t][:, 0:n], g2[:, P * m:P * m + P], k.u[:, 13, 1 + a:1 + a + n],
                                    start=True, stop=True)
                ins.then_inc(g_mm, 1)

            gate(0)
            pe.wait_ge(inv_done, 1)
            for m in range(PAIRS):
                if m >= 1:
                    pe.wait_ge(scaled, m)
                rows_to_heads(k, pe, k.psum[0:3], m, rows).then_inc(back_mm, 1)
                if m >= 1:
                    gate(m)

        @block.vector
        def _(dve):
            for m in range(PAIRS):
                dve.wait_ge(mean_mm, m + 1)
                for t, (a, n) in enumerate(UTILES):
                    ins = dve.tensor_tensor(o(m, a, n), o(m, a, n), k.psum[3 * (m % 2) + t][:, 0:n], ALU.subtract)
                ins.then_inc(dev_done, 1)
            dve.memset(rows[:], 1.0)
            dve.drain()
            dve.wait_ge(var_mm, PAIRS)
            for t, (a, n) in enumerate(UTILES):
                r = slice(32 * t, 32 * t + 8)
                ins = dve.tensor_scalar(rows[r, 0:n], k.psum[6][r, 0:n], 1.0 / HD, LNX_EPS, ALU.mult, ALU.add)
            ins.then_inc(var_done, 1)
            dve.wait_ge(root_done, 1)
            dve.reciprocal(rows[0:72, :], rows[0:72, :]).then_inc(inv_done, 1)

            def gated(m):
                dve.wait_ge(bonus_done, m + 1)
                dve.wait_ge(g_mm, m + 1)
                for t, (a, n) in enumerate(UTILES):
                    ins = dve.tensor_tensor(o(m, a, n), o(m, a, n), k.psum[3 + t][:, 0:n], ALU.mult)
                ins.then_inc(out_done, 1)

            for m in range(PAIRS):
                dve.wait_ge(back_mm, m + 1)
                for t, (a, n) in enumerate(UTILES):
                    ins = dve.tensor_tensor(o(m, a, n), o(m, a, n), k.psum[t][:, 0:n], ALU.mult)
                ins.then_inc(scaled, 1)
                if m >= 1:
                    gated(m - 1)
            gated(PAIRS - 1)

        @block.scalar
        def _(act):
            for m in range(PAIRS):
                act.wait_ge(dev_done, m + 1)
                if m >= 2:
                    act.wait_ge(var_mm, m - 1)
                act.activation(sq[m % 2][:], o(m), ACT.Square).then_inc(sq_done, 1)
            act.wait_ge(var_done, 1)
            act.activation(rows[0:72, :], rows[0:72, :], ACT.Sqrt).then_inc(root_done, 1)
            for m in range(PAIRS):
                act.wait_ge(scaled, m + 1)
                act.activation(o(m), o(m), ACT.Identity, scale=k.p2("ln_x_w", m), bias=k.p2("ln_x_b", m)
                               ).then_inc(affine_done, 1)

        @block.gpsimd
        def _(pool):
            for m in range(PAIRS):
                pool.wait_ge(affine_done, m + 1)
                pool.tensor_tensor(o(m), o(m), k.bon[:, m], ALU.add).then_inc(bonus_done, 1)


class MixSplit:

    def __init__(self, k):
        self.k = k
        self.hi_done, self.lo_done, self.att_done, self.x_back = (
            k.sem(f"split_{n}") for n in ("hi_done", "lo_done", "att_done", "x_back"))

    def parts(self, t):
        k, (a, n) = self.k, TILES[t]
        np_ = min(n, NP_TOK - a)
        out = [(k.u[:, 0:4, 1 + a:1 + a + np_], slice(0, 4), slice(a, a + np_), False)]
        if np_ < n:
            sample = k.u[:, 0:4, 1 + NP_TOK:UW].rearrange("p c (s t) -> p c s t", t=TSEQ + 1)[:, :, :, 1:]
            out.append((sample, slice(0, 4), slice(NP_TOK, T), True))
        out.append((k.qkv[:, 0:4, a:a + n], slice(4, 8), slice(a, a + n), False))
        return out

    def view(self, tensor, chunks, cols, by_seq):
        v = tensor[:, chunks, cols]
        return v.rearrange("p c (s t) -> p c s t", t=TSEQ) if by_seq else v

    def dve(self, dve):
        k = self.k
        for t in range(NT):
            parts = self.parts(t)
            for src, chunks, cols, by_seq in parts:
                dve.tensor_copy(self.view(k.hh, chunks, cols, by_seq), src)
            dve.drain().then_inc(self.hi_done, 1)
            src, chunks, cols, by_seq = parts[-1]
            dve.tensor_tensor(self.view(k.hl, chunks, cols, by_seq), src,
                              self.view(k.hh, chunks, cols, by_seq).bitcast(F32), ALU.subtract).then_inc(self.att_done, 1)

    def pool(self, pool):
        k = self.k
        for t in range(NT):
            pool.wait_ge(self.hi_done, t + 1)
            for src, chunks, cols, by_seq in self.parts(t)[:-1]:
                ins = pool.tensor_tensor(self.view(k.hl, chunks, cols, by_seq), src,
                                         self.view(k.hh, chunks, cols, by_seq).bitcast(F32), ALU.subtract)
            ins.then_inc(self.lo_done, 1)

    def pe_ready(self, pe, t):
        pe.wait_ge(self.att_done, t + 1)
        pe.wait_ge(self.lo_done, t + 1)

    def restore_x(self, act):
        act.wait_ge(self.att_done, NT)
        act.dma_start(self.k.x[:], self.k.dram["x_spill"]).then_inc(self.x_back, 16)


def output_projection(k):
    split = MixSplit(k)
    w = k.dram["w_out"][0]
    wr = w[0:RW].rearrange("(k p) (f n) -> p f k n", p=P, n=P)
    wa = w[RW:].rearrange("(h c p) (f n) -> h p f c n", h=2, p=HD, n=P)
    scratch = k.at("w_out_scratch", R2_AT + 24 * KB, [P, 2, NS_TOK])

    def load(f0):
        def run(sp, raw, i, j, sem):
            if sp is not None:
                f = bass.ds(2 * i + f0 + j, 1)
                sp.dma_start(raw[:, 0:4], wr[:, f].rearrange("p o k n -> p (o k) n")).then_inc(sem, 16)
                for h in range(2):
                    sp.dma_start(raw[HD * h:HD * h + HD, 4:8], wa[h][:, f].rearrange("p o c n -> p (o c) n")
                                 ).then_inc(sem, 16)
            return 3
        return run

    def evac(f0):
        def run(dve, i, j, t, bank):
            return add_gated(dve, k, 5, 2 * i + f0 + j, t, bank, scratch[:, j])
        return run

    stream_product(k, "w_out", R2_AT, [(1, load(0), evac(0)), (KD // 2 - 1, load(2), evac(2))], k.hh, k.hl, False,
                   split=split)


def store_output(k):
    x_now = [k.at(f"x_now{j}", WT_AT + 4096 * j, [P, KD, P]) for j in range(2)]
    rows = [k.at(f"y_rows{j}", WT_AT + 4096 * (2 + j), [P, D]) for j in range(2)]
    squares = k.at("y_squares", WT_AT + 4096 * 4, [P, D])
    weight = k.at("y_weight", WT_AT + 4096 * 5, [P, D])
    sums = [k.at(f"y_sums{j}", WT_AT + 4096 * 6 + 32 * j, [P, 4]) for j in range(2)]
    weight_in, now_done, turned, sq_done, sum_done, root_done, rows_done = (
        k.sem(f"y_{n}") for n in ("weight_in", "now_done", "turned", "sq_done", "sum_done", "root_done", "rows_done"))
    y_out = [k.sem(f"y_out{j}") for j in range(2)]
    NTT = NP_TOK // P
    yv = k.dram["y_prompt"][0].rearrange("(i j p) n -> j p i n", p=P, j=2)

    def tiles(eng, body):
        with eng.Fori(0, NTT // 2 - 1) as i:
            for j in range(2):
                body(i, j, P, P)
        body(NTT // 2 - 1, 0, P, P)
        body(NTT // 2 - 1, 1, P, NS_TOK)
        body(NTT // 2, 0, NS_TOK, 0)

    with k.nc.Block() as block:
        @block.vector
        def _(dve):
            def take(i, j, n):
                dve.wait_ge(turned, 2 * i + j + 1)
                dve.tensor_scalar(x_now[j][:, :, 0:n], k.x[:, :, bass.ds(256 * i + 128 * j, n)], 1.0, None, ALU.mult
                                  ).then_inc(now_done, 1)

            def tile(i, j, n, n_next):
                if n_next:
                    take(i + j, 1 - j, n_next)
                dve.wait_ge(sq_done, 2 * i + j + 1)
                dve.tensor_tensor(sums[j][0:n, 2:3], sums[j][0:n, 0:1], sums[j][0:n, 1:2], ALU.add).then_inc(sum_done, 1)
                dve.wait_ge(root_done, 2 * i + j + 1)
                dve.reciprocal(sums[j][0:n, 3:4], sums[j][0:n, 3:4])
                dve.drain()
                dve.wait_ge(y_out[j], 16 * i + 16)
                for h in range(2):
                    col = slice(512 * h, 512 * h + 512)
                    ins = dve.scalar_tensor_tensor(rows[j][0:n, col], k.psum[2 * j + h][0:n, :], sums[j][0:n, 3:4],
                                                   weight[0:n, col], ALU.mult, ALU.mult)
                ins.then_inc(rows_done, 1)

            dve.sem_inc(rows_done, 2)
            take(0, 0, P)
            dve.wait_ge(weight_in, 16)
            tiles(dve, tile)

        @block.tensor
        def _(pe):
            def tile(i, j, n, n_next):
                pe.wait_ge(now_done, 2 * i + j + 1)
                pe.wait_ge(rows_done, 2 * i + j + 1)
                for c in range(KD):
                    ins = pe.transpose(k.psum[2 * j + c // 4][0:n, P * (c % 4):P * (c % 4) + P], x_now[j][:, c, 0:n],
                                       k.c("ident"))
                ins.then_inc(turned, 1)

            pe.sem_inc(turned, 2)
            tiles(pe, tile)

        @block.scalar
        def _(act):
            def tile(i, j, n, n_next):
                act.wait_ge(turned, 2 * i + j + 3)
                for h in range(2):
                    ins = act.activation(squares[0:n, 512 * h:512 * h + 512], k.psum[2 * j + h][0:n, :], ACT.Square,
                                         accum_out=sums[j][0:n, h:h + 1])
                ins.then_inc(sq_done, 1)
                act.wait_ge(sum_done, 2 * i + j + 1)
                act.activation(sums[j][0:n, 3:4], sums[j][0:n, 2:3], ACT.Sqrt, scale=1.0 / D, bias=k.c("eps")[0:n]
                               ).then_inc(root_done, 1)
                act.drain()

            tiles(act, tile)

        @block.sync
        def _(sp):
            sp.dma_start(weight[:], k.dram["norm_final"].rearrange("(o n) -> o n", o=1).broadcast_to([P, D])
                         ).then_inc(weight_in, 16)
            for j in range(2):
                sp.sem_inc(y_out[j], 16)
            with sp.Fori(0, NTT // 2) as i:
                for j in range(2):
                    sp.wait_ge(rows_done, 2 * i + j + 3)
                    sp.dma_start(yv[j][:, bass.ds(i, 1)].rearrange("p o n -> p (o n)"), rows[j][:]).then_inc(y_out[j], 16)
            sp.wait_ge(rows_done, NTT + 3)
            sp.dma_start(k.dram["y_sample"].rearrange("s t n -> (s t) n"), rows[0][0:NS_TOK, :]).then_inc(y_out[0], 16)
            sp.wait_ge(y_out[0], 16 * (NTT // 2 + 2))
            sp.wait_ge(y_out[1], 16 * (NTT // 2 + 1))
            sp.wait_ge(k.cache_out, 16 * k.n_cache_out)


OUTS = [("y_prompt", [1, NP_TOK, D]), ("y_sample", [NSEQ, TSEQ, D]), ("prompt_wkv", [1, 1, 8, HD, HD]),
        ("prompt_shift", [1, 1, U_COLS]), ("prompt_k", [1, 1, WINDOW, 2, HD]), ("prompt_v", [1, 1, WINDOW, 2, HD]),
        ("sample_wkv", [1, NSEQ, 8, HD, HD]), ("sample_shift", [1, NSEQ, U_COLS]),
        ("sample_k", [1, NSEQ, WINDOW, 2, HD]), ("sample_v", [1, NSEQ, WINDOW, 2, HD])]


def build(nc, dram):
    with ExitStack() as ctx:
        k = Core(nc, dram, ctx)
        load_and_modulate(k)
        ffn(k, "f1", dram["ffn1_w_gu"], dram["ffn1_w_down"], 0)
        input_projection(k)
        attention_prepare(k)
        attention_prompt(k)
        attention_sample(k)
        k.release(keep=(k.cache_out,))
        rwkv_shift(k)
        rwkv_keys(k)
        rwkv_decay(k)
        rwkv_prompt(k)
        rwkv_sample(k)
        rwkv_finish(k)
        output_projection(k)
        k.release(keep=(k.cache_out,))
        ffn(k, "f2", dram["ffn2_w_gu"], dram["ffn2_w_down"], 6)
        store_output(k)


def kernel(**inputs):
    import concourse.bacc as bacc
    from concourse.bass_utils import run_bass_kernel_spmd

    cos, sin = rope_tables()
    given = dict(inputs, consts=np.concatenate(list(CONST.values()), axis=1), scan_keep=scan_keep(), cos=cos, sin=sin)
    nc = bacc.Bacc("TRN2", target_bir_lowering=False, num_devices=1)
    arrays, dram = {}, {}
    for name, value in given.items():
        a = np.ascontiguousarray(value)
        arrays[f"in_{name}"] = a
        dram[name] = nc.dram_tensor(f"in_{name}", a.shape, mybir.dt.from_np(a.dtype), kind="ExternalInput").ap()
    for name, shape in OUTS:
        dram[name] = nc.dram_tensor(f"out_{name}", shape, F32, kind="ExternalOutput").ap()
    dram["x_spill"] = nc.dram_tensor("x_spill", [P, KD, T], F32, kind="Internal").ap()
    build(nc, dram)
    r = run_bass_kernel_spmd(nc, [arrays], core_ids=[0])
    return tuple(r.results[0][f"out_{name}"] for name, _ in OUTS)
```
